# Optimizing a Trainium2 kernel written in Bass

```python
import math
import jax, jax.numpy as jnp
from jax import lax
import numpy as np

D_MODEL = 1024
BATCH = 1
SEQ = 512
DEPTH = 2

N_MIXERS = 2
N_GDN_LAYERS = (DEPTH + 1) // 2
N_MLA_LAYERS = DEPTH // 2

GDN_K_HEADS = 8
GDN_V_HEADS = 16
GDN_HEAD_DIM = 128
GDN_QK_WIDTH = GDN_K_HEADS * GDN_HEAD_DIM
GDN_V_WIDTH = GDN_V_HEADS * GDN_HEAD_DIM
GDN_CONV_WIDTH = 4
GDN_CONV_CH = 2 * GDN_QK_WIDTH + GDN_V_WIDTH
GDN_IN_WIDTH = GDN_CONV_CH + GDN_V_WIDTH + 2 * GDN_V_HEADS
GDN_CHUNK = 64

MLA_HEADS = 16
MLA_Q_LORA = 256
MLA_KV_LORA = 128
MLA_NOPE = 128
MLA_ROPE = 64
MLA_V = 128
MLA_IN_WIDTH = MLA_Q_LORA + MLA_KV_LORA + MLA_ROPE
MLA_Q_BLOCK = 128
MLA_SCALE = (MLA_NOPE + MLA_ROPE) ** -0.5
ROPE_THETA = 10000.0

MOE_GROUPS = 8
MOE_EXPERTS_PER_GROUP = 8
MOE_EXPERTS = MOE_GROUPS * MOE_EXPERTS_PER_GROUP
MOE_TOP_K = 2
MOE_FF = 256
MOE_BLOCK = 128

PLE_DIM = 256
NORM_EPS = 1e-6

kernel_name = 'hybrid_gdn_mla_hmoe_ple'

def rms_norm(x, g):
    xf = x.astype(jnp.float32)
    y = xf * lax.rsqrt(jnp.mean(xf * xf, axis=-1, keepdims=True) + NORM_EPS)
    return (y * g.astype(jnp.float32)).astype(x.dtype)

def l2_normalize(x):
    xf = x.astype(jnp.float32)
    return xf * lax.rsqrt(jnp.sum(xf * xf, axis=-1, keepdims=True) + NORM_EPS)

def rope_tables(positions):
    inv_freq = ROPE_THETA ** (-jnp.arange(0, MLA_ROPE, 2, dtype=jnp.float32) / MLA_ROPE)
    ang = positions.astype(jnp.float32)[..., None] * inv_freq
    return jnp.cos(ang), jnp.sin(ang)

def apply_rope(x, cos, sin):
    xf = x.astype(jnp.float32)
    half = xf.shape[-1] // 2
    x1, x2 = xf[..., :half], xf[..., half:]
    return jnp.concatenate([x1 * cos - x2 * sin, x2 * cos + x1 * sin], axis=-1).astype(x.dtype)

def causal_depthwise_conv(x, w):
    k_width, ch = w.shape
    return lax.conv_general_dilated(
        x, w[:, None, :].astype(x.dtype), window_strides=(1,), padding=[(k_width - 1, 0)],
        dimension_numbers=('NWC', 'WIO', 'NWC'), feature_group_count=ch)

def chunk_gated_delta_rule(q, k, v, g, beta):
    b, s, h, dk = q.shape
    dv = v.shape[-1]
    c = GDN_CHUNK
    nc = s // c

    def chunks(t):
        t = jnp.moveaxis(t, 2, 1)
        return t.reshape((b, h, nc, c) + t.shape[3:])

    q = chunks(q) * (dk ** -0.5)
    k = chunks(k)
    v = chunks(v)
    beta = chunks(beta)
    g = jnp.cumsum(chunks(g), axis=-1)
    idx = jnp.arange(c)
    incl = idx[:, None] >= idx[None, :]
    strict = idx[:, None] > idx[None, :]
    diff = g[..., :, None] - g[..., None, :]
    decay = jnp.where(incl, jnp.exp(jnp.where(incl, diff, 0.0)), 0.0)
    k_beta = k * beta[..., None]
    kk = jnp.einsum('bhnid,bhnjd->bhnij', k_beta, k) * decay
    lower = jnp.where(strict, kk, 0.0) + jnp.eye(c, dtype=jnp.float32)
    rhs = jnp.concatenate([v * beta[..., None], k_beta * jnp.exp(g)[..., None]], axis=-1)
    sol = lax.linalg.triangular_solve(lower, rhs, left_side=True, lower=True, unit_diagonal=True)
    u, w = sol[..., :dv], sol[..., dv:]
    qk = jnp.einsum('bhnid,bhnjd->bhnij', q, k) * decay
    q_in = q * jnp.exp(g)[..., None]
    k_out = k * jnp.exp(g[..., -1:] - g)[..., None]
    g_end = jnp.exp(g[..., -1])
    xs = tuple(jnp.moveaxis(t, 2, 0) for t in (q_in, k_out, u, w, qk, g_end))

    def step(state, inp):
        q_c, k_c, u_c, w_c, a_c, ge = inp
        v_new = u_c - jnp.einsum('bhcd,bhdv->bhcv', w_c, state)
        o = jnp.einsum('bhcd,bhdv->bhcv', q_c, state) + jnp.einsum('bhij,bhjv->bhiv', a_c, v_new)
        state = state * ge[..., None, None] + jnp.einsum('bhcd,bhcv->bhdv', k_c, v_new)
        return state, o

    state0 = jnp.zeros((b, h, dk, dv), jnp.float32)
    _, o = lax.scan(step, state0, xs)
    o = jnp.moveaxis(o, 0, 2).reshape(b, h, s, dv)
    return jnp.moveaxis(o, 1, 2)

def gated_deltanet(h, w_in, conv_w, a_log, dt_bias, norm_g, w_out):
    b, s, _ = h.shape
    proj = h @ w_in
    o1 = GDN_CONV_CH
    o2 = o1 + GDN_V_WIDTH
    o3 = o2 + GDN_V_HEADS
    qkv = jax.nn.silu(causal_depthwise_conv(proj[..., :o1], conv_w)).astype(jnp.float32)
    z = proj[..., o1:o2].reshape(b, s, GDN_V_HEADS, GDN_HEAD_DIM).astype(jnp.float32)
    beta = jax.nn.sigmoid(proj[..., o2:o3].astype(jnp.float32))
    g = -jnp.exp(a_log.astype(jnp.float32)) * jax.nn.softplus(
        proj[..., o3:].astype(jnp.float32) + dt_bias.astype(jnp.float32))
    rep = GDN_V_HEADS // GDN_K_HEADS
    q = qkv[..., :GDN_QK_WIDTH].reshape(b, s, GDN_K_HEADS, GDN_HEAD_DIM)
    k = qkv[..., GDN_QK_WIDTH:2 * GDN_QK_WIDTH].reshape(b, s, GDN_K_HEADS, GDN_HEAD_DIM)
    v = qkv[..., 2 * GDN_QK_WIDTH:].reshape(b, s, GDN_V_HEADS, GDN_HEAD_DIM)
    q = jnp.repeat(l2_normalize(q), rep, axis=2)
    k = jnp.repeat(l2_normalize(k), rep, axis=2)
    o = chunk_gated_delta_rule(q, k, v, g, beta)
    o = rms_norm(o, norm_g) * jax.nn.silu(z)
    return o.reshape(b, s, GDN_V_WIDTH).astype(h.dtype) @ w_out

def mla_attention(h, cos, sin, w_in, q_norm_g, kv_norm_g, w_q_up, w_kv_up, w_out):
    b, s, _ = h.shape
    proj = h @ w_in
    q_a = proj[..., :MLA_Q_LORA]
    c_kv = rms_norm(proj[..., MLA_Q_LORA:MLA_Q_LORA + MLA_KV_LORA], kv_norm_g)
    k_rope = apply_rope(proj[..., MLA_Q_LORA + MLA_KV_LORA:], cos, sin)
    q = (rms_norm(q_a, q_norm_g) @ w_q_up).reshape(b, s, MLA_HEADS, MLA_NOPE + MLA_ROPE)
    q_nope = q[..., :MLA_NOPE]
    q_rope = apply_rope(q[..., MLA_NOPE:], cos[:, :, None, :], sin[:, :, None, :])
    w_kv = w_kv_up.reshape(MLA_KV_LORA, MLA_HEADS, MLA_NOPE + MLA_V)
    w_uk = w_kv[..., :MLA_NOPE]
    w_uv = w_kv[..., MLA_NOPE:]
    q_lat = jnp.einsum('bshn,chn->bshc', q_nope, w_uk)
    q_cat = jnp.concatenate([q_lat, q_rope], axis=-1)
    k_cat = jnp.concatenate([c_kv, k_rope], axis=-1)
    nb = s // MLA_Q_BLOCK
    ck = MLA_KV_LORA + MLA_ROPE
    q_blocks = jnp.moveaxis(q_cat.reshape(b, nb, MLA_Q_BLOCK, MLA_HEADS, ck), 1, 0)
    key_pos = jnp.arange(s)
    neg = jnp.finfo(jnp.float32).min

    def attend(args):
        q_blk, blk = args
        sc = jnp.einsum('bqhc,bkc->bhqk', q_blk, k_cat, preferred_element_type=jnp.float32) * MLA_SCALE
        q_pos = blk * MLA_Q_BLOCK + jnp.arange(MLA_Q_BLOCK)
        sc = jnp.where(key_pos[None, :] <= q_pos[:, None], sc, neg)
        a = jax.nn.softmax(sc, axis=-1).astype(c_kv.dtype)
        return jnp.einsum('bhqk,bkc->bqhc', a, c_kv)

    o_lat = lax.map(attend, (q_blocks, jnp.arange(nb)))
    o_lat = jnp.moveaxis(o_lat, 0, 1).reshape(b, s, MLA_HEADS, MLA_KV_LORA)
    o = jnp.einsum('bshc,chv->bshv', o_lat, w_uv).reshape(b, s, MLA_HEADS * MLA_V)
    return o @ w_out

def routed_experts(ht, expert_idx, expert_w, w_gate_up, w_down):
    t, d = ht.shape
    n_assign = t * MOE_TOP_K
    e_flat = expert_idx.reshape(-1)
    tok_flat = jnp.repeat(jnp.arange(t, dtype=jnp.int32), MOE_TOP_K)
    w_flat = expert_w.reshape(-1)
    order = jnp.argsort(e_flat)
    e_sorted = e_flat[order]
    tok_sorted = tok_flat[order]
    w_sorted = w_flat[order]
    counts = jnp.bincount(e_flat, length=MOE_EXPERTS)
    start = jnp.cumsum(counts) - counts
    padded = (counts + MOE_BLOCK - 1) // MOE_BLOCK * MOE_BLOCK
    pend = jnp.cumsum(padded)
    pstart = pend - padded
    dest = pstart[e_sorted] + jnp.arange(n_assign) - start[e_sorted]
    n_rows = -(-n_assign // MOE_BLOCK) * MOE_BLOCK + MOE_EXPERTS * MOE_BLOCK
    n_blocks = n_rows // MOE_BLOCK
    xd = jnp.zeros((n_rows, d), ht.dtype).at[dest].set(ht[tok_sorted])
    block_e = jnp.clip(jnp.searchsorted(pend, jnp.arange(n_blocks) * MOE_BLOCK, side='right'),
                       0, MOE_EXPERTS - 1)

    def expert_block(args):
        xb, e = args
        gu = xb @ w_gate_up[e]
        return (jax.nn.silu(gu[:, :MOE_FF]) * gu[:, MOE_FF:]) @ w_down[e]

    out = lax.map(expert_block, (xd.reshape(n_blocks, MOE_BLOCK, d), block_e)).reshape(n_rows, d)
    contrib = out[dest].astype(jnp.float32) * w_sorted[:, None]
    return jax.ops.segment_sum(contrib, tok_sorted, num_segments=t).astype(ht.dtype)

def hierarchical_moe(h, w_router_group, w_router_expert, w_gate_up, w_down):
    b, s, d = h.shape
    t = b * s
    ht = h.reshape(t, d)
    p_group = jax.nn.softmax((ht @ w_router_group).astype(jnp.float32), axis=-1)
    g_prob, g_idx = lax.top_k(p_group, 1)
    e_logits = (ht @ w_router_expert).astype(jnp.float32).reshape(t, MOE_GROUPS, MOE_EXPERTS_PER_GROUP)
    in_group = e_logits[jnp.arange(t), g_idx[:, 0]]
    p_exp = jax.nn.softmax(in_group, axis=-1)
    e_prob, e_local = lax.top_k(p_exp, MOE_TOP_K)
    e_prob = e_prob / jnp.sum(e_prob, axis=-1, keepdims=True)
    expert_idx = g_idx * MOE_EXPERTS_PER_GROUP + e_local
    expert_w = g_prob * e_prob
    return routed_experts(ht, expert_idx, expert_w, w_gate_up, w_down).reshape(b, s, d)

def setup_inputs(seed: int = 0) -> dict:
    key = jax.random.key(seed)
    ks = jax.random.split(key, 32)
    f32 = jnp.float32

    def normal(k, shape, fan_in):
        return jax.random.normal(k, shape, f32) * (fan_in ** -0.5)

    def gain(k, shape):
        return 1.0 + 0.02 * jax.random.normal(k, shape, f32)

    offsets = jax.random.randint(ks[2], (BATCH,), 0, 4096, dtype=jnp.int32)
    positions = offsets[:, None] + jnp.arange(SEQ, dtype=jnp.int32)[None, :]
    dt = jnp.exp(jax.random.uniform(ks[8], (N_GDN_LAYERS, GDN_V_HEADS), f32,
                                    math.log(1e-3), math.log(1e-1)))
    return {
        'x': jax.random.normal(ks[0], (BATCH, SEQ, D_MODEL), f32),
        'p': jax.random.normal(ks[1], (DEPTH, BATCH, SEQ, PLE_DIM), f32),
        'positions': positions,
        'norm_mix_g': gain(ks[3], (DEPTH, D_MODEL)),
        'norm_ffn_g': gain(ks[4], (DEPTH, D_MODEL)),
        'norm_ple_g': gain(ks[5], (DEPTH, D_MODEL)),
        'gdn_w_in': normal(ks[6], (N_GDN_LAYERS, D_MODEL, GDN_IN_WIDTH), D_MODEL),
        'gdn_conv_w': normal(ks[7], (N_GDN_LAYERS, GDN_CONV_WIDTH, GDN_CONV_CH), GDN_CONV_WIDTH),
        'gdn_a_log': jnp.log(jax.random.uniform(ks[9], (N_GDN_LAYERS, GDN_V_HEADS), f32, 1.0, 16.0)),
        'gdn_dt_bias': dt + jnp.log(-jnp.expm1(-dt)),
        'gdn_norm_g': gain(ks[10], (N_GDN_LAYERS, GDN_HEAD_DIM)),
        'gdn_w_out': normal(ks[11], (N_GDN_LAYERS, GDN_V_WIDTH, D_MODEL), GDN_V_WIDTH),
        'mla_w_in': normal(ks[12], (N_MLA_LAYERS, D_MODEL, MLA_IN_WIDTH), D_MODEL),
        'mla_q_norm_g': gain(ks[13], (N_MLA_LAYERS, MLA_Q_LORA)),
        'mla_kv_norm_g': gain(ks[14], (N_MLA_LAYERS, MLA_KV_LORA)),
        'mla_w_q_up': normal(ks[15], (N_MLA_LAYERS, MLA_Q_LORA, MLA_HEADS * (MLA_NOPE + MLA_ROPE)), MLA_Q_LORA),
        'mla_w_kv_up': normal(ks[16], (N_MLA_LAYERS, MLA_KV_LORA, MLA_HEADS * (MLA_NOPE + MLA_V)), MLA_KV_LORA),
        'mla_w_out': normal(ks[17], (N_MLA_LAYERS, MLA_HEADS * MLA_V, D_MODEL), MLA_HEADS * MLA_V),
        'moe_router_group': normal(ks[18], (DEPTH, D_MODEL, MOE_GROUPS), D_MODEL),
        'moe_router_expert': normal(ks[19], (DEPTH, D_MODEL, MOE_EXPERTS), D_MODEL),
        'moe_w_gate_up': normal(ks[20], (DEPTH, MOE_EXPERTS, D_MODEL, 2 * MOE_FF), D_MODEL),
        'moe_w_down': normal(ks[21], (DEPTH, MOE_EXPERTS, MOE_FF, D_MODEL), MOE_FF),
        'ple_w_proj': normal(ks[22], (DEPTH, PLE_DIM, D_MODEL), PLE_DIM),
        'ple_w_gate': normal(ks[23], (DEPTH, D_MODEL, D_MODEL), D_MODEL),
        'final_norm_g': gain(ks[24], (D_MODEL,)),
    }

def reference(x, p, positions, norm_mix_g, norm_ffn_g, norm_ple_g,
              gdn_w_in, gdn_conv_w, gdn_a_log, gdn_dt_bias, gdn_norm_g, gdn_w_out,
              mla_w_in, mla_q_norm_g, mla_kv_norm_g, mla_w_q_up, mla_w_kv_up, mla_w_out,
              moe_router_group, moe_router_expert, moe_w_gate_up, moe_w_down,
              ple_w_proj, ple_w_gate, final_norm_g):
    cos, sin = rope_tables(positions)
    for i in range(DEPTH):
        j = i // N_MIXERS
        h = rms_norm(x, norm_mix_g[i])
        if i % N_MIXERS == 0:
            x = x + gated_deltanet(h, gdn_w_in[j], gdn_conv_w[j], gdn_a_log[j], gdn_dt_bias[j],
                                   gdn_norm_g[j], gdn_w_out[j])
        else:
            x = x + mla_attention(h, cos, sin, mla_w_in[j], mla_q_norm_g[j], mla_kv_norm_g[j],
                                  mla_w_q_up[j], mla_w_kv_up[j], mla_w_out[j])
        h = rms_norm(x, norm_ffn_g[i])
        x = x + hierarchical_moe(h, moe_router_group[i], moe_router_expert[i],
                                 moe_w_gate_up[i], moe_w_down[i])
        gate = jax.nn.sigmoid(rms_norm(x, norm_ple_g[i]) @ ple_w_gate[i])
        x = x + (p[i] @ ple_w_proj[i]) * gate
    return rms_norm(x, final_norm_g)


_drawn_inputs = setup_inputs


def setup_inputs(seed=0):
    import zlib

    import numpy as np

    out = dict(_drawn_inputs(seed))
    spreads = {}
    factors = {'norm_ple_g': 8.0, 'mla_q_norm_g': 8.0, 'mla_kv_norm_g': 8.0, 'final_norm_g': 2.85}
    for name, (base, spread) in spreads.items():
        noise = np.random.default_rng([zlib.crc32(name.encode()), seed]).standard_normal(out[name].shape)
        drawn = base * np.exp(spread * noise) if base else spread * noise
        out[name] = __import__('jax').numpy.asarray(drawn.astype(out[name].dtype))
    for name, factor in factors.items():
        out[name] = (out[name] * factor).astype(out[name].dtype)
    return out
```

```python
from contextlib import ExitStack, contextmanager

import numpy as np
import concourse.bass as bass
from concourse import mybir

P = 128
F32 = mybir.dt.float32
I32 = mybir.dt.int32
U32 = mybir.dt.uint32
ALU = mybir.AluOpType
ACT = mybir.ActivationFunctionType
AX = mybir.AxisListType.X

SEQ, D = 512, 1024
T = SEQ // P
KD = D // P
EPS = 1e-6

EXPERTS, GROUPS, PER_GROUP, FF = 64, 8, 8, 256
SLOTS = 32
OVER = 2 * SEQ // SLOTS
ROWS = (EXPERTS + OVER) * SLOTS
NBUF = 4
GU = KD * 2 * FF
DN = 2 * D


class Memory:
    pass


@contextmanager
def semaphores_of(nc, g):
    outer, taken = g.sem, []

    def take(name):
        taken.append(nc.alloc_semaphore(name=name))
        return taken[-1]
    g.sem = take
    yield
    g.sem = outer
    nc.clear_and_free_semaphores(taken)
    nc.all_engine_barrier()


def make_shared(nc, ctx):
    def sb(name, shape, dt=F32):
        return ctx.enter_context(nc.sbuf_tensor(name, shape, dt))
    g = Memory()
    g.sem = lambda name: ctx.enter_context(nc.semaphore(name))
    g.bank = [ctx.enter_context(nc.psum_tensor(f"bank{i}", [P, 512], F32)) for i in range(8)]
    g.x = sb("x_res", [P, T, D])
    g.hT = sb("hT", [P, KD, SEQ])
    g.big = sb("big", [P, 8192])
    g.xn = g.big[:, 0:T * D].rearrange("p (t d) -> p t d", t=T)
    g.w = sb("w_ring", [P, NBUF, GU + DN])
    g.ident = sb("ident", [P, P])
    g.ones = sb("ones", [P, P])
    g.tri = sb("tri", [P, P])
    g.tri_strict = sb("tri_strict", [P, P])
    g.eps = sb("eps", [P, 1])
    g.sel = sb("sel", [P, 2, SLOTS])
    g.half = sb("half", [P, 2])
    g.iota8 = sb("iota8", [P, 8])
    g.iota_e = sb("iota_e", [P, EXPERTS])
    g.iota_b = sb("iota_b", [P, OVER])
    g.gains = sb("gains", [P, 6, KD])
    g.ss = sb("ss", [P, T])
    g.lnss = sb("lnss", [P, T])
    g.ss2 = sb("ss2", [P, T])
    g.rstd = sb("rstd", [P, T])
    return g


def stage_setup(nc, g, a):
    step, small, xin = g.sem("setup_step"), g.sem("small_loaded"), g.sem("x_loaded")
    with nc.Block() as block:
        @block.sync
        def _(sp):
            sp.dma_start(g.x[:, :, :], a["x"][0].rearrange("(t p) d -> p t d", p=P)).then_inc(xin, 16)
            for n, src in enumerate((a["norm_mix_g"], a["norm_ffn_g"], a["norm_ple_g"])):
                for layer in range(2):
                    sp.dma_start(g.gains[:, 2 * n + layer, :],
                                 src[layer].rearrange("(p k) -> p k", k=KD)).then_inc(small, 16)
            sp.wait_ge(small, 96)
            sp.wait_ge(xin, 16)

        @block.gpsimd
        def _(pool):
            count = [0]

            def done(ins):
                count[0] += 1
                ins.then_inc(step, 1)
                pool.wait_ge(step, count[0])

            pool.memset(g.ones[:, :], 1.0).then_inc(step, 1)
            pool.memset(g.eps[:, :], EPS).then_inc(step, 1)
            pool.memset(g.ident[:, :], 0.0).then_inc(step, 1)
            pool.memset(g.tri[:, :], 1.0).then_inc(step, 1)
            pool.memset(g.tri_strict[:, :], 1.0).then_inc(step, 1)
            pool.memset(g.sel[:, :, :], 0.0).then_inc(step, 1)
            count[0] = 6
            done(pool.memset(g.half[:, :], 0.0))
            for q in range(4):
                done(pool.memset(g.half[32 * q:32 * q + 32, q % 2:q % 2 + 1], 1.0))
            done(pool.affine_select(out=g.ident[:, :], in_=g.ident[:, :], compare_op=ALU.not_equal, fill=1.0,
                                    base=0, pattern=[[-1, P]], channel_multiplier=1))
            done(pool.affine_select(out=g.tri[:, :], in_=g.tri[:, :], compare_op=ALU.is_ge, fill=0.0,
                                    base=0, pattern=[[1, P]], channel_multiplier=-1))
            done(pool.affine_select(out=g.tri_strict[:, :], in_=g.tri_strict[:, :], compare_op=ALU.is_gt, fill=0.0,
                                    base=0, pattern=[[1, P]], channel_multiplier=-1))
            for q in range(2):
                done(pool.affine_select(out=g.sel[:, :, :], in_=g.sel[:, :, :], compare_op=ALU.not_equal, fill=1.0,
                                        base=-32 * q, pattern=[[-64, 2], [-1, SLOTS]], channel_multiplier=1))
            done(pool.iota(g.iota8[:, :], pattern=[[1, 8]], base=-8, channel_multiplier=0,
                           allow_small_or_imprecise_dtypes=True))
            done(pool.iota(g.iota_e[:, :], pattern=[[SLOTS, EXPERTS]], base=0, channel_multiplier=0,
                           allow_small_or_imprecise_dtypes=True))
            done(pool.iota(g.iota_b[:, :], pattern=[[1, OVER]], base=0, channel_multiplier=0,
                           allow_small_or_imprecise_dtypes=True))


def stage_norm(nc, g, tag, gain, sync_work=None):
    sq, rs, xn = g.sem(tag + "_squares"), g.sem(tag + "_rstd"), g.sem(tag + "_xn")
    tp, ev = g.sem(tag + "_transposed"), [g.sem(tag + "_taken_dve"), g.sem(tag + "_taken_act")]
    gcol = g.gains[:, gain, :]
    with nc.Block() as block:
        if sync_work:
            block.sync(sync_work)

        @block.scalar
        def _(act):
            for t in range(T):
                act.activation(g.xn[:, t, :], g.x[:, t, :], ACT.Square, accum_out=g.ss[:, t:t + 1]).then_inc(sq, 1)
            act.wait_ge(sq, T)
            act.activation(g.lnss[:, :], g.ss[:, :], ACT.Ln, scale=1.0 / D, bias=g.eps[:, 0:1]).then_inc(rs, 1)
            act.wait_ge(rs, 1)
            act.activation(g.rstd[:, :], g.lnss[:, :], ACT.Exp, scale=-0.5).then_inc(rs, 1)
            for k in range(1, KD, 2):
                act.wait_ge(tp, k + 1)
                act.activation(g.hT[:, k, :], g.bank[k][:, :], ACT.Copy, scale=gcol[:, k:k + 1]).then_inc(ev[1], 1)

        @block.vector
        def _(dve):
            dve.wait_ge(rs, 2)
            for t in range(T):
                dve.tensor_scalar(g.xn[:, t, :], g.x[:, t, :], g.rstd[:, t:t + 1], None, ALU.mult).then_inc(xn, 1)
            for k in range(0, KD, 2):
                dve.wait_ge(tp, k + 1)
                dve.tensor_scalar(g.hT[:, k, :], g.bank[k][:, :], gcol[:, k:k + 1], None, ALU.mult).then_inc(ev[0], 1)

        @block.tensor
        def _(pe):
            pe.wait_ge(xn, T)
            for k in range(KD):
                for t in range(T):
                    last = pe.transpose(g.bank[k][:, t * P:(t + 1) * P], g.xn[:, t, k::KD], g.ident[:, :])
                last.then_inc(tp, 1)


def moe_memory(nc, ctx, g):
    def sb(name, shape, dt=F32):
        return ctx.enter_context(nc.sbuf_tensor(name, shape, dt))
    m = Memory()
    m.wr = sb("w_router", [P, KD, GROUPS + EXPERTS])
    m.lg = sb("logits", [P, T, GROUPS + EXPERTS])
    m.s = {n: sb("r_" + n, [P, T]) for n in
           "gmax gidx gz gprob m1 i1 m2 i2 dif q s r".split()}
    m.e8 = {n: sb("r_" + n, [P, T, 8]) for n in "eq cand ohg gexp ing oh1 oh2 masked".split()}
    m.ew = [sb(f"expert_w{k}", [P, T]) for k in range(2)]
    m.oh = [sb(f"onehot{k}", [P, T, EXPERTS]) for k in range(2)]
    m.both = sb("onehot_both", [P, T, EXPERTS])
    m.rank = sb("rank", [P, T, EXPERTS])
    m.tmp = sb("rank_tmp", [P, T, EXPERTS])
    m.cnt = sb("cnt", [P, EXPERTS])
    m.cnt_i = sb("cnt_i", [P, EXPERTS], I32)
    m.nov = sb("nov", [P, EXPERTS])
    m.cs = [sb(f"cs{i}", [P, EXPERTS]) for i in range(2)]
    m.base = sb("base", [P, EXPERTS])
    m.first = sb("first", [P, EXPERTS])
    m.destf = sb("destf", [P, 2, T])
    m.dest = [sb(f"dest{k}_{t}", [P, 1], U32) for k in range(2) for t in range(T)]
    m.cmp = sb("cmp", [1, OVER, EXPERTS])
    m.tblf = sb("tblf", [1, OVER + 1])
    m.tbl = sb("tbl", [1, OVER + 1], I32)
    m.xT = [sb(f"xT{i}", [P, KD, SLOTS]) for i in range(2)]
    m.sg = [sb(f"sg{i}", [P, 64]) for i in range(2)]
    m.um = [sb(f"um{i}", [P, 2, 64]) for i in range(2)]
    m.h2 = [sb(f"h2_{i}", [P, 2, 64]) for i in range(2)]
    m.hTe = [sb(f"hTe{i}", [P, 2, SLOTS]) for i in range(2)]
    m.y = [sb(f"y{i}", [P, 256]) for i in range(2)]
    m.xs = [g.big[0:SLOTS, 4096 + D * i:4096 + D * (i + 1)] for i in range(NBUF)]
    m.gu = [g.w[:, i, 0:GU].rearrange("p (k f) -> p k f", k=KD) for i in range(NBUF)]
    m.dn = [g.w[:, i, GU:GU + DN].rearrange("p (i d) -> p i d", i=2) for i in range(NBUF)]
    m.xd = nc.dram_tensor("rows_in", [ROWS, D], F32, kind="Internal").ap()
    m.yd = nc.dram_tensor("rows_out", [ROWS, D], F32, kind="Internal").ap()
    m.loaded = [[g.sem(f"expert_w_loaded{l}_{i}") for i in range(NBUF)] for l in range(2)]
    return m


def load_expert(sp, m, a, layer, buf, e, signal):
    if isinstance(e, int):
        gu, dn = a["moe_w_gate_up"][layer, e], a["moe_w_down"][layer, e]
        gu, dn = gu.rearrange("(p k) f -> p k f", k=KD), dn.rearrange("(i p) d -> p i d", p=P)
    else:
        gu = a["moe_w_gate_up"][layer, bass.ds(e, 1)].rearrange("a (p k) f -> p (a k) f", k=KD)
        dn = a["moe_w_down"][layer, bass.ds(e, 1)].rearrange("a (i p) d -> p (a i) d", p=P)
    sp.dma_start(m.gu[buf], gu).then_inc(signal, 16)
    sp.dma_start(m.dn[buf], dn).then_inc(signal, 16)


def stage_route(nc, g, m, a, layer, sync_work=None):
    tag = f"route{layer}"
    wr_in, logits, lgc = g.sem(tag + "_w_in"), g.sem(tag + "_logits"), g.sem(tag + "_logits_taken")
    vs, ex_in, ex = g.sem(tag + "_step"), g.sem(tag + "_exp_in"), g.sem(tag + "_exp")
    both, counted, rows = g.sem(tag + "_onehots"), g.sem(tag + "_counted"), g.sem(tag + "_dest")
    sent = g.sem(tag + "_rows_sent")
    with nc.Block() as block:
        @block.sync
        def _(sp):
            if sync_work:
                sync_work(sp)

        @block.tensor
        def _(pe):
            pe.wait_ge(m.wr_in[layer], 32)
            n = GROUPS + EXPERTS
            for t in range(T):
                for k in range(KD):
                    last = pe.matmul(g.bank[0][:, t * n:(t + 1) * n], g.hT[:, k, t * P:(t + 1) * P], m.wr[:, k, :],
                                     start=k == 0, stop=k == KD - 1)
            last.then_inc(logits, 1)
            pe.wait_ge(both, 1)
            for t in range(T):
                for u in range(t + 1):
                    pe.matmul(g.bank[1][:, t * EXPERTS:(t + 1) * EXPERTS], g.ones[:, :] if u < t else g.tri_strict[:, :],
                              m.both[:, u, :], start=u == 0, stop=u == t)
            for u in range(T):
                last = pe.matmul(g.bank[2][:, 0:EXPERTS], g.ones[:, :], m.both[:, u, :], start=u == 0, stop=u == T - 1)
            last.then_inc(counted, 1)

        @block.scalar
        def _(act):
            act.wait_ge(ex_in, 1)
            act.activation(m.e8["gexp"][:, :, :], m.e8["cand"][:, :, :], ACT.Exp).then_inc(ex, 1)
            act.wait_ge(ex_in, 2)
            act.activation(m.s["q"][:, :], m.s["dif"][:, :], ACT.Exp).then_inc(ex, 1)

        @block.vector
        def _(dve):
            count = [0]

            def done(ins):
                count[0] += 1
                ins.then_inc(vs, 1)
                dve.wait_ge(vs, count[0])

            def bc(v, n):
                return v[:, :].unsqueeze(2).to_broadcast([P, T, n])

            def first_of(src, top, idx, onehot):
                done(dve.tensor_reduce(top[:, :], src, AX, ALU.max))
                done(dve.tensor_tensor(m.e8["eq"][:, :, :], src, bc(top, 8), ALU.is_equal))
                done(dve.tensor_tensor(m.e8["masked"][:, :, :], m.e8["eq"][:, :, :], iota8, ALU.mult))
                done(dve.tensor_reduce(idx[:, :], m.e8["masked"][:, :, :], AX, ALU.min))
                done(dve.tensor_tensor(onehot[:, :, :], iota8, bc(idx, 8), ALU.is_equal))

            iota8 = g.iota8[:, :].unsqueeze(1).to_broadcast([P, T, 8])
            s, e8 = m.s, m.e8
            dve.wait_ge(logits, 1)
            done(dve.tensor_copy(m.lg[:, :, :], g.bank[0][:, 0:T * 72].rearrange("p (t n) -> p t n", t=T)))
            gl = m.lg[:, :, 0:GROUPS]
            el = m.lg[:, :, GROUPS:].rearrange("p t (g e) -> p t g e", g=GROUPS)
            first_of(gl, s["gmax"], s["gidx"], e8["ohg"])
            dve.tensor_tensor(e8["cand"][:, :, :], gl, bc(s["gmax"], 8), ALU.subtract).then_inc(ex_in, 1)
            picked = m.tmp[:, :, :].rearrange("p t (g e) -> p t g e", g=GROUPS)
            done(dve.tensor_tensor(picked, el, e8["ohg"][:, :, :].unsqueeze(3).to_broadcast([P, T, GROUPS, PER_GROUP]),
                                   ALU.mult))
            done(dve.tensor_reduce(e8["ing"][:, :, :], m.tmp[:, :, :].rearrange("p t (g e) -> p t e g", g=GROUPS),
                                   AX, ALU.add))
            first_of(e8["ing"][:, :, :], s["m1"], s["i1"], e8["oh1"])
            done(dve.scalar_tensor_tensor(out=e8["eq"][:, :, :], in0=e8["oh1"][:, :, :],
                                          scalar=-3e38, in1=e8["ing"][:, :, :], op0=ALU.mult, op1=ALU.add))
            done(dve.tensor_copy(e8["ing"][:, :, :], e8["eq"][:, :, :]))
            first_of(e8["ing"][:, :, :], s["m2"], s["i2"], e8["oh2"])
            dve.tensor_tensor(s["dif"][:, :], s["m2"][:, :], s["m1"][:, :], ALU.subtract).then_inc(ex_in, 1)
            for k, name in enumerate(("oh1", "oh2")):
                done(dve.tensor_tensor(m.oh[k][:, :, :].rearrange("p t (g e) -> p t g e", g=GROUPS),
                                       e8["ohg"][:, :, :].unsqueeze(3).to_broadcast([P, T, GROUPS, PER_GROUP]),
                                       e8[name][:, :, :].unsqueeze(2).to_broadcast([P, T, GROUPS, PER_GROUP]), ALU.mult))
            dve.tensor_tensor(m.both[:, :, :], m.oh[0][:, :, :], m.oh[1][:, :, :], ALU.add).then_inc(both, 1)
            dve.wait_ge(ex, 2)
            done(dve.tensor_reduce(s["gz"][:, :], e8["gexp"][:, :, :], AX, ALU.add))
            done(dve.reciprocal(s["gprob"][:, :], s["gz"][:, :]))
            done(dve.tensor_scalar(s["s"][:, :], s["q"][:, :], 1.0, None, ALU.add))
            done(dve.reciprocal(s["r"][:, :], s["s"][:, :]))
            done(dve.tensor_tensor(m.ew[0][:, :], s["gprob"][:, :], s["r"][:, :], ALU.mult))
            done(dve.tensor_tensor(m.ew[1][:, :], m.ew[0][:, :], s["q"][:, :], ALU.mult))
            dve.wait_ge(counted, 1)
            done(dve.tensor_copy(m.rank[:, :, :], g.bank[1][:, 0:T * EXPERTS].rearrange("p (t e) -> p t e", t=T)))
            done(dve.tensor_scalar(m.cnt_i[:, :], g.bank[2][:, 0:EXPERTS], SLOTS - 1.0, None, ALU.add))
            done(dve.tensor_scalar(m.cnt_i[:, :], m.cnt_i[:, :], SLOTS.bit_length() - 1, None, ALU.arith_shift_right))
            done(dve.tensor_scalar(m.nov[:, :], m.cnt_i[:, :], -1.0, 0.0, ALU.add, ALU.max))
            done(dve.tensor_copy(m.cs[0][:, :], m.nov[:, :]))
            now, n = 0, 1
            while n < EXPERTS:
                done(dve.tensor_copy(m.cs[1 - now][:, 0:n], m.cs[now][:, 0:n]))
                done(dve.tensor_tensor(m.cs[1 - now][:, n:], m.cs[now][:, n:], m.cs[now][:, 0:EXPERTS - n], ALU.add))
                now, n = 1 - now, 2 * n
            cs = m.cs[now]
            done(dve.tensor_tensor(m.base[:, :], cs[:, :], m.nov[:, :], ALU.subtract))
            done(dve.tensor_scalar(m.base[:, :], m.base[:, :], float(SLOTS), float(SLOTS * (EXPERTS - 1)), ALU.mult, ALU.add))
            done(dve.tensor_tensor(m.first[:, :], g.iota_e[:, :], m.base[:, :], ALU.subtract))
            done(dve.tensor_scalar(m.tmp[:, :, :], m.rank[:, :, :], float(SLOTS), None, ALU.is_lt))
            done(dve.tensor_tensor(m.tmp[:, :, :], m.tmp[:, :, :],
                                   m.first[:, :].unsqueeze(1).to_broadcast([P, T, EXPERTS]), ALU.mult))
            done(dve.tensor_tensor(m.rank[:, :, :], m.rank[:, :, :], m.tmp[:, :, :], ALU.add))
            done(dve.tensor_tensor(m.rank[:, :, :], m.rank[:, :, :],
                                   m.base[:, :].unsqueeze(1).to_broadcast([P, T, EXPERTS]), ALU.add))
            for k in range(2):
                done(dve.tensor_tensor(m.tmp[:, :, :], m.rank[:, :, :], m.oh[k][:, :, :], ALU.mult))
                done(dve.tensor_reduce(m.destf[:, k, :], m.tmp[:, :, :], AX, ALU.add))
                for t in range(T):
                    dve.tensor_copy(m.dest[k * T + t][:, :], m.destf[:, k, t:t + 1]).then_inc(rows, 1)
            done(dve.tensor_tensor(m.cmp[:, :, :], cs[0:1, :].unsqueeze(1).to_broadcast([1, OVER, EXPERTS]),
                                   g.iota_b[0:1, :].unsqueeze(2).to_broadcast([1, OVER, EXPERTS]), ALU.is_le))
            done(dve.tensor_reduce(m.tblf[:, 0:OVER], m.cmp[:, :, :], AX, ALU.add))
            done(dve.tensor_scalar(m.tbl[:, 0:OVER], m.tblf[:, 0:OVER], EXPERTS - 1.0, None, ALU.min))
            done(dve.tensor_scalar(m.tbl[:, OVER:OVER + 1], cs[0:1, EXPERTS - 1:EXPERTS], 1.0, None, ALU.max))

        @block.gpsimd
        def _(pool):
            for i in range(2 * T):
                pool.wait_ge(rows, i + 1)
                pool.indirect_dma_start(m.xd, bass.IndirectOffsetOnAxis(ap=m.dest[i][:, 0:1], axis=0),
                                        g.xn[:, i % T, :], None).then_inc(sent, 16)
            pool.wait_ge(sent, 16 * 2 * T)


def stage_experts(nc, g, m, a, layer):
    tag = f"exp{layer}"
    loaded = m.loaded[layer]
    xs_in = [g.sem(f"{tag}_rows_in{i}") for i in range(NBUF)]
    names = "xt xT gu sg um h2 ht hT dn y".split()
    S = {n: g.sem(f"{tag}_{n}") for n in names}
    y_out = [g.sem(f"{tag}_y_out{i}") for i in range(2)]
    gcol = g.gains[:, 2 + layer, :].unsqueeze(2).to_broadcast([P, KD, SLOTS])
    PASSES = EXPERTS // NBUF
    with nc.Block() as block:
        @block.sync
        def _(sp):
            for i in range(NBUF):
                sp.dma_start(m.xs[i], m.xd[SLOTS * i:SLOTS * (i + 1), :]).then_inc(xs_in[i], 16)
            with sp.Fori(1, PASSES) as it:
                for i in range(NBUF):
                    sp.wait_ge(S["dn"], NBUF * (it - 1) + i + 1)
                    load_expert(sp, m, a, layer, i, NBUF * it + i, loaded[i])
                    sp.dma_start(m.xs[i], m.xd[bass.ds(SLOTS * (NBUF * it + i), SLOTS), :]).then_inc(xs_in[i], 16)

        @block.tensor
        def _(pe):
            def rows(it, i):
                j = i % 2
                pe.wait_ge(xs_in[i], 16 * (it + 1))
                if not (isinstance(it, int) and it == 0 and i < 2):
                    pe.wait_ge(S["xT"], NBUF * it + i - 1)
                for k in range(KD):
                    last = pe.matmul(g.bank[j][:, SLOTS * k:SLOTS * (k + 1)], m.xs[i][:, k::KD],
                                     g.ident[0:SLOTS, 0:SLOTS], start=True, stop=True)
                last.then_inc(S["xt"], 1)

            def gate_up(it, i):
                j = i % 2
                pe.wait_ge(loaded[i], 32 * (it + 1))
                pe.wait_ge(S["xT"], NBUF * it + i + 1)
                if not (isinstance(it, int) and it == 0 and i < 2):
                    pe.wait_ge(S["um"], NBUF * it + i - 1)
                    pe.wait_ge(S["sg"], NBUF * it + i - 1)
                for k in range(KD):
                    w = m.gu[i][:, k, :].rearrange("p (h q c) -> p q h c", h=2, q=4)
                    for q in range(4):
                        last = pe.matmul(g.bank[2 + j][32 * q:32 * q + 32, 0:P].rearrange("p (h c) -> p h c", h=2),
                                         m.xT[j][:, k, :], w[:, q], start=k == 0, stop=k == KD - 1)
                last.then_inc(S["gu"], 1)

            def down(it, i):
                j, b = (i - 1) % NBUF, NBUF * it + i - 1
                r = j % 2
                pe.wait_ge(S["h2"], b + 1)
                if not (isinstance(b, int) and b < 2):
                    pe.wait_ge(S["hT"], b - 1)
                pe.matmul(g.bank[4 + r][:, 0:2 * SLOTS], m.h2[r][:, :, :].rearrange("p h c -> p (h c)"),
                          g.sel[:, :, :].rearrange("p i s -> p (i s)"), start=True, stop=True).then_inc(S["ht"], 1)
                pe.wait_ge(S["hT"], b + 1)
                if not (isinstance(b, int) and b < 2):
                    pe.wait_ge(S["y"], b - 1)
                for n in range(2):
                    for q in range(4):
                        last = pe.matmul(g.bank[6 + r][32 * q:32 * q + 32, 0:256], m.hTe[r][:, n, :],
                                         m.dn[j][:, n, 256 * q:256 * (q + 1)], start=n == 0, stop=n == 1)
                last.then_inc(S["dn"], 1)

            def turn(it):
                for i in range(NBUF):
                    rows(it, i)
                    if not (isinstance(it, int) and it == 0 and i == 0):
                        down(it, i)
                    gate_up(it, i)

            turn(0)
            with pe.Fori(1, PASSES) as it:
                turn(it)
            down(PASSES, 0)

        def vector_turn(dve, it):
            first = isinstance(it, int)
            for i in range(NBUF):
                j, b = i % 2, NBUF * it + i
                early = first and i < 2
                dve.wait_ge(S["xt"], b + 1)
                if not early:
                    dve.wait_ge(S["gu"], b - 1)
                dve.tensor_tensor(m.xT[j][:, :, :], g.bank[j][:, 0:KD * SLOTS].rearrange("p (k s) -> p k s", k=KD),
                                  gcol, ALU.mult).then_inc(S["xT"], 1)
                dve.wait_ge(S["gu"], b + 1)
                dve.wait_ge(S["sg"], b + 1)
                dve.tensor_tensor(m.um[j][:, :, :], g.bank[2 + j][:, 64:128].unsqueeze(1).to_broadcast([P, 2, 64]),
                                  g.half[:, :].unsqueeze(2).to_broadcast([P, 2, 64]), ALU.mult).then_inc(S["um"], 1)
                dve.wait_ge(S["um"], b + 1)
                if not early:
                    dve.wait_ge(S["ht"], b - 1)
                dve.tensor_tensor(m.h2[j][:, :, :], m.um[j][:, :, :],
                                  m.sg[j][:, :].unsqueeze(1).to_broadcast([P, 2, 64]), ALU.mult).then_inc(S["h2"], 1)
                dve.wait_ge(S["ht"], b + 1)
                if not early:
                    dve.wait_ge(S["dn"], b - 1)
                dve.tensor_copy(m.hTe[j][:, :, :],
                                g.bank[4 + j][:, 0:2 * SLOTS].rearrange("p (i s) -> p i s", i=2)).then_inc(S["hT"], 1)

        @block.vector
        def _(dve):
            vector_turn(dve, 0)
            with dve.Fori(1, PASSES) as it:
                vector_turn(dve, it)

        def scalar_turn(act, it):
            first = isinstance(it, int)
            for i in range(NBUF):
                j, b = i % 2, NBUF * it + i
                early = first and i < 2
                act.wait_ge(S["gu"], b + 1)
                if not early:
                    act.wait_ge(S["h2"], b - 1)
                act.activation(m.sg[j][:, :], g.bank[2 + j][:, 0:64], ACT.Silu).then_inc(S["sg"], 1)
                act.wait_ge(S["dn"], b + 1)
                if not early:
                    act.wait_ge(y_out[j], 16 * 4 * (2 * it + i // 2))
                act.activation(m.y[j][:, :], g.bank[6 + j][:, 0:256], ACT.Copy).then_inc(S["y"], 1)

        @block.scalar
        def _(act):
            scalar_turn(act, 0)
            with act.Fori(1, PASSES) as it:
                scalar_turn(act, it)

        def store_turn(pool, it):
            for i in range(NBUF):
                j, b = i % 2, NBUF * it + i
                pool.wait_ge(S["y"], b + 1)
                for q in range(4):
                    pool.dma_start(m.yd[bass.ds(SLOTS * b, SLOTS), 256 * q:256 * (q + 1)],
                                   m.y[j][32 * q:32 * q + 32, :]).then_inc(y_out[j], 16)

        @block.gpsimd
        def _(pool):
            store_turn(pool, 0)
            with pool.Fori(1, PASSES) as it:
                store_turn(pool, it)
            for j in range(2):
                pool.wait_ge(y_out[j], 16 * 4 * EXPERTS // 2)


def stage_overflow(nc, g, m, a, layer):
    tag = f"over{layer}"
    names = "w xs xt xT gu sg um h2 ht hT dn y out".split()
    S = {n: g.sem(f"{tag}_{n}") for n in names}
    gcol = g.gains[:, 2 + layer, :].unsqueeze(2).to_broadcast([P, KD, SLOTS])

    def blocks(eng):
        return eng.value_load(m.tbl[0:1, OVER:OVER + 1], min_val=1, max_val=OVER)

    with nc.Block() as block:
        @block.sync
        def _(sp):
            with sp.Fori(0, blocks(sp)) as it:
                sp.wait_ge(S["dn"], it + 1)
                e = sp.value_load(m.tbl[0:1, bass.ds(it, 1)], min_val=0, max_val=EXPERTS - 1)
                load_expert(sp, m, a, layer, 0, e, S["w"])
                sp.dma_start(m.xs[0], m.xd[bass.ds(SLOTS * (EXPERTS + it), SLOTS), :]).then_inc(S["xs"], 16)

        @block.tensor
        def _(pe):
            pe.sem_inc(S["dn"], 1)
            with pe.Fori(0, blocks(pe)) as it:
                pe.wait_ge(S["xs"], 16 * (it + 1))
                for k in range(KD):
                    last = pe.matmul(g.bank[0][:, SLOTS * k:SLOTS * (k + 1)], m.xs[0][:, k::KD],
                                     g.ident[0:SLOTS, 0:SLOTS], start=True, stop=True)
                last.then_inc(S["xt"], 1)
                pe.wait_ge(S["w"], 32 * (it + 1))
                pe.wait_ge(S["xT"], it + 1)
                for k in range(KD):
                    w = m.gu[0][:, k, :].rearrange("p (h q c) -> p q h c", h=2, q=4)
                    for q in range(4):
                        last = pe.matmul(g.bank[2][32 * q:32 * q + 32, 0:P].rearrange("p (h c) -> p h c", h=2),
                                         m.xT[0][:, k, :], w[:, q], start=k == 0, stop=k == KD - 1)
                last.then_inc(S["gu"], 1)
                pe.wait_ge(S["h2"], it + 1)
                pe.matmul(g.bank[4][:, 0:2 * SLOTS], m.h2[0][:, :, :].rearrange("p h c -> p (h c)"),
                          g.sel[:, :, :].rearrange("p i s -> p (i s)"), start=True, stop=True).then_inc(S["ht"], 1)
                pe.wait_ge(S["hT"], it + 1)
                for n in range(2):
                    for q in range(4):
                        last = pe.matmul(g.bank[6][32 * q:32 * q + 32, 0:256], m.hTe[0][:, n, :],
                                         m.dn[0][:, n, 256 * q:256 * (q + 1)], start=n == 0, stop=n == 1)
                last.then_inc(S["dn"], 1)
                pe.wait_ge(S["y"], it + 1)

        @block.vector
        def _(dve):
            with dve.Fori(0, blocks(dve)) as it:
                dve.wait_ge(S["xt"], it + 1)
                dve.tensor_tensor(m.xT[0][:, :, :], g.bank[0][:, 0:KD * SLOTS].rearrange("p (k s) -> p k s", k=KD),
                                  gcol, ALU.mult).then_inc(S["xT"], 1)
                dve.wait_ge(S["gu"], it + 1)
                dve.wait_ge(S["sg"], it + 1)
                dve.tensor_tensor(m.um[0][:, :, :], g.bank[2][:, 64:128].unsqueeze(1).to_broadcast([P, 2, 64]),
                                  g.half[:, :].unsqueeze(2).to_broadcast([P, 2, 64]), ALU.mult).then_inc(S["um"], 1)
                dve.wait_ge(S["um"], it + 1)
                dve.tensor_tensor(m.h2[0][:, :, :], m.um[0][:, :, :],
                                  m.sg[0][:, :].unsqueeze(1).to_broadcast([P, 2, 64]), ALU.mult).then_inc(S["h2"], 1)
                dve.wait_ge(S["ht"], it + 1)
                dve.tensor_copy(m.hTe[0][:, :, :],
                                g.bank[4][:, 0:2 * SLOTS].rearrange("p (i s) -> p i s", i=2)).then_inc(S["hT"], 1)

        @block.scalar
        def _(act):
            with act.Fori(0, blocks(act)) as it:
                act.wait_ge(S["gu"], it + 1)
                act.activation(m.sg[0][:, :], g.bank[2][:, 0:64], ACT.Silu).then_inc(S["sg"], 1)
                act.wait_ge(S["dn"], it + 2)
                act.activation(m.y[0][:, :], g.bank[6][:, 0:256], ACT.Copy).then_inc(S["y"], 1)
                act.wait_ge(S["out"], 16 * 4 * (it + 1))

        @block.gpsimd
        def _(pool):
            n = blocks(pool)
            with pool.Fori(0, n) as it:
                pool.wait_ge(S["y"], it + 1)
                for q in range(4):
                    pool.dma_start(m.yd[bass.ds(SLOTS * (EXPERTS + it), SLOTS), 256 * q:256 * (q + 1)],
                                   m.y[0][32 * q:32 * q + 32, :]).then_inc(S["out"], 16)
                pool.wait_ge(S["out"], 16 * 4 * (it + 1))


def stage_combine(nc, g, m, layer, sync_work=None):
    tag = f"comb{layer}"
    got = [g.sem(f"{tag}_row{i}") for i in range(2 * T)]
    added = g.sem(tag + "_added")
    rows = g.big[:, :].rearrange("p (n d) -> p n d", d=D)
    with nc.Block() as block:
        if sync_work:
            block.sync(sync_work)

        @block.gpsimd
        def _(pool):
            for i in range(2 * T):
                pool.indirect_dma_start(rows[:, i, :], None, m.yd,
                                        bass.IndirectOffsetOnAxis(ap=m.dest[i][:, 0:1], axis=0)).then_inc(got[i], 16)

        @block.vector
        def _(dve):
            for i in range(2 * T):
                t = i % T
                dve.wait_ge(got[i], 16)
                if i >= T:
                    dve.wait_ge(added, i - T + 1)
                dve.scalar_tensor_tensor(out=g.x[:, t, :], in0=rows[:, i, :], scalar=m.ew[i // T][:, t:t + 1],
                                         in1=g.x[:, t, :], op0=ALU.mult, op1=ALU.add).then_inc(added, 1)


def ple_load(sp, a, g, layer, wsem):
    flat = g.w[:, 2:4, :].rearrange("p n f -> p (n f)")
    sp.dma_start(flat[:, 0:KD * D].rearrange("p (k n) -> p k n", k=KD),
                 a["ple_w_gate"][layer].rearrange("(p k) n -> p k n", k=KD)).then_inc(wsem, 16)
    sp.dma_start(flat[:, KD * D:KD * D + 2 * D].rearrange("p (k n) -> p k n", k=2),
                 a["ple_w_proj"][layer].rearrange("(k p) n -> p k n", p=P)).then_inc(wsem, 16)


def stage_ple(nc, g, a, layer, wsem, sync_work=None):
    tag = f"ple{layer}"
    pin, tp, pT = g.sem(tag + "_p_in"), g.sem(tag + "_p_transposed"), g.sem(tag + "_pT")
    gate, proj, sig, mul, add = (g.sem(f"{tag}_{n}") for n in "gate proj sigmoid product added".split())
    pn = g.big[:, 4096:5120].rearrange("p (t c) -> p t c", t=T)
    pTt = g.big[:, 5120:6144].rearrange("p (k s) -> p k s", k=2)
    sg = [g.big[:, 6144 + 512 * i:6656 + 512 * i] for i in range(2)]
    pr = [g.big[:, 7168 + 512 * i:7680 + 512 * i] for i in range(2)]
    flat = g.w[:, 2:4, :].rearrange("p n f -> p (n f)")
    wg = flat[:, 0:KD * D].rearrange("p (k n) -> p k n", k=KD)
    wp = flat[:, KD * D:KD * D + 2 * D].rearrange("p (k n) -> p k n", k=2)
    steps = [(t, h) for t in range(T) for h in range(2)]
    with nc.Block() as block:
        @block.sync
        def _(sp):
            sp.dma_start(pn, a["p"][layer, 0].rearrange("(t p) c -> p t c", p=P)).then_inc(pin, 16)
            if sync_work:
                sync_work(sp)

        @block.tensor
        def _(pe):
            pe.wait_ge(pin, 16)
            for k in range(2):
                for t in range(T):
                    last = pe.transpose(g.bank[6 + k][:, t * P:(t + 1) * P], pn[:, t, k * P:(k + 1) * P], g.ident[:, :])
                last.then_inc(tp, 1)
            pe.wait_ge(wsem, 32)
            pe.wait_ge(pT, 2)
            for n, (t, h) in enumerate(steps):
                if n >= 3:
                    pe.wait_ge(sig, n - 2)
                for k in range(KD):
                    last = pe.matmul(g.bank[n % 3][:, :], g.hT[:, k, t * P:(t + 1) * P], wg[:, k, 512 * h:512 * (h + 1)],
                                     start=k == 0, stop=k == KD - 1)
                last.then_inc(gate, 1)
                if n >= 3:
                    pe.wait_ge(mul, n - 2)
                for k in range(2):
                    last = pe.matmul(g.bank[3 + n % 3][:, :], pTt[:, k, t * P:(t + 1) * P], wp[:, k, 512 * h:512 * (h + 1)],
                                     start=k == 0, stop=k == 1)
                last.then_inc(proj, 1)

        @block.scalar
        def _(act):
            for n in range(len(steps)):
                act.wait_ge(gate, n + 1)
                if n >= 2:
                    act.wait_ge(mul, n - 1)
                act.activation(sg[n % 2], g.bank[n % 3][:, :], ACT.Sigmoid).then_inc(sig, 1)

        @block.vector
        def _(dve):
            for k in range(2):
                dve.wait_ge(tp, k + 1)
                dve.tensor_copy(pTt[:, k, :], g.bank[6 + k][:, :]).then_inc(pT, 1)
            for n, (t, h) in enumerate(steps):
                dve.wait_ge(sig, n + 1)
                dve.wait_ge(proj, n + 1)
                if n >= 2:
                    dve.wait_ge(add, n - 1)
                dve.tensor_tensor(pr[n % 2], g.bank[3 + n % 3][:, :], sg[n % 2], ALU.mult).then_inc(mul, 1)
                dve.wait_ge(mul, n + 1)
                xv = g.x[:, t, 512 * h:512 * (h + 1)]
                dve.tensor_tensor(xv, xv, pr[n % 2], ALU.add).then_inc(add, 1)


def stage_zero(nc, g, m):
    zeroed, wz = g.sem("rows_zeroed"), g.sem("zeros_made")
    with nc.Block() as block:
        @block.gpsimd
        def _(pool):
            pool.memset(g.hT[:, :, :], 0.0).then_inc(wz, 1)
            pool.wait_ge(wz, 1)
            src = g.hT[:, :, :].rearrange("p k s -> p (k s)")
            chunks = [m.xd[n:n + 512, :] for n in range(0, ROWS, 512)]
            chunks += [m.yd[n:n + 512, :] for n in range(EXPERTS * SLOTS, ROWS, 512)]
            for rows in chunks:
                pool.dma_start(rows.rearrange("(p r) d -> p (r d)", p=P), src).then_inc(zeroed, 16)
            pool.wait_ge(zeroed, 16 * len(chunks))


def stage_final(nc, g, a, out):
    sq, rs, gin = g.sem("final_squares"), g.sem("final_rstd"), g.sem("final_gain_in")
    fin, sent = g.sem("final_rows"), g.sem("final_sent")
    gb = g.big[:, 4096:5120]
    with nc.Block() as block:
        @block.sync
        def _(sp):
            sp.dma_start(gb, a["final_norm_g"].partition_broadcast(P)).then_inc(gin, 16)
            for t in range(T):
                sp.wait_ge(fin, t + 1)
                sp.dma_start(out[0, t * P:(t + 1) * P, :], g.xn[:, t, :]).then_inc(sent, 16)
            sp.wait_ge(sent, 16 * T)

        @block.scalar
        def _(act):
            for t in range(T):
                act.activation(g.xn[:, t, :], g.x[:, t, :], ACT.Square, accum_out=g.ss[:, t:t + 1]).then_inc(sq, 1)
            act.wait_ge(sq, T)
            act.activation(g.lnss[:, :], g.ss[:, :], ACT.Ln, scale=1.0 / D, bias=g.eps[:, 0:1]).then_inc(rs, 1)
            act.wait_ge(rs, 1)
            act.activation(g.rstd[:, :], g.lnss[:, :], ACT.Exp, scale=-0.5).then_inc(rs, 1)

        @block.vector
        def _(dve):
            dve.wait_ge(rs, 2)
            dve.wait_ge(gin, 16)
            for t in range(T):
                dve.scalar_tensor_tensor(out=g.xn[:, t, :], in0=g.x[:, t, :], scalar=g.rstd[:, t:t + 1],
                                         in1=gb, op0=ALU.mult, op1=ALU.mult).then_inc(fin, 1)


HEADS = 16
NOPE, ROPE, VDIM, QL, KVL = 128, 64, 128, 256, 128
QK = NOPE + ROPE
MLA_SCALE = QK ** -0.5
NEG = -1e30


def workspace(g, first, nbufs):
    flat = g.w[:, first:first + nbufs, :].rearrange("p n f -> p (n f)")
    at = [0]

    def take(*shape):
        n = int(np.prod(shape))
        v = flat[:, at[0]:at[0] + n]
        at[0] += n
        assert at[0] <= nbufs * (GU + DN), at[0]
        if len(shape) == 2:
            v = v.rearrange("p (a b) -> p a b", a=shape[0])
        if len(shape) == 3:
            v = v.rearrange("p (a b c) -> p a b c", a=shape[0], b=shape[1])
        return v
    return take


def rope_columns():
    inv = (np.float32(10000.0) ** (-np.arange(0, ROPE, 2, dtype=np.float32) / np.float32(ROPE))).astype(np.float32)
    turns = np.repeat(np.array([0.25, 0.25, 0.5, 0.0], np.float32), 32)
    return np.stack([np.tile(inv, 4), turns, (turns.astype(np.float64) * 2 * np.pi).astype(np.float32)], axis=1)


def mla_memory(nc, g):
    s = Memory()
    take = workspace(g, 2, 2)
    s.wn = take(KD, QL + KVL)
    s.qn = take(T, QL)
    s.cs = take(SEQ)
    s.kdup = take(SEQ)
    s.ckv = take(T, KVL)
    s.ckvT = take(SEQ)
    s.qaT = take(2, SEQ)
    s.neg = take(P)
    s.dup = take(P)
    s.cols = take(4)
    s.gq = take(2)
    take = workspace(g, 1, 1)
    s.wr = take(KD, P)
    s.pos = take(SEQ).bitcast(I32)
    s.gkv = take(KVL)
    s.ang = take(SEQ)
    s.n = take(SEQ)
    h = Memory()
    flat = g.w[:, 2:4, :].rearrange("p n f -> p (n f)")
    at = [0]

    def reuse(*shape):
        n = int(np.prod(shape))
        v = flat[:, at[0]:at[0] + n]
        at[0] += n
        assert at[0] <= KD * (QL + KVL) + T * QL
        return v.rearrange("p (a b) -> p a b", a=shape[0]) if len(shape) == 2 else v
    h.qlatT, h.rot, h.qnT = reuse(SEQ), reuse(SEQ), reuse(SEQ)
    h.p = [reuse((t + 1) * P) for t in range(T)]
    h.wukT = reuse(P)
    take2 = workspace(g, 1, 1)
    h.pT = [take2((T - k) * P) for k in range(T)]
    h.olT = take2(SEQ)
    h.wq = [take2(2, 2 * P) for _ in range(2)]
    h.wkv = [take2(2 * P) for _ in range(2)]
    h.mx, h.nm, h.rs, h.ri = (take2(T) for _ in range(4))
    s.h = h
    return s


def stage_mla_in(nc, g, s, a, w_in):
    tag = "mla_in"
    cst, mm, rs, nat = g.sem(tag + "_consts"), g.sem(tag + "_products"), g.sem(tag + "_rstd"), g.sem(tag + "_natural")
    sq, tp, tpc, tab = g.sem(tag + "_squares"), g.sem(tag + "_transposed"), g.sem(tag + "_taken"), g.sem(tag + "_table")
    kd, ang = g.sem(tag + "_key_dup"), g.sem(tag + "_angles")
    with nc.Block() as block:
        @block.gpsimd
        def _(pool):
            pool.memset(s.neg, 0.0).then_inc(cst, 1)
            pool.memset(s.dup, 0.0).then_inc(cst, 1)
            pool.wait_ge(cst, 2)
            pool.affine_select(out=s.neg, in_=s.neg, compare_op=ALU.is_ge, fill=NEG, base=0, pattern=[[-1, P]],
                               channel_multiplier=1).then_inc(cst, 1)
            for n, base in enumerate((0, 64, -64)):
                pool.wait_ge(cst, 3 + n)
                pool.affine_select(out=s.dup, in_=s.dup, compare_op=ALU.not_equal, fill=1.0, base=base,
                                   pattern=[[-1, P]], channel_multiplier=1).then_inc(cst, 1)

        @block.tensor
        def _(pe):
            pe.wait_ge(w_in, 128)
            for k in range(KD):
                last = pe.matmul(g.bank[4][:, :], s.wr[:, k, :], g.hT[:, k, :], start=k == 0, stop=k == KD - 1)
            last.then_inc(mm, 1)
            for t in range(T):
                for k in range(KD):
                    last = pe.matmul(g.bank[t][:, 0:QL + KVL], g.hT[:, k, t * P:(t + 1) * P], s.wn[:, k, :],
                                     start=k == 0, stop=k == KD - 1)
                last.then_inc(mm, 1)
            pe.wait_ge(kd, 1)
            pe.wait_ge(cst, 6)
            pe.matmul(g.bank[5][:, :], s.dup, s.n, start=True, stop=True).then_inc(mm, 1)
            pe.wait_ge(nat, 2 * T)
            for n in range(3):
                for t in range(T):
                    src = s.qn[:, t, n::2] if n < 2 else s.ckv[:, t, :]
                    if n == 2 and t == 0:
                        pe.wait_ge(tpc, 1)
                    last = pe.transpose(g.bank[(6, 7, 4)[n]][:, t * P:(t + 1) * P], src, g.ident[:, :])
                last.then_inc(tp, 1)

        @block.scalar
        def _(act):
            for t in range(T):
                act.wait_ge(mm, 2 + t)
                act.activation(g.xn[:, t, 0:QL], g.bank[t][:, 0:QL], ACT.Square, accum_out=g.ss[:, t:t + 1]).then_inc(sq, 1)
                act.activation(g.xn[:, t, QL:QL + KVL], g.bank[t][:, QL:QL + KVL], ACT.Square,
                               accum_out=g.lnss[:, t:t + 1]).then_inc(sq, 1)
            act.wait_ge(sq, 2 * T)
            act.activation(g.rstd[:, :], g.ss[:, :], ACT.Ln, scale=1.0 / QL, bias=g.eps[:, 0:1]).then_inc(rs, 1)
            act.activation(g.ss2[:, :], g.lnss[:, :], ACT.Ln, scale=1.0 / KVL, bias=g.eps[:, 0:1]).then_inc(rs, 1)
            act.wait_ge(rs, 2)
            act.activation(g.ss[:, :], g.rstd[:, :], ACT.Exp, scale=-0.5).then_inc(rs, 1)
            act.activation(g.lnss[:, :], g.ss2[:, :], ACT.Exp, scale=-0.5).then_inc(rs, 1)
            act.wait_ge(ang, 10)
            act.activation(s.cs, s.ang, ACT.Sin).then_inc(tab, 1)

        @block.vector
        def _(dve):
            count = [0]

            def done(ins):
                count[0] += 1
                ins.then_inc(ang, 1)
                dve.wait_ge(ang, count[0])

            c1 = 6.28125
            c2 = float(np.float32(np.round((2 * np.pi - c1) * 2 ** 21) / 2 ** 21))
            c3 = 2 * np.pi - c1 - c2
            magic = 1.5 * 2 ** 23
            dve.wait_ge(w_in, 128)
            done(dve.tensor_copy(s.n, s.pos))
            done(dve.tensor_scalar(s.ang, s.n, s.cols[:, 0:1], None, ALU.mult))
            done(dve.tensor_scalar(s.n, s.ang, 1.0 / (2 * np.pi), s.cols[:, 1:2], ALU.mult, ALU.add))
            done(dve.tensor_scalar(s.n, s.n, magic, None, ALU.add))
            done(dve.tensor_scalar(s.n, s.n, -magic, None, ALU.add))
            for c in (c1, c2, c3):
                done(dve.scalar_tensor_tensor(out=s.ang, in0=s.n, scalar=-c, in1=s.ang, op0=ALU.mult, op1=ALU.add))
            done(dve.tensor_scalar(s.ang, s.ang, s.cols[:, 2:3], None, ALU.add))
            done(dve.tensor_scalar(s.ang, s.ang, 3.1415925, -3.1415925, ALU.min, ALU.max))
            dve.wait_ge(tab, 1)
            dve.wait_ge(mm, 1)
            dve.tensor_tensor(s.n, g.bank[4][:, :], s.cs, ALU.mult).then_inc(kd, 1)
            dve.wait_ge(rs, 4)
            for t in range(T):
                dve.tensor_scalar(s.qn[:, t, :], g.bank[t][:, 0:QL], g.ss[:, t:t + 1], None, ALU.mult).then_inc(nat, 1)
                dve.scalar_tensor_tensor(out=s.ckv[:, t, :], in0=g.bank[t][:, QL:QL + KVL], scalar=g.lnss[:, t:t + 1],
                                         in1=s.gkv, op0=ALU.mult, op1=ALU.mult).then_inc(nat, 1)
            dve.wait_ge(mm, 2 + T)
            dve.tensor_copy(s.kdup, g.bank[5][:, :]).then_inc(tpc, 1)
            for n in range(2):
                dve.wait_ge(tp, n + 1)
                dve.tensor_scalar(s.qaT[:, n, :], g.bank[6 + n][:, :], s.gq[:, n:n + 1], None, ALU.mult).then_inc(tpc, 1)
            dve.wait_ge(tp, 3)
            dve.tensor_copy(s.ckvT, g.bank[4][:, :]).then_inc(tpc, 1)


def load_mla_in(sp, s, a, w_in):
    w = a["mla_w_in"][0].rearrange("(p k) n -> p k n", k=KD)
    sp.dma_start(s.wn, w[:, :, 0:QL + KVL]).then_inc(w_in, 16)
    r = QL + KVL
    half = ROPE // 2
    sp.dma_start(s.wr[:, :, 0:ROPE], w[:, :, r:r + ROPE]).then_inc(w_in, 16)
    sp.dma_start(s.wr[:, :, ROPE:ROPE + half], w[:, :, r + half:r + ROPE]).then_inc(w_in, 16)
    sp.dma_start(s.wr[:, :, ROPE + half:], w[:, :, r:r + half]).then_inc(w_in, 16)
    sp.dma_start(s.pos, a["positions"][0].partition_broadcast(P)).then_inc(w_in, 16)
    sp.dma_start(s.gkv, a["mla_kv_norm_g"][0].partition_broadcast(P)).then_inc(w_in, 16)
    sp.dma_start(s.gq, a["mla_q_norm_g"][0].rearrange("(p k) -> p k", k=2)).then_inc(w_in, 16)
    sp.dma_start(s.cols[:, 0:3], a["rope_cols"]).then_inc(w_in, 16)


def stage_mla_heads(nc, g, s, a, sync_work=None):
    h = s.h
    tag = "mla"
    w_in = [g.sem(f"{tag}_w_in{i}") for i in range(2)]
    S = {n: g.sem(f"{tag}_{n}") for n in
         "wuk wukT qn qnT qr rot qlat qlatT sc max nmax exp rinv pn pt pT_dve pT_act ol olT o oT".split()}
    wq_d = a["mla_w_q_up"][0].rearrange("(p k) n -> p k n", k=2)
    oT = g.big[:, :].rearrange("p (h s) -> p h s", h=HEADS)
    half = ROPE // 2
    with nc.Block() as block:
        @block.sync
        def _(sp):
            def load(it, i):
                hd = 2 * it + i
                c0 = QK * hd
                parts = ((0, NOPE, 0), (NOPE, ROPE, NOPE), (NOPE + ROPE, half, NOPE + half), (NOPE + ROPE + half, half, NOPE))
                for to, n, frm in parts:
                    sp.dma_start(h.wq[i][:, :, to:to + n], wq_d[:, :, bass.ds(c0 + frm, n)]).then_inc(w_in[i], 16)
                sp.dma_start(h.wkv[i], a["mla_w_kv_up"][0][:, bass.ds(256 * hd, 256)]).then_inc(w_in[i], 16)
            load(0, 0)
            load(0, 1)
            with sp.Fori(1, HEADS // 2) as it:
                for i in range(2):
                    sp.wait_ge(S["o"], 2 * it + i - 1)
                    load(it, i)
            if sync_work:
                sync_work(sp)

        def is_first(it, i):
            return isinstance(it, int) and it == 0 and i == 0

        @block.tensor
        def _(pe):
            def queries(it, i):
                n = 2 * it + i
                pe.wait_ge(w_in[i], 80 * (it + 1))
                if not is_first(it, i):
                    pe.wait_ge(S["qlatT"], n)
                pe.transpose(g.bank[4][:, 0:P], h.wkv[i][:, 0:NOPE], g.ident[:, :]).then_inc(S["wuk"], 1)
                for k in range(2):
                    last = pe.matmul(g.bank[5][:, :], h.wq[i][:, k, 0:NOPE], s.qaT[:, k, :], start=k == 0, stop=k == 1)
                last.then_inc(S["qn"], 1)
                if not is_first(it, i):
                    pe.wait_ge(S["rot"], n)
                for k in range(2):
                    last = pe.matmul(g.bank[6][:, :], h.wq[i][:, k, NOPE:], s.qaT[:, k, :], start=k == 0, stop=k == 1)
                last.then_inc(S["qr"], 1)
                pe.wait_ge(S["wukT"], n + 1)
                pe.wait_ge(S["qnT"], n + 1)
                pe.matmul(g.bank[4][:, :], h.wukT, h.qnT, start=True, stop=True).then_inc(S["qlat"], 1)

            def scores(it, i):
                n = 2 * it + i
                if not is_first(it, i):
                    pe.wait_ge(S["pT_dve"], 2 * n)
                    pe.wait_ge(S["pT_act"], n)
                    pe.wait_ge(S["olT"], n)
                pe.wait_ge(S["qlatT"], n + 1)
                pe.wait_ge(S["rot"], n + 1)
                for t in range(T):
                    keys, tok = (t + 1) * P, slice(t * P, (t + 1) * P)
                    pe.matmul(g.bank[t][:, 0:keys], h.qlatT[:, tok], s.ckvT[:, 0:keys], start=True, stop=False)
                    pe.matmul(g.bank[t][:, 0:keys], h.rot[:, tok], s.kdup[:, 0:keys], start=False, stop=False)
                    pe.matmul(g.bank[t][:, tok], g.ident[:, :], s.neg, start=False, stop=True).then_inc(S["sc"], 1)

            def values(it, i):
                n = 2 * it + i
                pe.wait_ge(S["pn"], T * (n + 1))
                for k in range(T):
                    b, at = min(k, 2), 0 if k < 3 else 2 * P
                    for t in range(k, T):
                        last = pe.transpose(g.bank[b][:, at + (t - k) * P:at + (t - k + 1) * P],
                                            h.p[t][:, k * P:(k + 1) * P], g.ident[:, :])
                    if k != 2:
                        last.then_inc(S["pt"], 1)
                for k in range(T):
                    if k < 2:
                        pe.wait_ge(S["pT_dve"], 2 * n + k + 1)
                    else:
                        pe.wait_ge(S["pT_act"], n + 1)
                    last = pe.matmul(g.bank[3][:, k * P:], s.ckv[:, k, :], h.pT[k], start=k == 0, stop=k == T - 1)
                last.then_inc(S["ol"], 1)
                if not is_first(it, i):
                    pe.wait_ge(S["oT"], n)
                pe.wait_ge(S["olT"], n + 1)
                pe.matmul(g.bank[7][:, :], h.wkv[i][:, NOPE:], h.olT, start=True, stop=True).then_inc(S["o"], 1)

            queries(0, 0)
            scores(0, 0)
            queries(0, 1)
            values(0, 0)
            with pe.Fori(1, HEADS // 2) as it:
                scores(it - 1, 1)
                queries(it, 0)
                values(it - 1, 1)
                scores(it, 0)
                queries(it, 1)
                values(it, 0)
            scores(HEADS // 2 - 1, 1)
            values(HEADS // 2 - 1, 1)

        @block.vector
        def _(dve):
            def queries(it, i):
                n = 2 * it + i
                dve.wait_ge(S["wuk"], n + 1)
                if not is_first(it, i):
                    dve.wait_ge(S["qlat"], n)
                dve.tensor_copy(h.wukT, g.bank[4][:, 0:P]).then_inc(S["wukT"], 1)
                dve.wait_ge(S["qn"], n + 1)
                dve.tensor_copy(h.qnT, g.bank[5][:, :]).then_inc(S["qnT"], 1)
                dve.wait_ge(S["qr"], n + 1)
                if not is_first(it, i):
                    dve.wait_ge(S["sc"], T * n)
                dve.tensor_tensor(h.rot, g.bank[6][:, :], s.cs, ALU.mult).then_inc(S["rot"], 1)
                dve.wait_ge(S["qlat"], n + 1)
                dve.tensor_copy(h.qlatT, g.bank[4][:, :]).then_inc(S["qlatT"], 1)

            def maxima(it, i):
                n = 2 * it + i
                if not is_first(it, i):
                    dve.wait_ge(S["exp"], T * n)
                for t in range(T):
                    dve.wait_ge(S["sc"], T * n + t + 1)
                    dve.tensor_reduce(h.mx[:, t:t + 1], g.bank[t][:, 0:(t + 1) * P], AX, ALU.max).then_inc(S["max"], 1)
                    dve.wait_ge(S["max"], T * n + t + 1)
                    dve.tensor_scalar(h.nm[:, t:t + 1], h.mx[:, t:t + 1], -MLA_SCALE, None, ALU.mult).then_inc(S["nmax"], 1)

            def normalize(it, i):
                n = 2 * it + i
                for t in range(T):
                    dve.wait_ge(S["exp"], T * n + t + 1)
                    dve.reciprocal(h.ri[:, t:t + 1], h.rs[:, t:t + 1]).then_inc(S["rinv"], 1)
                    dve.wait_ge(S["rinv"], T * n + t + 1)
                    dve.tensor_scalar(h.p[t], h.p[t], h.ri[:, t:t + 1], None, ALU.mult).then_inc(S["pn"], 1)

            def turned(it, i):
                n = 2 * it + i
                if not is_first(it, i):
                    dve.wait_ge(S["ol"], n)
                for k in range(2):
                    dve.wait_ge(S["pt"], 3 * n + k + 1)
                    dve.tensor_copy(h.pT[k], g.bank[k][:, 0:(T - k) * P]).then_inc(S["pT_dve"], 1)

            queries(0, 0)
            maxima(0, 0)
            queries(0, 1)
            normalize(0, 0)
            turned(0, 0)
            with dve.Fori(1, HEADS // 2) as it:
                maxima(it - 1, 1)
                queries(it, 0)
                normalize(it - 1, 1)
                turned(it - 1, 1)
                maxima(it, 0)
                queries(it, 1)
                normalize(it, 0)
                turned(it, 0)
            maxima(HEADS // 2 - 1, 1)
            normalize(HEADS // 2 - 1, 1)
            turned(HEADS // 2 - 1, 1)

        @block.scalar
        def _(act):
            def head(it, i):
                n = 2 * it + i
                if not is_first(it, i):
                    act.wait_ge(S["pt"], 3 * n)
                for t in range(T):
                    act.wait_ge(S["nmax"], T * n + t + 1)
                    act.activation(h.p[t], g.bank[t][:, 0:(t + 1) * P], ACT.Exp, bias=h.nm[:, t:t + 1], scale=MLA_SCALE,
                                   accum_out=h.rs[:, t:t + 1]).then_inc(S["exp"], 1)
                act.wait_ge(S["pt"], 3 * n + 3)
                for k in (2, 3):
                    at = 0 if k == 2 else 2 * P
                    if not is_first(it, i):
                        act.wait_ge(S["ol"], n)
                    last = act.activation(h.pT[k], g.bank[2][:, at:at + (T - k) * P], ACT.Copy)
                last.then_inc(S["pT_act"], 1)
                act.wait_ge(S["ol"], n + 1)
                if not is_first(it, i):
                    act.wait_ge(S["o"], n)
                act.activation(h.olT, g.bank[3][:, :], ACT.Copy).then_inc(S["olT"], 1)
                act.wait_ge(S["o"], n + 1)
                act.activation(oT[:, bass.ds(n, 1), :], g.bank[7][:, :].unsqueeze(1), ACT.Copy).then_inc(S["oT"], 1)
            head(0, 0)
            head(0, 1)
            with act.Fori(1, HEADS // 2) as it:
                head(it, 0)
                head(it, 1)


def stage_out(nc, g, tag, w_dram, sync_work=None):
    NS = 12
    slots = g.w[:, 2:4, :].rearrange("p n (s d) -> p (n s) d", d=D)
    w_in = [g.sem(f"{tag}_w_in{i}") for i in range(NS)]
    used, mm, add = g.sem(tag + "_w_used"), g.sem(tag + "_products"), g.sem(tag + "_added")
    oT = g.big[:, :].rearrange("p (h s) -> p h s", h=HEADS)
    with nc.Block() as block:
        @block.sync
        def _(sp):
            for k in range(HEADS):
                if k >= NS:
                    sp.wait_ge(used, k - NS + 1)
                sp.dma_start(slots[:, k % NS, :], w_dram[k * P:(k + 1) * P, :]).then_inc(w_in[k % NS], 16)
            if sync_work:
                sync_work(sp)

        @block.tensor
        def _(pe):
            for k in range(HEADS):
                pe.wait_ge(w_in[k % NS], 16 * (k // NS + 1))
                for t in range(T):
                    for n in range(2):
                        last = pe.matmul(g.bank[2 * t + n][:, :], oT[:, k, t * P:(t + 1) * P],
                                         slots[:, k % NS, 512 * n:512 * (n + 1)], start=k == 0, stop=k == HEADS - 1)
                        if k == HEADS - 1:
                            last.then_inc(mm, 1)
                if k < HEADS - 1:
                    last.then_inc(used, 1)

        @block.vector
        def _(dve):
            for b in range(2 * T):
                dve.wait_ge(mm, b + 1)
                xv = g.x[:, b // 2, 512 * (b % 2):512 * (b % 2) + 512]
                dve.tensor_tensor(xv, g.bank[b][:, :], xv, ALU.add).then_inc(add, 1)



K_HEADS, V_HEADS = 8, 16
CONV = 4
QKW, VW = K_HEADS * P, V_HEADS * P
LEVELS = 7
BETA, NBETA, G, GLOG, BEG = range(5)
(PQ, PK, PV0, PV1, PZ0, PZ1) = range(6)


def gdn_memory(nc, ctx, g):
    s = Memory()
    parts = [workspace(g, 0, 1), workspace(g, 2, 2)]
    left = [GU + DN, 2 * (GU + DN)]

    def tile():
        i = 0 if left[0] >= SEQ else 1
        left[i] -= SEQ
        return parts[i](T, P)
    s.c = [tile() for _ in range(4)]
    s.zn = [tile() for _ in range(2)]
    s.zw = [tile() for _ in range(2)]
    s.qT, s.kT, s.kn = tile(), tile(), tile()
    s.vb, s.kbg, s.kout, s.E, s.eG, s.QKT, s.qin, s.A, s.TT, s.W, s.vn = (
        [tile() for _ in range(2)] for _ in range(11))
    s.B, s.Tm = s.E, s.eG
    w = workspace(g, 1, 1)
    s.wq, s.wk, s.wv, s.wz = w(KD, P), w(KD, P), w(KD, 2 * P), w(KD, 2 * P)

    def sb(name, *shape):
        return ctx.enter_context(nc.sbuf_tensor(name, [P, *shape], F32))
    s.tab = sb("gdn_tab", V_HEADS, 5, T)
    s.st = sb("gdn_tab_now", 2, 5, T)
    s.cw = sb("gdn_conv_w", 32, CONV)
    s.cws = sb("gdn_conv_w_now", 4, CONV)
    s.S = [sb(f"gdn_state{i}", P) for i in range(2)]
    s.ge = [sb(f"gdn_end_decay{i}", T) for i in range(2)]
    s.gcol = sb("gdn_gain", 1)
    s.lm = sb("level_masks", LEVELS, P)
    f = g.big[:, 0:4096]
    s.wba, s.cwr = f[:, 0:256].rearrange("p (k n) -> p k n", k=KD), f[:, 256:384]
    s.dt, s.al = f[:, 384:400], f[:, 400:416]
    s.xa, s.ab, s.sp, s.gl = (f[:, 512 + 64 * i:576 + 64 * i].rearrange("p (t h) -> p t h", t=T) for i in range(4))
    s.bt, s.Gc, s.eGc = (f[:, 768 + 64 * i:832 + 64 * i].rearrange("p (t h) -> p t h", t=T) for i in range(3))
    return s


def load_gates(sp, s, a, w_in):
    w = a["gdn_w_in"][0].rearrange("(p k) n -> p k n", k=KD)
    sp.dma_start(s.wba, w[:, :, 2 * QKW + 2 * VW:]).then_inc(w_in, 16)
    sp.dma_start(s.cwr, a["gdn_conv_w"][0].rearrange("c (n p) -> (c n) p", p=P)).then_inc(w_in, 16)
    sp.dma_start(s.dt, a["gdn_dt_bias"][0].partition_broadcast(P)).then_inc(w_in, 16)
    sp.dma_start(s.al, a["gdn_a_log"][0].partition_broadcast(P)).then_inc(w_in, 16)
    sp.dma_start(s.gcol[:, :], a["gdn_norm_g"][0].rearrange("(p o) -> p o", o=1)).then_inc(w_in, 16)


def stage_gates(nc, g, s, a, w_in):
    tag = "gates"
    proj, act_s, dve_s, run = g.sem(tag + "_products"), g.sem(tag + "_act"), g.sem(tag + "_dve"), g.sem(tag + "_sums")
    lm = g.sem(tag + "_masks")
    with nc.Block() as block:
        @block.sync
        def _(sp):
            load_gates(sp, s, a, w_in)

        @block.gpsimd
        def _(pool):
            pool.memset(s.lm[:, :, :], 0.0).then_inc(lm, 1)
            n = 1
            for lv in range(LEVELS):
                b = 1 << lv
                low = s.lm[:, lv, :].rearrange("p (n h c) -> p n h c", h=2, c=b)[:, :, 0, :]
                pool.wait_ge(lm, n)
                pool.memset(low, 1.0).then_inc(lm, 1)
                pool.wait_ge(lm, n + 1)
                pool.affine_select(out=low, in_=low, compare_op=ALU.is_ge, fill=0.0, base=-b,
                                   pattern=[[-2 * b, P // (2 * b)], [0, b]], channel_multiplier=1).then_inc(lm, 1)
                pool.wait_ge(lm, n + 2)
                pool.affine_select(out=low, in_=low, compare_op=ALU.is_ge, fill=0.0, base=2 * b - 1,
                                   pattern=[[2 * b, P // (2 * b)], [0, b]], channel_multiplier=-1).then_inc(lm, 1)
                n += 3

        @block.tensor
        def _(pe):
            pe.wait_ge(w_in, 80)
            for t in range(T):
                for k in range(KD):
                    last = pe.matmul(g.bank[0][:, 32 * t:32 * t + 32], g.hT[:, k, t * P:(t + 1) * P], s.wba[:, k, :],
                                     start=k == 0, stop=k == KD - 1)
            last.then_inc(proj, 1)
            pe.transpose(g.bank[1][:, 0:P], s.cwr, g.ident[:, :]).then_inc(proj, 1)
            pe.wait_ge(dve_s, 4)
            pe.matmul(g.bank[2][:, 0:T * V_HEADS], g.tri[:, :], s.gl.rearrange("p t h -> p (t h)"),
                      start=True, stop=True).then_inc(proj, 1)

        @block.scalar
        def _(act):
            ba = g.bank[0][:, 0:128].rearrange("p (t c h) -> p t c h", t=T, c=2)
            act.wait_ge(proj, 1)
            act.activation(s.bt, ba[:, :, 0, :], ACT.Sigmoid).then_inc(act_s, 1)
            act.activation(s.al, s.al, ACT.Exp).then_inc(act_s, 1)
            act.wait_ge(dve_s, 1)
            act.activation(s.ab, s.xa, ACT.Abs).then_inc(act_s, 1)
            act.wait_ge(act_s, 3)
            act.activation(s.sp, s.ab, ACT.Exp, scale=-1.0).then_inc(act_s, 1)
            act.wait_ge(act_s, 4)
            act.activation(s.sp, s.sp, ACT.Ln, bias=g.ones[:, 0:1]).then_inc(act_s, 1)
            act.wait_ge(dve_s, 6)
            act.activation(s.eGc, s.Gc, ACT.Exp).then_inc(act_s, 1)

        @block.vector
        def _(dve):
            count = [0]

            def done(ins):
                count[0] += 1
                ins.then_inc(dve_s, 1)
                dve.wait_ge(dve_s, count[0])

            def bc(v):
                return v.unsqueeze(1).to_broadcast([P, T, V_HEADS])
            ba = g.bank[0][:, 0:128].rearrange("p (t c h) -> p t c h", t=T, c=2)
            dve.wait_ge(w_in, 80)
            dve.wait_ge(act_s, 1)
            done(dve.tensor_tensor(s.xa, ba[:, :, 1, :], bc(s.dt), ALU.add))
            dve.wait_ge(act_s, 5)
            done(dve.scalar_tensor_tensor(out=s.gl, in0=s.xa, scalar=0.0, in1=s.sp, op0=ALU.max, op1=ALU.add))
            done(dve.tensor_tensor(s.gl, s.gl, bc(s.al), ALU.mult))
            done(dve.tensor_scalar(s.gl, s.gl, -1.0, None, ALU.mult))
            dve.wait_ge(proj, 2)
            done(dve.tensor_copy(s.cw[:, :, :], g.bank[1][:, 0:P].rearrange("p (c n) -> p n c", c=CONV)))
            dve.wait_ge(proj, 3)
            done(dve.tensor_copy(s.Gc, g.bank[2][:, 0:T * V_HEADS].rearrange("p (t h) -> p t h", t=T)))
            dve.wait_ge(act_s, 6)

            def put(n, v):
                return dve.tensor_copy(s.tab[:, :, n, :], v.rearrange("p t h -> p h t"))
            done(put(BETA, s.bt))
            done(put(G, s.Gc))
            done(put(GLOG, s.gl))
            done(dve.tensor_scalar(s.tab[:, :, NBETA, :], s.tab[:, :, BETA, :], -1.0, None, ALU.mult))
            done(dve.tensor_tensor(s.tab[:, :, BEG, :], s.bt.rearrange("p t h -> p h t"),
                                   s.eGc.rearrange("p t h -> p h t"), ALU.mult))


def stage_delta(nc, g, s, a):
    S = {n: g.sem("gd_" + n) for n in
         ("squares norms_sum norms qk v_turned tables decay_rhs decay_bc v_beta decay_diff exp_diff exp_G k_turned kk kq "
          "k_nat k_beta k_out A_raw A QKT_raw QKT q_in end_decay z_now masked T0 TT first_product W YT Y T "
          "w_product w_neg v_product v_new o state_product state o_squares o_sums o_rstd o_normed o_gated "
          "projected conv_step silu z_next conv_w").split()}
    w_in = [g.sem(f"gd_w_in{i}") for i in range(4)]
    oT = g.big[:, :].rearrange("p (h t i) -> p h t i", h=V_HEADS, t=T)
    w_d = a["gdn_w_in"][0].rearrange("(p k) n -> p k n", k=KD)
    bank = [b[:, :].rearrange("p (t i) -> p t i", t=T) for b in g.bank]
    LAST = K_HEADS - 1

    def wait(eng, name, per, it, n):
        eng.wait_ge(S[name], per * it + n)

    def first(it):
        return isinstance(it, int) and it == 0

    def cols(v):
        return v.unsqueeze(2).to_broadcast([P, T, P])

    def rows(v):
        return v.unsqueeze(1).to_broadcast([P, T, P])

    def weights(tile):
        return (s.wq[:, :, :], s.wk[:, :, :], s.wv[:, :, 0:P], s.wv[:, :, P:], s.wz[:, :, 0:P], s.wz[:, :, P:])[tile]

    with nc.Block() as block:
        @block.sync
        def _(sp):
            def load(part, kh):
                dst, base, n = ((s.wq, 0, P), (s.wk, QKW, P), (s.wv, 2 * QKW, 2 * P), (s.wz, 2 * QKW + VW, 2 * P))[part]
                sp.dma_start(dst, w_d[:, :, bass.ds(base + n * kh, n)]).then_inc(w_in[part], 16)
            for part in range(4):
                load(part, 0)
            with sp.Fori(1, K_HEADS) as kh:
                for part, used in enumerate((1, 2, 4, 6)):
                    sp.wait_ge(S["projected"], 6 * (kh - 1) + used)
                    load(part, kh)

        @block.tensor
        def _(pe):
            def project(n, tile, ks):
                if 0 in ks:
                    pe.wait_ge(w_in[(0, 1, 2, 2, 3, 3)[tile]], 16 * (n + 1))
                    if tile >= 2:
                        wait(pe, "conv_step", 16, n, 4 * (tile - 1))
                    elif not first(n):
                        wait(pe, "z_next", 2, n - 1, tile + 1)
                for k in ks:
                    last = pe.matmul(g.bank[tile % 2][:, :], weights(tile)[:, k, :], g.hT[:, k, :],
                                     start=k == 0, stop=k == KD - 1)
                if KD - 1 in ks:
                    last.then_inc(S["projected"], 1)

            def each(out, lhs, rhs, transposed=False):
                for t in range(T):
                    if transposed:
                        last = pe.transpose(out[:, t, :], lhs[:, t, :], g.ident[:, :])
                    else:
                        last = pe.matmul(out[:, t, :], lhs[:, t, :], rhs[:, t, :], start=True, stop=True)
                return last

            def flat(v):
                return v.rearrange("p t i -> p (t i)")

            def head_pair(it, more):
                n = it + 1
                for i in range(2):
                    wait(pe, "squares", 2, it, i + 1)
                    if not first(it):
                        wait(pe, "o_normed", 2, it - 1, 2)
                    pe.matmul(g.bank[4 + i][:, :], g.ones[:, :], flat(s.E[i]), start=True, stop=True)\
                        .then_inc(S["norms_sum"], 1)
                for i in range(2):
                    wait(pe, "silu", 4, it, 3 + i)
                    if not first(it):
                        wait(pe, "o_rstd", 4, it - 1, 4)
                    each(bank[2 + i], s.c[2 + i], None, True).then_inc(S["v_turned"], 1)
                for i in range(2):
                    wait(pe, "decay_rhs", 2, it, i + 1)
                    pe.matmul(g.bank[6 + i][:, :], g.ones[:, :], flat(s.W[i]), start=True, stop=True)\
                        .then_inc(S["decay_bc"], 1)
                wait(pe, "norms", 4, it, 4)
                wait(pe, "qk", 2, it, 2)
                each(bank[4], s.kT, None, True).then_inc(S["k_turned"], 1)
                each(bank[5], s.kT, s.kT).then_inc(S["kk"], 1)
                wait(pe, "v_beta", 2, it, 1)
                each(bank[2], s.kT, s.qT).then_inc(S["kq"], 1)
                for i in range(2):
                    wait(pe, "masked", 14, it, i + 1)
                    if i == 0:
                        wait(pe, "QKT_raw", 2, it, 2)
                    else:
                        wait(pe, "v_beta", 2, it, 2)
                    each(bank[2 + i], s.B[i], None, True).then_inc(S["first_product"], 1)
                for lv in range(1, LEVELS):
                    for i in range(2):
                        wait(pe, "masked", 14, it, 2 * lv + i + 1)
                        wait(pe, "TT", 14, it, 2 * (lv - 1) + i + 1)
                        if lv > 1:
                            wait(pe, "W", 12, it, 2 * (lv - 2) + i + 1)
                        each(bank[2 + i], s.B[i], s.TT[i]).then_inc(S["first_product"], 1)
                    if more:
                        project(n, lv - 1, (0, 1, 2))
                    for i in range(2):
                        wait(pe, "W", 12, it, 2 * (lv - 1) + i + 1)
                        if lv == 1:
                            wait(pe, "T0", 2, it, i + 1)
                            wait(pe, "exp_G", 2, it, 2)
                            wait(pe, "k_nat", 1, it, 1)
                            wait(pe, "A_raw", 2, it, 2)
                        else:
                            wait(pe, "T", 10, it, 2 * (lv - 2) + i + 1)
                        each(bank[5 + 2 * i], s.Tm[i], s.W[i]).then_inc(S["YT"], 1)
                        if lv < LEVELS - 1:
                            each(bank[4 + 2 * i], s.W[i], s.Tm[i]).then_inc(S["Y"], 1)
                        if more:
                            project(n, lv - 1, ((3, 4), (5, 6, 7))[i])
                for i in range(2):
                    wait(pe, "TT", 14, it, 2 * (LEVELS - 1) + i + 1)
                    wait(pe, "k_beta", 2, it, i + 1)
                    each(bank[2 + i], s.kbg[i], s.TT[i]).then_inc(S["w_product"], 1)
                for c in range(T):
                    for i in range(2):
                        if c == 0:
                            wait(pe, "w_neg", 2, it, i + 1)
                        else:
                            wait(pe, "v_new", 8, it, 2 * (c - 1) + i + 1)
                        last = pe.matmul(bank[2 + i][:, c, :], s.TT[i][:, c, :], s.vb[i][:, c, :], start=True, stop=c == 0)
                        if c > 0:
                            wait(pe, "state", 6, it, 2 * (c - 1) + i + 1)
                            last = pe.matmul(bank[2 + i][:, c, :], s.W[i][:, c, :], s.S[i][:, :], start=False, stop=True)
                        last.then_inc(S["v_product"], 1)
                    for i in range(2):
                        if c == 0:
                            wait(pe, "q_in", 2, it, i + 1)
                            wait(pe, "QKT", 2, it, i + 1)
                            wait(pe, "k_out", 2, it, i + 1)
                            wait(pe, "T", 10, it, 8 + i + 1)
                        if c > 0:
                            pe.matmul(bank[4 + 2 * i][:, c, :], s.S[i][:, :], s.qin[i][:, c, :], start=True, stop=False)
                        wait(pe, "v_new", 8, it, 2 * c + i + 1)
                        pe.matmul(bank[4 + 2 * i][:, c, :], s.vn[i][:, c, :], s.QKT[i][:, c, :], start=c == 0, stop=True)\
                            .then_inc(S["o"], 1)
                        if c < T - 1:
                            pe.matmul(bank[5 + 2 * i][:, 0, :], s.kout[i][:, c, :], s.vn[i][:, c, :], start=True, stop=True)\
                                .then_inc(S["state_product"], 1)
                for i in range(2):
                    wait(pe, "o_squares", 2, it, i + 1)
                    wait(pe, "v_new", 8, it, 7 + i)
                    pe.matmul(g.bank[2 + i][:, :], g.ones[:, :], flat(s.W[i]), start=True, stop=True)\
                        .then_inc(S["o_sums"], 1)

            for tile in range(6):
                project(0, tile, range(KD))
            head_pair(0, True)
            with pe.Fori(1, LAST) as it:
                head_pair(it, True)
            head_pair(LAST, False)

        @block.vector
        def _(dve):
            def conv(n, tile):
                c = s.c[tile].rearrange("p t i -> p (t i)")
                wait(dve, "projected", 6, n, tile + 1)
                if tile == 0:
                    wait(dve, "conv_w", 3, n, 3)
                if not first(n):
                    if tile < 2:
                        wait(dve, "squares", 2, n - 1, tile + 1)
                        wait(dve, "qk", 2, n - 1, tile + 1)
                    else:
                        wait(dve, "v_turned", 2, n - 1, tile - 1)
                src, cw = g.bank[tile % 2], s.cws[:, tile, :]
                dve.tensor_scalar(c, src[:, :], cw[:, CONV - 1:CONV], None, ALU.mult).then_inc(S["conv_step"], 1)
                for lag in range(1, CONV):
                    wait(dve, "conv_step", 16, n, 4 * tile + lag)
                    dve.scalar_tensor_tensor(out=c[:, lag:], in0=src[:, 0:SEQ - lag], scalar=cw[:, CONV - 1 - lag:CONV - lag],
                                             in1=c[:, lag:], op0=ALU.mult, op1=ALU.add).then_inc(S["conv_step"], 1)

            def conv_weights(n):
                if not first(n):
                    wait(dve, "conv_step", 16, n - 1, 16)
                dve.tensor_copy(s.cws[:, 0:1, :], s.cw[:, bass.ds(n, 1), :]).then_inc(S["conv_w"], 1)
                dve.tensor_copy(s.cws[:, 1:2, :], s.cw[:, bass.ds(K_HEADS + n, 1), :]).then_inc(S["conv_w"], 1)
                dve.tensor_copy(s.cws[:, 2:4, :], s.cw[:, bass.ds(2 * K_HEADS + 2 * n, 2), :]).then_inc(S["conv_w"], 1)

            def head_pair(it, more):
                n = it + 1
                if not first(it):
                    wait(dve, "A", 2, it - 1, 2)
                    wait(dve, "k_beta", 2, it - 1, 2)
                    wait(dve, "decay_rhs", 2, it - 1, 2)
                dve.tensor_copy(s.st[:, :, :, :], s.tab[:, bass.ds(2 * it, 2), :, :]).then_inc(S["tables"], 1)
                if more:
                    conv_weights(n)
                wait(dve, "tables", 1, it, 1)
                for i in range(2):
                    wait(dve, "v_turned", 2, it, i + 1)
                    dve.tensor_tensor(s.vb[i], bank[2 + i], cols(s.st[:, i, BETA, :]), ALU.mult).then_inc(S["v_beta"], 1)
                wait(dve, "norms", 4, it, 4)
                dve.scalar_tensor_tensor(out=s.qT.rearrange("p t i -> p (t i)"), in0=s.c[PQ].rearrange("p t i -> p (t i)"),
                                         scalar=float(P) ** -0.5, in1=s.A[0].rearrange("p t i -> p (t i)"),
                                         op0=ALU.mult, op1=ALU.mult).then_inc(S["qk"], 1)
                dve.tensor_tensor(s.kT, s.c[PK], s.A[1], ALU.mult).then_inc(S["qk"], 1)
                for i in range(2):
                    wait(dve, "decay_bc", 2, it, i + 1)
                    wait(dve, "norms_sum", 2, it, i + 1)
                    dve.tensor_tensor(s.E[i], bank[6 + i], cols(s.st[:, i, G, :]), ALU.subtract)\
                        .then_inc(S["decay_diff"], 1)
                wait(dve, "k_turned", 1, it, 1)
                if not first(it):
                    wait(dve, "k_out", 2, it - 1, 2)
                dve.tensor_copy(s.kn, bank[4]).then_inc(S["k_nat"], 1)
                for i in range(2):
                    wait(dve, "kk", 1, it, 1)
                    wait(dve, "exp_diff", 4, it, 2 * i + 2)
                    wait(dve, "qk", 2, it, 2)
                    dve.tensor_tensor(s.A[i], bank[5], s.E[i], ALU.mult).then_inc(S["A_raw"], 1)
                for i in range(2):
                    wait(dve, "kq", 1, it, 1)
                    dve.tensor_tensor(s.QKT[i], bank[2], s.E[i], ALU.mult).then_inc(S["QKT_raw"], 1)
                for i in range(2):
                    wait(dve, "first_product", 14, it, i + 1)
                    dve.tensor_tensor(s.TT[i], bank[2 + i], rows(g.ident[:, :]), ALU.add).then_inc(S["TT"], 1)
                for lv in range(1, LEVELS):
                    for i in range(2):
                        wait(dve, "YT", 12, it, 2 * (lv - 1) + i + 1)
                        wait(dve, "TT", 14, it, 2 * (lv - 1) + i + 1)
                        dve.tensor_tensor(s.TT[i], bank[5 + 2 * i], s.TT[i], ALU.add).then_inc(S["TT"], 1)
                        if lv < LEVELS - 1:
                            wait(dve, "Y", 10, it, 2 * (lv - 1) + i + 1)
                            if lv > 1:
                                wait(dve, "T", 10, it, 2 * (lv - 2) + i + 1)
                            dve.tensor_tensor(s.Tm[i], bank[4 + 2 * i], s.Tm[i], ALU.add).then_inc(S["T"], 1)
                    if more and 2 <= lv < 6:
                        conv(n, lv - 2)
                for c in range(T - 1):
                    for i in range(2):
                        wait(dve, "state_product", 6, it, 2 * c + i + 1)
                        if c == 0:
                            dve.tensor_copy(s.S[i][:, :], bank[5 + 2 * i][:, 0, :]).then_inc(S["state"], 1)
                        else:
                            wait(dve, "state", 6, it, 2 * (c - 1) + i + 1)
                            wait(dve, "end_decay", 2, it, i + 1)
                            dve.scalar_tensor_tensor(out=s.S[i][:, :], in0=s.S[i][:, :], scalar=s.ge[i][:, c:c + 1],
                                                     in1=bank[5 + 2 * i][:, 0, :], op0=ALU.mult, op1=ALU.add)\
                                .then_inc(S["state"], 1)
                for i in range(2):
                    wait(dve, "o_rstd", 4, it, 2 * i + 2)
                    dve.scalar_tensor_tensor(out=s.vn[i].rearrange("p t i -> p (t i)"), in0=g.bank[4 + 2 * i][:, :],
                                             scalar=s.gcol[:, 0:1], in1=s.A[i].rearrange("p t i -> p (t i)"),
                                             op0=ALU.mult, op1=ALU.mult).then_inc(S["o_normed"], 1)
                    wait(dve, "o_normed", 2, it, i + 1)
                    wait(dve, "z_now", 2, it, i + 1)
                    dve.tensor_tensor(oT[:, bass.ds(2 * it + i, 1)], s.vn[i].unsqueeze(1), s.zw[i].unsqueeze(1), ALU.mult)\
                        .then_inc(S["o_gated"], 1)

            conv_weights(0)
            for tile in range(4):
                conv(0, tile)
            head_pair(0, True)
            with dve.Fori(1, LAST) as it:
                head_pair(it, True)
            head_pair(LAST, False)

        @block.scalar
        def _(act):
            def silu_conv(n, tile):
                wait(act, "conv_step", 16, n, 4 * tile + 4)
                act.activation(s.c[tile], s.c[tile], ACT.Silu).then_inc(S["silu"], 1)

            def silu_z(n, i):
                wait(act, "projected", 6, n, 5 + i)
                if not first(n):
                    wait(act, "z_now", 2, n - 1, i + 1)
                act.activation(s.zn[i], bank[i], ACT.Silu).then_inc(S["z_next"], 1)

            def head_pair(it, more):
                n = it + 1
                for i in range(2):
                    wait(act, "silu", 4, it, i + 1)
                    act.activation(s.E[i], s.c[i], ACT.Square).then_inc(S["squares"], 1)
                for i in range(2):
                    wait(act, "norms_sum", 2, it, i + 1)
                    act.activation(s.A[i], bank[4 + i], ACT.Ln, bias=g.eps[:, 0:1]).then_inc(S["norms"], 1)
                    wait(act, "norms", 4, it, 2 * i + 1)
                    act.activation(s.A[i], s.A[i], ACT.Exp, scale=-0.5).then_inc(S["norms"], 1)
                for i in range(2):
                    wait(act, "decay_diff", 2, it, i + 1)
                    act.activation(s.E[i], s.E[i], ACT.Abs).then_inc(S["exp_diff"], 1)
                    wait(act, "exp_diff", 4, it, 2 * i + 1)
                    act.activation(s.E[i], s.E[i], ACT.Exp, scale=-1.0).then_inc(S["exp_diff"], 1)
                    act.activation(s.eG[i], bank[6 + i], ACT.Exp).then_inc(S["exp_G"], 1)
                for lv in range(1, LEVELS):
                    for i in range(2):
                        wait(act, "first_product", 14, it, 2 * lv + i + 1)
                        act.activation(s.W[i], bank[2 + i], ACT.Copy).then_inc(S["W"], 1)
                    if more and 3 <= lv:
                        silu_conv(n, lv - 3)
                    if more and lv == 6:
                        silu_z(n, 0)
                if more:
                    silu_z(n, 1)
                for i in range(2):
                    wait(act, "w_product", 2, it, i + 1)
                    act.activation(s.W[i], bank[2 + i], ACT.Copy, scale=-1.0).then_inc(S["w_neg"], 1)
                for c in range(T):
                    for i in range(2):
                        wait(act, "v_product", 8, it, 2 * c + i + 1)
                        if c == 0 and not first(it):
                            wait(act, "o_gated", 2, it - 1, i + 1)
                        act.activation(s.vn[i][:, c, :], bank[2 + i][:, c, :], ACT.Copy).then_inc(S["v_new"], 1)
                for i in range(2):
                    wait(act, "o", 8, it, 7 + i)
                    act.activation(s.W[i], bank[4 + 2 * i], ACT.Square).then_inc(S["o_squares"], 1)
                for i in range(2):
                    wait(act, "o_sums", 2, it, i + 1)
                    act.activation(s.A[i], bank[2 + i], ACT.Ln, scale=1.0 / P, bias=g.eps[:, 0:1]).then_inc(S["o_rstd"], 1)
                    wait(act, "o_rstd", 4, it, 2 * i + 1)
                    act.activation(s.A[i], s.A[i], ACT.Exp, scale=-0.5).then_inc(S["o_rstd"], 1)

            for tile in range(4):
                silu_conv(0, tile)
            for i in range(2):
                silu_z(0, i)
            head_pair(0, True)
            with act.Fori(1, LAST) as it:
                head_pair(it, True)
            head_pair(LAST, False)

        @block.gpsimd
        def _(pool):
            def head_pair(it):
                for i in range(2):
                    wait(pool, "tables", 1, it, 1)
                    if not first(it):
                        wait(pool, "o_sums", 2, it - 1, i + 1)
                    pool.tensor_tensor(s.W[i], rows(g.tri[:, :]), cols(s.st[:, i, GLOG, :]), ALU.mult)\
                        .then_inc(S["decay_rhs"], 1)
                for i in range(2):
                    wait(pool, "z_next", 2, it, i + 1)
                    if not first(it):
                        wait(pool, "o_gated", 2, it - 1, i + 1)
                    pool.tensor_tensor(s.zw[i], s.zn[i], rows(g.ones[:, :]), ALU.mult).then_inc(S["z_now"], 1)
                for i in range(2):
                    wait(pool, "A_raw", 2, it, i + 1)
                    pool.tensor_tensor(s.A[i], s.A[i], cols(s.st[:, i, NBETA, :]), ALU.mult).then_inc(S["A"], 1)
                for i in range(2):
                    if not first(it):
                        wait(pool, "w_product", 2, it - 1, i + 1)
                    wait(pool, "k_nat", 1, it, 1)
                    pool.tensor_tensor(s.kout[i], s.kn, s.E[i][:, :, P - 1:P].to_broadcast([P, T, P]), ALU.mult)\
                        .then_inc(S["k_out"], 1)
                    wait(pool, "exp_G", 2, it, i + 1)
                    wait(pool, "qk", 2, it, 1)
                    pool.tensor_tensor(s.qin[i], s.qT, s.eG[i], ALU.mult).then_inc(S["q_in"], 1)
                    pool.tensor_copy(s.ge[i][:, :], s.eG[i][:, :, P - 1]).then_inc(S["end_decay"], 1)
                for i in range(2):
                    wait(pool, "QKT_raw", 2, it, i + 1)
                    wait(pool, "A", 2, it, i + 1)
                    wait(pool, "k_out", 2, it, i + 1)
                    pool.tensor_tensor(s.B[i], s.A[i], rows(s.lm[:, 0, :]), ALU.mult).then_inc(S["masked"], 1)
                for i in range(2):
                    wait(pool, "masked", 14, it, i + 1)
                    wait(pool, "q_in", 2, it, i + 1)
                    wait(pool, "end_decay", 2, it, i + 1)
                    pool.tensor_tensor(s.Tm[i], s.B[i], rows(g.ident[:, :]), ALU.add).then_inc(S["T0"], 1)
                for lv in range(1, LEVELS):
                    for i in range(2):
                        wait(pool, "first_product", 14, it, 2 * (lv - 1) + i + 1)
                        if lv == 1:
                            wait(pool, "T0", 2, it, i + 1)
                        pool.tensor_tensor(s.B[i], s.A[i], rows(s.lm[:, lv, :]), ALU.mult).then_inc(S["masked"], 1)
                        if lv == 1:
                            pool.tensor_tensor(s.QKT[i], s.QKT[i], rows(g.tri[:, :]), ALU.mult).then_inc(S["QKT"], 1)
                        if lv == 2:
                            pool.tensor_tensor(s.kbg[i], s.kn, cols(s.st[:, i, BEG, :]), ALU.mult).then_inc(S["k_beta"], 1)

            head_pair(0)
            with pool.Fori(1, LAST) as it:
                head_pair(it)
            head_pair(LAST)


def build(nc, a, out, parts):
    with ExitStack() as ctx:
        g = make_shared(nc, ctx)
        m = moe_memory(nc, ctx, g)
        gd, ml = gdn_memory(nc, ctx, g), mla_memory(nc, g)
        m.wr_in = [g.sem(f"router_in{l}") for l in range(2)]
        ple_w = [g.sem(f"ple_w_in{l}") for l in range(2)]
        for layer in range(2):
            def load_router(sp, layer=layer):
                for dst, src in ((m.wr[:, :, 0:GROUPS], a["moe_router_group"]), (m.wr[:, :, GROUPS:], a["moe_router_expert"])):
                    sp.dma_start(dst, src[layer].rearrange("(p k) n -> p k n", k=KD)).then_inc(m.wr_in[layer], 16)
                for i in range(2):
                    load_expert(sp, m, a, layer, i, i, m.loaded[layer][i])

            def load_more(sp, layer=layer):
                if ("gdn", "mla")[layer] not in parts:
                    load_router(sp)
                for i in range(2, NBUF):
                    load_expert(sp, m, a, layer, i, i, m.loaded[layer][i])

            if layer == 0:
                with semaphores_of(nc, g):
                    stage_setup(nc, g, a)
                    stage_zero(nc, g, m)
            if ("gdn", "mla")[layer] in parts:
                with semaphores_of(nc, g):
                    w_in = g.sem(f"mixer_w_in{layer}")
                    if layer == 0:
                        stage_norm(nc, g, "gdn_norm", 0)
                        stage_gates(nc, g, gd, a, w_in)
                        stage_delta(nc, g, gd, a)
                        stage_out(nc, g, "gdn_out", a["gdn_w_out"][0], load_router if "moe" in parts else None)
                    else:
                        stage_norm(nc, g, "mla_norm", 1, lambda sp: load_mla_in(sp, ml, a, w_in))
                        stage_mla_in(nc, g, ml, a, w_in)
                        stage_mla_heads(nc, g, ml, a)
                        stage_out(nc, g, "mla_out", a["mla_w_out"][0], load_router if "moe" in parts else None)
            if "moe" not in parts:
                continue
            with semaphores_of(nc, g):
                stage_norm(nc, g, f"ffn_norm{layer}", 2 + layer, load_more)
                stage_route(nc, g, m, a, layer)
                stage_experts(nc, g, m, a, layer)
                stage_overflow(nc, g, m, a, layer)
                stage_combine(nc, g, m, layer, lambda sp, layer=layer: ple_load(sp, a, g, layer, ple_w[layer]))
                stage_norm(nc, g, f"ple_norm{layer}", 4 + layer)
                stage_ple(nc, g, a, layer, ple_w[layer])
        with semaphores_of(nc, g):
            stage_final(nc, g, a, out)


_INS = ['x', 'p', 'positions', 'norm_mix_g', 'norm_ffn_g', 'norm_ple_g', 'gdn_w_in', 'gdn_conv_w', 'gdn_a_log',
        'gdn_dt_bias', 'gdn_norm_g', 'gdn_w_out', 'mla_w_in', 'mla_q_norm_g', 'mla_kv_norm_g', 'mla_w_q_up',
        'mla_w_kv_up', 'mla_w_out', 'moe_router_group', 'moe_router_expert', 'moe_w_gate_up', 'moe_w_down',
        'ple_w_proj', 'ple_w_gate', 'final_norm_g']
PARTS = ["gdn", "mla", "moe"]


def kernel(**inputs):
    import concourse.bacc as bacc
    from concourse.bass_utils import run_bass_kernel_spmd
    nc = bacc.Bacc("TRN2", target_bir_lowering=False, num_devices=1)
    arrays, a = {}, {}
    given = {name: np.ascontiguousarray(inputs[name]) for name in _INS}
    given["rope_cols"] = rope_columns()
    for name, v in given.items():
        arrays["in_" + name] = v
        ap = nc.dram_tensor("in_" + name, v.shape, mybir.dt.from_np(v.dtype), kind="ExternalInput").ap()
        a[name] = ap
    out = nc.dram_tensor("out_0", (1, SEQ, D), F32, kind="ExternalOutput").ap()
    build(nc, a, out, PARTS)
    r = run_bass_kernel_spmd(nc, [arrays], core_ids=[0])
    return r.results[0]["out_0"]
```

```python
from contextlib import ExitStack, contextmanager

import numpy as np
import concourse.bass as bass
from concourse import mybir

P = 128
F32 = mybir.dt.float32
I32 = mybir.dt.int32
U32 = mybir.dt.uint32
ALU = mybir.AluOpType
ACT = mybir.ActivationFunctionType
AX = mybir.AxisListType.X

SEQ, D = 512, 1024
T = SEQ // P
KD = D // P
EPS = 1e-6

EXPERTS, GROUPS, PER_GROUP, FF = 64, 8, 8, 256
SLOTS = 32
OVER = 2 * SEQ // SLOTS
ROWS = (EXPERTS + OVER) * SLOTS
NBUF = 4
GU = KD * 2 * FF
DN = 2 * D


class Memory:
    pass


@contextmanager
def semaphores_of(nc, g):
    outer, taken = g.sem, []

    def take(name):
        taken.append(nc.alloc_semaphore(name=name))
        return taken[-1]
    g.sem = take
    yield
    g.sem = outer
    nc.clear_and_free_semaphores(taken)
    nc.all_engine_barrier()


def make_shared(nc, ctx):
    def sb(name, shape, dt=F32):
        return ctx.enter_context(nc.sbuf_tensor(name, shape, dt))
    g = Memory()
    g.sem = lambda name: ctx.enter_context(nc.semaphore(name))
    g.bank = [ctx.enter_context(nc.psum_tensor(f"bank{i}", [P, 512], F32)) for i in range(8)]
    g.x = sb("x_res", [P, T, D])
    g.hT = sb("hT", [P, KD, SEQ])
    g.big = sb("big", [P, 8192])
    g.xn = g.big[:, 0:T * D].rearrange("p (t d) -> p t d", t=T)
    g.w = sb("w_ring", [P, NBUF, GU + DN])
    g.ident = sb("ident", [P, P])
    g.ones = sb("ones", [P, P])
    g.tri = sb("tri", [P, P])
    g.tri_strict = sb("tri_strict", [P, P])
    g.eps = sb("eps", [P, 1])
    g.sel = sb("sel", [P, 2, SLOTS])
    g.half = sb("half", [P, 2])
    g.iota8 = sb("iota8", [P, 8])
    g.iota_e = sb("iota_e", [P, EXPERTS])
    g.iota_b = sb("iota_b", [P, OVER])
    g.gains = sb("gains", [P, 6, KD])
    g.ss = sb("ss", [P, T])
    g.lnss = sb("lnss", [P, T])
    g.ss2 = sb("ss2", [P, T])
    g.rstd = sb("rstd", [P, T])
    return g


def zero_chunks(m):
    return [m.xd[n:n + 512, :] for n in range(0, ROWS, 512)] +\
        [m.yd[n:n + 512, :] for n in range(EXPERTS * SLOTS, ROWS, 512)]


def stage_setup(nc, g, m, gd, a):
    wz = g.sem("zeros_made")
    step, small, xin = g.sem("setup_step"), g.sem("small_loaded"), g.sem("x_loaded")
    with nc.Block() as block:
        @block.sync
        def _(sp):
            sp.dma_start(g.x[:, :, :], a["x"][0].rearrange("(t p) d -> p t d", p=P)).then_inc(xin, 16)
            for n, src in enumerate((a["norm_mix_g"], a["norm_ffn_g"], a["norm_ple_g"])):
                for layer in range(2):
                    sp.dma_start(g.gains[:, 2 * n + layer, :],
                                 src[layer].rearrange("(p k) -> p k", k=KD)).then_inc(small, 16)
            load_gates(sp, gd, a)
            for part in range(4):
                load_delta(sp, gd, a, part, 0)
            sp.wait_ge(wz, 1)
            for rows in zero_chunks(m):
                sp.dma_start(rows.rearrange("(p r) (a c) -> p (r a) c", p=P, a=4),
                             m.zeros.unsqueeze(1).to_broadcast([P, 16, 256])).then_inc(m.rows_zeroed, 16)
            sp.wait_ge(small, 96)
            sp.wait_ge(xin, 16)

        @block.gpsimd
        def _(pool):
            count = [0]

            def done(ins):
                count[0] += 1
                ins.then_inc(step, 1)
                pool.wait_ge(step, count[0])

            pool.memset(m.zeros, 0.0).then_inc(wz, 1)
            pool.memset(g.ones[:, :], 1.0).then_inc(step, 1)
            pool.memset(g.eps[:, :], EPS).then_inc(step, 1)
            pool.memset(g.ident[:, :], 0.0).then_inc(step, 1)
            pool.memset(g.tri[:, :], 1.0).then_inc(step, 1)
            pool.memset(g.tri_strict[:, :], 1.0).then_inc(step, 1)
            pool.memset(g.sel[:, :, :], 0.0).then_inc(step, 1)
            count[0] = 6
            done(pool.memset(g.half[:, :], 0.0))
            for q in range(4):
                done(pool.memset(g.half[32 * q:32 * q + 32, q % 2:q % 2 + 1], 1.0))
            done(pool.affine_select(out=g.ident[:, :], in_=g.ident[:, :], compare_op=ALU.not_equal, fill=1.0,
                                    base=0, pattern=[[-1, P]], channel_multiplier=1))
            done(pool.affine_select(out=g.tri[:, :], in_=g.tri[:, :], compare_op=ALU.is_ge, fill=0.0,
                                    base=0, pattern=[[1, P]], channel_multiplier=-1))
            done(pool.affine_select(out=g.tri_strict[:, :], in_=g.tri_strict[:, :], compare_op=ALU.is_gt, fill=0.0,
                                    base=0, pattern=[[1, P]], channel_multiplier=-1))
            for q in range(2):
                done(pool.affine_select(out=g.sel[:, :, :], in_=g.sel[:, :, :], compare_op=ALU.not_equal, fill=1.0,
                                        base=-32 * q, pattern=[[-64, 2], [-1, SLOTS]], channel_multiplier=1))
            done(pool.iota(g.iota8[:, :], pattern=[[1, 8]], base=-8, channel_multiplier=0,
                           allow_small_or_imprecise_dtypes=True))
            done(pool.iota(g.iota_e[:, :], pattern=[[SLOTS, EXPERTS]], base=0, channel_multiplier=0,
                           allow_small_or_imprecise_dtypes=True))
            done(pool.iota(g.iota_b[:, :], pattern=[[1, OVER]], base=0, channel_multiplier=0,
                           allow_small_or_imprecise_dtypes=True))


def stage_norm(nc, g, tag, gain, sync_work=None):
    sq, rs, xn = g.sem(tag + "_squares"), g.sem(tag + "_rstd"), [g.sem(f"{tag}_xn{t}") for t in range(T)]
    halves = [(g.bank[2 * t], g.bank[2 * t + 1]) for t in range(T)]
    tp, ev = g.sem(tag + "_transposed"), [g.sem(tag + "_taken_dve"), g.sem(tag + "_taken_act")]
    gcol = g.gains[:, gain, :]
    with nc.Block() as block:
        if sync_work:
            block.sync(sync_work)

        @block.scalar
        def _(act):
            for t in range(T):
                act.activation(g.xn[:, t, :], g.x[:, t, :], ACT.Square, accum_out=g.ss[:, t:t + 1]).then_inc(sq, 1)
            act.wait_ge(sq, T)
            act.activation(g.lnss[:, :], g.ss[:, :], ACT.Ln, scale=1.0 / D, bias=g.eps[:, 0:1]).then_inc(rs, 1)
            act.wait_ge(rs, 1)
            act.activation(g.rstd[:, :], g.lnss[:, :], ACT.Exp, scale=-0.5).then_inc(rs, 1)
            for t in range(1, T, 2):
                act.wait_ge(rs, 2)
                act.activation(g.xn[:, t, :], g.x[:, t, :], ACT.Copy, scale=g.rstd[:, t:t + 1]).then_inc(xn[t], 1)
            for t in range(T):
                act.wait_ge(tp, 2 * t + 2)
                for k in range(KD // 2, KD):
                    act.activation(g.hT[:, k, t * P:(t + 1) * P], halves[t][1][:, (k - KD // 2) * P:(k - KD // 2 + 1) * P], ACT.Copy,
                                   scale=gcol[:, k:k + 1]).then_inc(ev[1], 1)

        @block.vector
        def _(dve):
            dve.wait_ge(rs, 2)
            for t in range(0, T, 2):
                dve.tensor_scalar(g.xn[:, t, :], g.x[:, t, :], g.rstd[:, t:t + 1], None, ALU.mult).then_inc(xn[t], 1)
            for t in range(T):
                dve.wait_ge(tp, 2 * t + 1)
                dve.tensor_tensor(g.hT[:, 0:KD // 2, t * P:(t + 1) * P],
                                  halves[t][0][:, :].rearrange("p (k i) -> p k i", k=KD // 2),
                                  gcol[:, 0:KD // 2].unsqueeze(2).to_broadcast([P, KD // 2, P]),
                                  ALU.mult).then_inc(ev[0], 1)

        @block.tensor
        def _(pe):
            for t in range(T):
                pe.wait_ge(xn[t], 1)
                for h in range(2):
                    for k in range(KD // 2):
                        last = pe.transpose(halves[t][h][:, k * P:(k + 1) * P], g.xn[:, t, KD // 2 * h + k::KD],
                                            g.ident[:, :])
                    last.then_inc(tp, 1)


def moe_memory(nc, ctx, g):
    def sb(name, shape, dt=F32):
        return ctx.enter_context(nc.sbuf_tensor(name, shape, dt))
    m = Memory()
    m.wr = sb("w_router", [P, KD, GROUPS + EXPERTS])
    m.lg = sb("logits", [P, T, GROUPS + EXPERTS])
    m.s = {n: sb("r_" + n, [P, T]) for n in
           "gmax gidx gz gprob m1 i1 m2 i2 dif q s r".split()}
    m.e8 = {n: sb("r_" + n, [P, T, 8]) for n in "eq cand ohg gexp ing oh1 oh2 masked".split()}
    m.ew = [sb(f"expert_w{k}", [P, T]) for k in range(2)]
    m.oh = [sb(f"onehot{k}", [P, T, EXPERTS]) for k in range(2)]
    m.both = sb("onehot_both", [P, T, EXPERTS])
    m.rank = sb("rank", [P, T, EXPERTS])
    m.tmp = sb("rank_tmp", [P, T, EXPERTS])
    m.cnt = sb("cnt", [P, EXPERTS])
    m.cnt_i = sb("cnt_i", [P, EXPERTS], I32)
    m.nov = sb("nov", [P, EXPERTS])
    m.cs = [sb(f"cs{i}", [P, EXPERTS]) for i in range(2)]
    m.base = sb("base", [P, EXPERTS])
    m.first = sb("first", [P, EXPERTS])
    m.destf = sb("destf", [P, 2, T])
    m.dest = [sb(f"dest{k}_{t}", [P, 1], U32) for k in range(2) for t in range(T)]
    m.cmp = sb("cmp", [1, OVER, EXPERTS])
    m.tblf = sb("tblf", [1, OVER + 1])
    m.tbl = sb("tbl", [1, OVER + 1], I32)
    m.xT = [sb(f"xT{i}", [P, KD, SLOTS]) for i in range(2)]
    m.sg = [sb(f"sg{i}", [P, 64]) for i in range(2)]
    m.um = [sb(f"um{i}", [P, 2, 64]) for i in range(2)]
    m.h2 = [sb(f"h2_{i}", [P, 2, 64]) for i in range(2)]
    m.hTe = [sb(f"hTe{i}", [P, 2, SLOTS]) for i in range(2)]
    m.y = [sb(f"y{i}", [P, 256]) for i in range(2)]
    m.xs = [g.big[0:SLOTS, 4096 + D * i:4096 + D * (i + 1)] for i in range(NBUF)]
    m.gu = [g.w[:, i, 0:GU].rearrange("p (k f) -> p k f", k=KD) for i in range(NBUF)]
    m.dn = [g.w[:, i, GU:GU + DN].rearrange("p (i d) -> p i d", i=2) for i in range(NBUF)]
    m.xd = nc.dram_tensor("rows_in", [ROWS, D], F32, kind="Internal").ap()
    m.yd = nc.dram_tensor("rows_out", [ROWS, D], F32, kind="Internal").ap()
    m.zeros = m.rank[:, :, :].rearrange("p t e -> p (t e)")
    m.rows_zeroed = g.sem("rows_zeroed")
    m.loaded = [[g.sem(f"expert_w_loaded{l}_{i}") for i in range(NBUF)] for l in range(2)]
    return m


def load_expert(sp, m, a, layer, buf, e, signal):
    if isinstance(e, int):
        gu, dn = a["moe_w_gate_up"][layer, e], a["moe_w_down"][layer, e]
        gu, dn = gu.rearrange("(p k) f -> p k f", k=KD), dn.rearrange("(i p) d -> p i d", p=P)
    else:
        gu = a["moe_w_gate_up"][layer, bass.ds(e, 1)].rearrange("a (p k) f -> p (a k) f", k=KD)
        dn = a["moe_w_down"][layer, bass.ds(e, 1)].rearrange("a (i p) d -> p (a i) d", p=P)
    sp.dma_start(m.gu[buf], gu).then_inc(signal, 16)
    sp.dma_start(m.dn[buf], dn).then_inc(signal, 16)


def stage_route(nc, g, m, a, layer, sync_work=None):
    tag = f"route{layer}"
    wr_in, logits, lgc = g.sem(tag + "_w_in"), g.sem(tag + "_logits"), g.sem(tag + "_logits_taken")
    vs, ex_in, ex = g.sem(tag + "_step"), g.sem(tag + "_exp_in"), g.sem(tag + "_exp")
    both, counted, rows = g.sem(tag + "_onehots"), g.sem(tag + "_counted"), g.sem(tag + "_dest")
    sent = g.sem(tag + "_rows_sent")
    with nc.Block() as block:
        @block.sync
        def _(sp):
            if sync_work:
                sync_work(sp)

        @block.tensor
        def _(pe):
            pe.wait_ge(m.wr_in[layer], 32)
            n = GROUPS + EXPERTS
            for t in range(T):
                for k in range(KD):
                    last = pe.matmul(g.bank[0][:, t * n:(t + 1) * n], g.hT[:, k, t * P:(t + 1) * P], m.wr[:, k, :],
                                     start=k == 0, stop=k == KD - 1)
            last.then_inc(logits, 1)
            pe.wait_ge(both, 1)
            for t in range(T):
                for u in range(t + 1):
                    pe.matmul(g.bank[1][:, t * EXPERTS:(t + 1) * EXPERTS], g.ones[:, :] if u < t else g.tri_strict[:, :],
                              m.both[:, u, :], start=u == 0, stop=u == t)
            for u in range(T):
                last = pe.matmul(g.bank[2][:, 0:EXPERTS], g.ones[:, :], m.both[:, u, :], start=u == 0, stop=u == T - 1)
            last.then_inc(counted, 1)

        @block.scalar
        def _(act):
            act.wait_ge(ex_in, 1)
            act.activation(m.e8["gexp"][:, :, :], m.e8["cand"][:, :, :], ACT.Exp).then_inc(ex, 1)
            act.wait_ge(ex_in, 2)
            act.activation(m.s["q"][:, :], m.s["dif"][:, :], ACT.Exp).then_inc(ex, 1)

        @block.vector
        def _(dve):
            count = [0]

            def done(ins):
                count[0] += 1
                ins.then_inc(vs, 1)
                dve.wait_ge(vs, count[0])

            def bc(v, n):
                return v[:, :].unsqueeze(2).to_broadcast([P, T, n])

            def first_of(src, top, idx, onehot):
                done(dve.tensor_reduce(top[:, :], src, AX, ALU.max))
                done(dve.tensor_tensor(m.e8["eq"][:, :, :], src, bc(top, 8), ALU.is_equal))
                done(dve.tensor_tensor(m.e8["masked"][:, :, :], m.e8["eq"][:, :, :], iota8, ALU.mult))
                done(dve.tensor_reduce(idx[:, :], m.e8["masked"][:, :, :], AX, ALU.min))
                done(dve.tensor_tensor(onehot[:, :, :], iota8, bc(idx, 8), ALU.is_equal))

            iota8 = g.iota8[:, :].unsqueeze(1).to_broadcast([P, T, 8])
            s, e8 = m.s, m.e8
            dve.wait_ge(logits, 1)
            done(dve.tensor_copy(m.lg[:, :, :], g.bank[0][:, 0:T * 72].rearrange("p (t n) -> p t n", t=T)))
            gl = m.lg[:, :, 0:GROUPS]
            el = m.lg[:, :, GROUPS:].rearrange("p t (g e) -> p t g e", g=GROUPS)
            first_of(gl, s["gmax"], s["gidx"], e8["ohg"])
            dve.tensor_tensor(e8["cand"][:, :, :], gl, bc(s["gmax"], 8), ALU.subtract).then_inc(ex_in, 1)
            picked = m.tmp[:, :, :].rearrange("p t (g e) -> p t g e", g=GROUPS)
            done(dve.tensor_tensor(picked, el, e8["ohg"][:, :, :].unsqueeze(3).to_broadcast([P, T, GROUPS, PER_GROUP]),
                                   ALU.mult))
            done(dve.tensor_reduce(e8["ing"][:, :, :], m.tmp[:, :, :].rearrange("p t (g e) -> p t e g", g=GROUPS),
                                   AX, ALU.add))
            first_of(e8["ing"][:, :, :], s["m1"], s["i1"], e8["oh1"])
            done(dve.scalar_tensor_tensor(out=e8["eq"][:, :, :], in0=e8["oh1"][:, :, :],
                                          scalar=-3e38, in1=e8["ing"][:, :, :], op0=ALU.mult, op1=ALU.add))
            done(dve.tensor_copy(e8["ing"][:, :, :], e8["eq"][:, :, :]))
            first_of(e8["ing"][:, :, :], s["m2"], s["i2"], e8["oh2"])
            dve.tensor_tensor(s["dif"][:, :], s["m2"][:, :], s["m1"][:, :], ALU.subtract).then_inc(ex_in, 1)
            for k, name in enumerate(("oh1", "oh2")):
                done(dve.tensor_tensor(m.oh[k][:, :, :].rearrange("p t (g e) -> p t g e", g=GROUPS),
                                       e8["ohg"][:, :, :].unsqueeze(3).to_broadcast([P, T, GROUPS, PER_GROUP]),
                                       e8[name][:, :, :].unsqueeze(2).to_broadcast([P, T, GROUPS, PER_GROUP]), ALU.mult))
            dve.tensor_tensor(m.both[:, :, :], m.oh[0][:, :, :], m.oh[1][:, :, :], ALU.add).then_inc(both, 1)
            dve.wait_ge(ex, 2)
            done(dve.tensor_reduce(s["gz"][:, :], e8["gexp"][:, :, :], AX, ALU.add))
            done(dve.reciprocal(s["gprob"][:, :], s["gz"][:, :]))
            done(dve.tensor_scalar(s["s"][:, :], s["q"][:, :], 1.0, None, ALU.add))
            done(dve.reciprocal(s["r"][:, :], s["s"][:, :]))
            done(dve.tensor_tensor(m.ew[0][:, :], s["gprob"][:, :], s["r"][:, :], ALU.mult))
            done(dve.tensor_tensor(m.ew[1][:, :], m.ew[0][:, :], s["q"][:, :], ALU.mult))
            dve.wait_ge(counted, 1)
            done(dve.tensor_copy(m.rank[:, :, :], g.bank[1][:, 0:T * EXPERTS].rearrange("p (t e) -> p t e", t=T)))
            done(dve.tensor_scalar(m.cnt_i[:, :], g.bank[2][:, 0:EXPERTS], SLOTS - 1.0, None, ALU.add))
            done(dve.tensor_scalar(m.cnt_i[:, :], m.cnt_i[:, :], SLOTS.bit_length() - 1, None, ALU.arith_shift_right))
            done(dve.tensor_scalar(m.nov[:, :], m.cnt_i[:, :], -1.0, 0.0, ALU.add, ALU.max))
            done(dve.tensor_copy(m.cs[0][:, :], m.nov[:, :]))
            now, n = 0, 1
            while n < EXPERTS:
                done(dve.tensor_copy(m.cs[1 - now][:, 0:n], m.cs[now][:, 0:n]))
                done(dve.tensor_tensor(m.cs[1 - now][:, n:], m.cs[now][:, n:], m.cs[now][:, 0:EXPERTS - n], ALU.add))
                now, n = 1 - now, 2 * n
            cs = m.cs[now]
            done(dve.tensor_tensor(m.base[:, :], cs[:, :], m.nov[:, :], ALU.subtract))
            done(dve.tensor_scalar(m.base[:, :], m.base[:, :], float(SLOTS), float(SLOTS * (EXPERTS - 1)), ALU.mult, ALU.add))
            done(dve.tensor_tensor(m.first[:, :], g.iota_e[:, :], m.base[:, :], ALU.subtract))
            done(dve.tensor_scalar(m.tmp[:, :, :], m.rank[:, :, :], float(SLOTS), None, ALU.is_lt))
            done(dve.tensor_tensor(m.tmp[:, :, :], m.tmp[:, :, :],
                                   m.first[:, :].unsqueeze(1).to_broadcast([P, T, EXPERTS]), ALU.mult))
            done(dve.tensor_tensor(m.rank[:, :, :], m.rank[:, :, :], m.tmp[:, :, :], ALU.add))
            done(dve.tensor_tensor(m.rank[:, :, :], m.rank[:, :, :],
                                   m.base[:, :].unsqueeze(1).to_broadcast([P, T, EXPERTS]), ALU.add))
            for k in range(2):
                done(dve.tensor_tensor(m.tmp[:, :, :], m.rank[:, :, :], m.oh[k][:, :, :], ALU.mult))
                done(dve.tensor_reduce(m.destf[:, k, :], m.tmp[:, :, :], AX, ALU.add))
                for t in range(T):
                    dve.tensor_copy(m.dest[k * T + t][:, :], m.destf[:, k, t:t + 1]).then_inc(rows, 1)
            done(dve.tensor_tensor(m.cmp[:, :, :], cs[0:1, :].unsqueeze(1).to_broadcast([1, OVER, EXPERTS]),
                                   g.iota_b[0:1, :].unsqueeze(2).to_broadcast([1, OVER, EXPERTS]), ALU.is_le))
            done(dve.tensor_reduce(m.tblf[:, 0:OVER], m.cmp[:, :, :], AX, ALU.add))
            done(dve.tensor_scalar(m.tbl[:, 0:OVER], m.tblf[:, 0:OVER], EXPERTS - 1.0, None, ALU.min))
            done(dve.tensor_scalar(m.tbl[:, OVER:OVER + 1], cs[0:1, EXPERTS - 1:EXPERTS], 0.0, None, ALU.max))

        @block.gpsimd
        def _(pool):
            for i in range(2 * T):
                pool.wait_ge(rows, i + 1)
                pool.indirect_dma_start(m.xd, bass.IndirectOffsetOnAxis(ap=m.dest[i][:, 0:1], axis=0),
                                        g.xn[:, i % T, :], None).then_inc(sent, 16)
            pool.wait_ge(sent, 16 * 2 * T)


def stage_experts(nc, g, m, a, layer):
    tag = f"exp{layer}"
    loaded = m.loaded[layer]
    xs_in = [g.sem(f"{tag}_rows_in{i}") for i in range(NBUF)]
    names = "xt xT gu sg um h2 ht hT dn y".split()
    S = {n: g.sem(f"{tag}_{n}") for n in names}
    y_out = [g.sem(f"{tag}_y_out{i}") for i in range(2)]
    gcol = g.gains[:, 2 + layer, :].unsqueeze(2).to_broadcast([P, KD, SLOTS])
    PASSES = EXPERTS // NBUF
    with nc.Block() as block:
        @block.sync
        def _(sp):
            for i in range(NBUF):
                sp.dma_start(m.xs[i], m.xd[SLOTS * i:SLOTS * (i + 1), :]).then_inc(xs_in[i], 16)
            with sp.Fori(1, PASSES) as it:
                for i in range(NBUF):
                    sp.wait_ge(S["dn"], NBUF * (it - 1) + i + 1)
                    load_expert(sp, m, a, layer, i, NBUF * it + i, loaded[i])
                    sp.dma_start(m.xs[i], m.xd[bass.ds(SLOTS * (NBUF * it + i), SLOTS), :]).then_inc(xs_in[i], 16)

        @block.tensor
        def _(pe):
            def rows(it, i):
                j = i % 2
                pe.wait_ge(xs_in[i], 16 * (it + 1))
                if not (isinstance(it, int) and it == 0 and i < 2):
                    pe.wait_ge(S["xT"], NBUF * it + i - 1)
                for k in range(KD):
                    last = pe.matmul(g.bank[j][:, SLOTS * k:SLOTS * (k + 1)], m.xs[i][:, k::KD],
                                     g.ident[0:SLOTS, 0:SLOTS], start=True, stop=True)
                last.then_inc(S["xt"], 1)

            def gate_up(it, i):
                j = i % 2
                pe.wait_ge(loaded[i], 32 * (it + 1))
                pe.wait_ge(S["xT"], NBUF * it + i + 1)
                if not (isinstance(it, int) and it == 0 and i < 2):
                    pe.wait_ge(S["um"], NBUF * it + i - 1)
                    pe.wait_ge(S["sg"], NBUF * it + i - 1)
                for k in range(KD):
                    w = m.gu[i][:, k, :].rearrange("p (h q c) -> p q h c", h=2, q=4)
                    for q in range(4):
                        last = pe.matmul(g.bank[2 + j][32 * q:32 * q + 32, 0:P].rearrange("p (h c) -> p h c", h=2),
                                         m.xT[j][:, k, :], w[:, q], start=k == 0, stop=k == KD - 1)
                last.then_inc(S["gu"], 1)

            def down(it, i):
                j, b = (i - 1) % NBUF, NBUF * it + i - 1
                r = j % 2
                pe.wait_ge(S["h2"], b + 1)
                if not (isinstance(b, int) and b < 2):
                    pe.wait_ge(S["hT"], b - 1)
                pe.matmul(g.bank[4 + r][:, 0:2 * SLOTS], m.h2[r][:, :, :].rearrange("p h c -> p (h c)"),
                          g.sel[:, :, :].rearrange("p i s -> p (i s)"), start=True, stop=True).then_inc(S["ht"], 1)
                pe.wait_ge(S["hT"], b + 1)
                if not (isinstance(b, int) and b < 2):
                    pe.wait_ge(S["y"], b - 1)
                for n in range(2):
                    for q in range(4):
                        last = pe.matmul(g.bank[6 + r][32 * q:32 * q + 32, 0:256], m.hTe[r][:, n, :],
                                         m.dn[j][:, n, 256 * q:256 * (q + 1)], start=n == 0, stop=n == 1)
                last.then_inc(S["dn"], 1)

            def turn(it):
                for i in range(NBUF):
                    rows(it, i)
                    if not (isinstance(it, int) and it == 0 and i == 0):
                        down(it, i)
                    gate_up(it, i)

            turn(0)
            with pe.Fori(1, PASSES) as it:
                turn(it)
            down(PASSES, 0)

        def vector_turn(dve, it):
            first = isinstance(it, int)
            for i in range(NBUF):
                j, b = i % 2, NBUF * it + i
                early = first and i < 2
                dve.wait_ge(S["xt"], b + 1)
                if not early:
                    dve.wait_ge(S["gu"], b - 1)
                dve.tensor_tensor(m.xT[j][:, :, :], g.bank[j][:, 0:KD * SLOTS].rearrange("p (k s) -> p k s", k=KD),
                                  gcol, ALU.mult).then_inc(S["xT"], 1)
                dve.wait_ge(S["gu"], b + 1)
                dve.wait_ge(S["sg"], b + 1)
                dve.tensor_tensor(m.um[j][:, :, :], g.bank[2 + j][:, 64:128].unsqueeze(1).to_broadcast([P, 2, 64]),
                                  g.half[:, :].unsqueeze(2).to_broadcast([P, 2, 64]), ALU.mult).then_inc(S["um"], 1)
                dve.wait_ge(S["um"], b + 1)
                if not early:
                    dve.wait_ge(S["ht"], b - 1)
                dve.tensor_tensor(m.h2[j][:, :, :], m.um[j][:, :, :],
                                  m.sg[j][:, :].unsqueeze(1).to_broadcast([P, 2, 64]), ALU.mult).then_inc(S["h2"], 1)
                dve.wait_ge(S["ht"], b + 1)
                if not early:
                    dve.wait_ge(S["dn"], b - 1)
                dve.tensor_copy(m.hTe[j][:, :, :],
                                g.bank[4 + j][:, 0:2 * SLOTS].rearrange("p (i s) -> p i s", i=2)).then_inc(S["hT"], 1)

        @block.vector
        def _(dve):
            vector_turn(dve, 0)
            with dve.Fori(1, PASSES) as it:
                vector_turn(dve, it)

        def scalar_turn(act, it):
            first = isinstance(it, int)
            for i in range(NBUF):
                j, b = i % 2, NBUF * it + i
                early = first and i < 2
                act.wait_ge(S["gu"], b + 1)
                if not early:
                    act.wait_ge(S["h2"], b - 1)
                act.activation(m.sg[j][:, :], g.bank[2 + j][:, 0:64], ACT.Silu).then_inc(S["sg"], 1)
                act.wait_ge(S["dn"], b + 1)
                if not early:
                    act.wait_ge(y_out[j], 16 * 4 * (2 * it + i // 2))
                act.activation(m.y[j][:, :], g.bank[6 + j][:, 0:256], ACT.Copy).then_inc(S["y"], 1)
                act.wait_ge(S["y"], b + 1)
                for q in range(4):
                    act.dma_start(m.yd[bass.ds(SLOTS * b, SLOTS), 256 * q:256 * (q + 1)],
                                  m.y[j][32 * q:32 * q + 32, :]).then_inc(y_out[j], 16)

        @block.scalar
        def _(act):
            scalar_turn(act, 0)
            with act.Fori(1, PASSES) as it:
                scalar_turn(act, it)
            for j in range(2):
                act.wait_ge(y_out[j], 16 * 4 * EXPERTS // 2)


def stage_overflow(nc, g, m, a, layer):
    tag = f"over{layer}"
    names = "w xs xt xT gu sg um h2 ht hT dn y out".split()
    S = {n: g.sem(f"{tag}_{n}") for n in names}
    gcol = g.gains[:, 2 + layer, :].unsqueeze(2).to_broadcast([P, KD, SLOTS])

    def blocks(eng):
        return eng.value_load(m.tbl[0:1, OVER:OVER + 1], min_val=0, max_val=OVER)

    with nc.Block() as block:
        @block.sync
        def _(sp):
            n = blocks(sp)
            with sp.If(n > 0), sp.Fori(0, n) as it:
                sp.wait_ge(S["dn"], it + 1)
                e = sp.value_load(m.tbl[0:1, bass.ds(it, 1)], min_val=0, max_val=EXPERTS - 1)
                load_expert(sp, m, a, layer, 0, e, S["w"])
                sp.dma_start(m.xs[0], m.xd[bass.ds(SLOTS * (EXPERTS + it), SLOTS), :]).then_inc(S["xs"], 16)

        @block.tensor
        def _(pe):
            pe.sem_inc(S["dn"], 1)
            n = blocks(pe)
            with pe.If(n > 0), pe.Fori(0, n) as it:
                pe.wait_ge(S["xs"], 16 * (it + 1))
                for k in range(KD):
                    last = pe.matmul(g.bank[0][:, SLOTS * k:SLOTS * (k + 1)], m.xs[0][:, k::KD],
                                     g.ident[0:SLOTS, 0:SLOTS], start=True, stop=True)
                last.then_inc(S["xt"], 1)
                pe.wait_ge(S["w"], 32 * (it + 1))
                pe.wait_ge(S["xT"], it + 1)
                for k in range(KD):
                    w = m.gu[0][:, k, :].rearrange("p (h q c) -> p q h c", h=2, q=4)
                    for q in range(4):
                        last = pe.matmul(g.bank[2][32 * q:32 * q + 32, 0:P].rearrange("p (h c) -> p h c", h=2),
                                         m.xT[0][:, k, :], w[:, q], start=k == 0, stop=k == KD - 1)
                last.then_inc(S["gu"], 1)
                pe.wait_ge(S["h2"], it + 1)
                pe.matmul(g.bank[4][:, 0:2 * SLOTS], m.h2[0][:, :, :].rearrange("p h c -> p (h c)"),
                          g.sel[:, :, :].rearrange("p i s -> p (i s)"), start=True, stop=True).then_inc(S["ht"], 1)
                pe.wait_ge(S["hT"], it + 1)
                for n in range(2):
                    for q in range(4):
                        last = pe.matmul(g.bank[6][32 * q:32 * q + 32, 0:256], m.hTe[0][:, n, :],
                                         m.dn[0][:, n, 256 * q:256 * (q + 1)], start=n == 0, stop=n == 1)
                last.then_inc(S["dn"], 1)
                pe.wait_ge(S["y"], it + 1)

        @block.vector
        def _(dve):
            n = blocks(dve)
            with dve.If(n > 0), dve.Fori(0, n) as it:
                dve.wait_ge(S["xt"], it + 1)
                dve.tensor_tensor(m.xT[0][:, :, :], g.bank[0][:, 0:KD * SLOTS].rearrange("p (k s) -> p k s", k=KD),
                                  gcol, ALU.mult).then_inc(S["xT"], 1)
                dve.wait_ge(S["gu"], it + 1)
                dve.wait_ge(S["sg"], it + 1)
                dve.tensor_tensor(m.um[0][:, :, :], g.bank[2][:, 64:128].unsqueeze(1).to_broadcast([P, 2, 64]),
                                  g.half[:, :].unsqueeze(2).to_broadcast([P, 2, 64]), ALU.mult).then_inc(S["um"], 1)
                dve.wait_ge(S["um"], it + 1)
                dve.tensor_tensor(m.h2[0][:, :, :], m.um[0][:, :, :],
                                  m.sg[0][:, :].unsqueeze(1).to_broadcast([P, 2, 64]), ALU.mult).then_inc(S["h2"], 1)
                dve.wait_ge(S["ht"], it + 1)
                dve.tensor_copy(m.hTe[0][:, :, :],
                                g.bank[4][:, 0:2 * SLOTS].rearrange("p (i s) -> p i s", i=2)).then_inc(S["hT"], 1)

        @block.scalar
        def _(act):
            n = blocks(act)
            with act.If(n > 0), act.Fori(0, n) as it:
                act.wait_ge(S["gu"], it + 1)
                act.activation(m.sg[0][:, :], g.bank[2][:, 0:64], ACT.Silu).then_inc(S["sg"], 1)
                act.wait_ge(S["dn"], it + 2)
                act.activation(m.y[0][:, :], g.bank[6][:, 0:256], ACT.Copy).then_inc(S["y"], 1)
                act.wait_ge(S["out"], 16 * 4 * (it + 1))

        @block.gpsimd
        def _(pool):
            n = blocks(pool)
            with pool.If(n > 0), pool.Fori(0, n) as it:
                pool.wait_ge(S["y"], it + 1)
                for q in range(4):
                    pool.dma_start(m.yd[bass.ds(SLOTS * (EXPERTS + it), SLOTS), 256 * q:256 * (q + 1)],
                                   m.y[0][32 * q:32 * q + 32, :]).then_inc(S["out"], 16)
                pool.wait_ge(S["out"], 16 * 4 * (it + 1))


def stage_combine(nc, g, m, layer, sync_work=None):
    tag = f"comb{layer}"
    got = [g.sem(f"{tag}_row{i}") for i in range(2 * T)]
    added = g.sem(tag + "_added")
    rows = g.big[:, :].rearrange("p (n d) -> p n d", d=D)
    with nc.Block() as block:
        @block.sync
        def _(sp):
            for i in range(2 * T):
                sp.wait_ge(got[i], 16)
            if sync_work:
                sync_work(sp)

        @block.gpsimd
        def _(pool):
            for i in range(2 * T):
                pool.indirect_dma_start(rows[:, i, :], None, m.yd,
                                        bass.IndirectOffsetOnAxis(ap=m.dest[i][:, 0:1], axis=0)).then_inc(got[i], 16)

        @block.vector
        def _(dve):
            for i in range(2 * T):
                t = i % T
                dve.wait_ge(got[i], 16)
                if i >= T:
                    dve.wait_ge(added, i - T + 1)
                dve.scalar_tensor_tensor(out=g.x[:, t, :], in0=rows[:, i, :], scalar=m.ew[i // T][:, t:t + 1],
                                         in1=g.x[:, t, :], op0=ALU.mult, op1=ALU.add).then_inc(added, 1)


def ple_load(sp, a, g, layer, wsem):
    flat = g.w[:, 2:4, :].rearrange("p n f -> p (n f)")
    sp.dma_start(flat[:, 0:KD * D].rearrange("p (k n) -> p k n", k=KD),
                 a["ple_w_gate"][layer].rearrange("(p k) n -> p k n", k=KD)).then_inc(wsem, 16)
    sp.dma_start(flat[:, KD * D:KD * D + 2 * D].rearrange("p (k n) -> p k n", k=2),
                 a["ple_w_proj"][layer].rearrange("(k p) n -> p k n", p=P)).then_inc(wsem, 16)


def stage_ple(nc, g, a, layer, wsem, sync_work=None):
    tag = f"ple{layer}"
    pin, tp, pT = g.sem(tag + "_p_in"), g.sem(tag + "_p_transposed"), g.sem(tag + "_pT")
    gate, proj, sig, mul, add = (g.sem(f"{tag}_{n}") for n in "gate proj sigmoid product added".split())
    pn = g.big[:, 4096:5120].rearrange("p (t c) -> p t c", t=T)
    pTt = g.big[:, 5120:6144].rearrange("p (k s) -> p k s", k=2)
    sg = [g.big[:, 6144 + 512 * i:6656 + 512 * i] for i in range(2)]
    pr = [g.big[:, 7168 + 512 * i:7680 + 512 * i] for i in range(2)]
    flat = g.w[:, 2:4, :].rearrange("p n f -> p (n f)")
    wg = flat[:, 0:KD * D].rearrange("p (k n) -> p k n", k=KD)
    wp = flat[:, KD * D:KD * D + 2 * D].rearrange("p (k n) -> p k n", k=2)
    steps = [(t, h) for t in range(T) for h in range(2)]
    with nc.Block() as block:
        @block.sync
        def _(sp):
            sp.dma_start(pn, a["p"][layer, 0].rearrange("(t p) c -> p t c", p=P)).then_inc(pin, 16)
            if sync_work:
                sync_work(sp)

        @block.tensor
        def _(pe):
            pe.wait_ge(pin, 16)
            for k in range(2):
                for t in range(T):
                    last = pe.transpose(g.bank[6 + k][:, t * P:(t + 1) * P], pn[:, t, k * P:(k + 1) * P], g.ident[:, :])
                last.then_inc(tp, 1)
            pe.wait_ge(wsem, 32)
            pe.wait_ge(pT, 2)
            for n, (t, h) in enumerate(steps):
                if n >= 3:
                    pe.wait_ge(sig, n - 2)
                for k in range(KD):
                    last = pe.matmul(g.bank[n % 3][:, :], g.hT[:, k, t * P:(t + 1) * P], wg[:, k, 512 * h:512 * (h + 1)],
                                     start=k == 0, stop=k == KD - 1)
                last.then_inc(gate, 1)
                if n >= 3:
                    pe.wait_ge(mul, n - 2)
                for k in range(2):
                    last = pe.matmul(g.bank[3 + n % 3][:, :], pTt[:, k, t * P:(t + 1) * P], wp[:, k, 512 * h:512 * (h + 1)],
                                     start=k == 0, stop=k == 1)
                last.then_inc(proj, 1)

        @block.scalar
        def _(act):
            for n in range(len(steps)):
                act.wait_ge(gate, n + 1)
                if n >= 2:
                    act.wait_ge(mul, n - 1)
                act.activation(sg[n % 2], g.bank[n % 3][:, :], ACT.Sigmoid).then_inc(sig, 1)

        @block.vector
        def _(dve):
            for k in range(2):
                dve.wait_ge(tp, k + 1)
                dve.tensor_copy(pTt[:, k, :], g.bank[6 + k][:, :]).then_inc(pT, 1)
            for n, (t, h) in enumerate(steps):
                dve.wait_ge(sig, n + 1)
                dve.wait_ge(proj, n + 1)
                if n >= 2:
                    dve.wait_ge(add, n - 1)
                dve.tensor_tensor(pr[n % 2], g.bank[3 + n % 3][:, :], sg[n % 2], ALU.mult).then_inc(mul, 1)
                dve.wait_ge(mul, n + 1)
                xv = g.x[:, t, 512 * h:512 * (h + 1)]
                dve.tensor_tensor(xv, xv, pr[n % 2], ALU.add).then_inc(add, 1)


def stage_final(nc, g, a, out):
    sq, rs, gin = g.sem("final_squares"), g.sem("final_rstd"), g.sem("final_gain_in")
    fin, sent = g.sem("final_rows"), g.sem("final_sent")
    gb = g.big[:, 4096:5120]
    with nc.Block() as block:
        @block.sync
        def _(sp):
            sp.dma_start(gb, a["final_norm_g"].partition_broadcast(P)).then_inc(gin, 16)
            for t in range(T):
                sp.wait_ge(fin, t + 1)
                sp.dma_start(out[0, t * P:(t + 1) * P, :], g.xn[:, t, :]).then_inc(sent, 16)
            sp.wait_ge(sent, 16 * T)

        @block.scalar
        def _(act):
            for t in range(T):
                act.activation(g.xn[:, t, :], g.x[:, t, :], ACT.Square, accum_out=g.ss[:, t:t + 1]).then_inc(sq, 1)
            act.wait_ge(sq, T)
            act.activation(g.lnss[:, :], g.ss[:, :], ACT.Ln, scale=1.0 / D, bias=g.eps[:, 0:1]).then_inc(rs, 1)
            act.wait_ge(rs, 1)
            act.activation(g.rstd[:, :], g.lnss[:, :], ACT.Exp, scale=-0.5).then_inc(rs, 1)

        @block.vector
        def _(dve):
            dve.wait_ge(rs, 2)
            dve.wait_ge(gin, 16)
            for t in range(T):
                dve.scalar_tensor_tensor(out=g.xn[:, t, :], in0=g.x[:, t, :], scalar=g.rstd[:, t:t + 1],
                                         in1=gb, op0=ALU.mult, op1=ALU.mult).then_inc(fin, 1)


HEADS = 16
NOPE, ROPE, VDIM, QL, KVL = 128, 64, 128, 256, 128
QK = NOPE + ROPE
MLA_SCALE = QK ** -0.5
NEG = -1e30


def workspace(g, first, nbufs):
    flat = g.w[:, first:first + nbufs, :].rearrange("p n f -> p (n f)")
    at = [0]

    def take(*shape):
        n = int(np.prod(shape))
        v = flat[:, at[0]:at[0] + n]
        at[0] += n
        assert at[0] <= nbufs * (GU + DN), at[0]
        if len(shape) == 2:
            v = v.rearrange("p (a b) -> p a b", a=shape[0])
        if len(shape) == 3:
            v = v.rearrange("p (a b c) -> p a b c", a=shape[0], b=shape[1])
        return v
    return take


def rope_columns():
    inv = (np.float32(10000.0) ** (-np.arange(0, ROPE, 2, dtype=np.float32) / np.float32(ROPE))).astype(np.float32)
    turns = np.repeat(np.array([0.25, 0.25, 0.5, 0.0], np.float32), 32)
    return np.stack([np.tile(inv, 4), turns, (turns.astype(np.float64) * 2 * np.pi).astype(np.float32)], axis=1)


def mla_memory(nc, g):
    s = Memory()
    take = workspace(g, 2, 2)
    s.wn = take(KD, QL + KVL)
    s.qn = take(T, QL)
    s.cs = take(SEQ)
    s.kdup = take(SEQ)
    s.ckv = take(T, KVL)
    s.ckvT = take(SEQ)
    s.qaT = take(2, SEQ)
    s.neg = take(P)
    s.dup = take(P)
    s.cols = take(4)
    s.gq = take(2)
    take = workspace(g, 1, 1)
    s.wr = take(KD, P)
    s.pos = take(SEQ).bitcast(I32)
    s.gkv = take(KVL)
    s.ang = take(SEQ)
    s.n = take(SEQ)
    h = Memory()
    flat = g.w[:, 2:4, :].rearrange("p n f -> p (n f)")
    at = [0]

    def reuse(*shape):
        n = int(np.prod(shape))
        v = flat[:, at[0]:at[0] + n]
        at[0] += n
        assert at[0] <= KD * (QL + KVL) + T * QL
        return v.rearrange("p (a b) -> p a b", a=shape[0]) if len(shape) == 2 else v
    h.qlatT, h.rot, h.qnT = reuse(SEQ), reuse(SEQ), reuse(SEQ)
    h.p = [reuse((t + 1) * P) for t in range(T)]
    h.wukT = reuse(P)
    take2 = workspace(g, 1, 1)
    h.pT = [take2((T - k) * P) for k in range(T)]
    h.olT = take2(SEQ)
    h.wq = [take2(2, 2 * P) for _ in range(2)]
    h.wkv = [take2(2 * P) for _ in range(2)]
    h.mx, h.nm, h.rs, h.ri = (take2(T) for _ in range(4))
    s.h = h
    return s


def stage_mla_in(nc, g, s, a, w_in):
    tag = "mla_in"
    cst, mm, rs, nat = g.sem(tag + "_consts"), g.sem(tag + "_products"), g.sem(tag + "_rstd"), g.sem(tag + "_natural")
    sq, tp, tpc, tab = g.sem(tag + "_squares"), g.sem(tag + "_transposed"), g.sem(tag + "_taken"), g.sem(tag + "_table")
    kd, ang = g.sem(tag + "_key_dup"), g.sem(tag + "_angles")
    with nc.Block() as block:
        @block.gpsimd
        def _(pool):
            pool.memset(s.neg, 0.0).then_inc(cst, 1)
            pool.memset(s.dup, 0.0).then_inc(cst, 1)
            pool.wait_ge(cst, 2)
            pool.affine_select(out=s.neg, in_=s.neg, compare_op=ALU.is_ge, fill=NEG, base=0, pattern=[[-1, P]],
                               channel_multiplier=1).then_inc(cst, 1)
            for n, base in enumerate((0, 64, -64)):
                pool.wait_ge(cst, 3 + n)
                pool.affine_select(out=s.dup, in_=s.dup, compare_op=ALU.not_equal, fill=1.0, base=base,
                                   pattern=[[-1, P]], channel_multiplier=1).then_inc(cst, 1)

        @block.tensor
        def _(pe):
            pe.wait_ge(w_in, 128)
            for k in range(KD):
                last = pe.matmul(g.bank[4][:, :], s.wr[:, k, :], g.hT[:, k, :], start=k == 0, stop=k == KD - 1)
            last.then_inc(mm, 1)
            for t in range(T):
                for k in range(KD):
                    last = pe.matmul(g.bank[t][:, 0:QL + KVL], g.hT[:, k, t * P:(t + 1) * P], s.wn[:, k, :],
                                     start=k == 0, stop=k == KD - 1)
                last.then_inc(mm, 1)
            pe.wait_ge(kd, 1)
            pe.wait_ge(cst, 6)
            pe.matmul(g.bank[5][:, :], s.dup, s.n, start=True, stop=True).then_inc(mm, 1)
            pe.wait_ge(nat, 2 * T)
            for n in range(3):
                for t in range(T):
                    src = s.qn[:, t, n::2] if n < 2 else s.ckv[:, t, :]
                    if n == 2 and t == 0:
                        pe.wait_ge(tpc, 1)
                    last = pe.transpose(g.bank[(6, 7, 4)[n]][:, t * P:(t + 1) * P], src, g.ident[:, :])
                last.then_inc(tp, 1)

        @block.scalar
        def _(act):
            for t in range(T):
                act.wait_ge(mm, 2 + t)
                act.activation(g.xn[:, t, 0:QL], g.bank[t][:, 0:QL], ACT.Square, accum_out=g.ss[:, t:t + 1]).then_inc(sq, 1)
                act.activation(g.xn[:, t, QL:QL + KVL], g.bank[t][:, QL:QL + KVL], ACT.Square,
                               accum_out=g.lnss[:, t:t + 1]).then_inc(sq, 1)
            act.wait_ge(sq, 2 * T)
            act.activation(g.rstd[:, :], g.ss[:, :], ACT.Ln, scale=1.0 / QL, bias=g.eps[:, 0:1]).then_inc(rs, 1)
            act.activation(g.ss2[:, :], g.lnss[:, :], ACT.Ln, scale=1.0 / KVL, bias=g.eps[:, 0:1]).then_inc(rs, 1)
            act.wait_ge(rs, 2)
            act.activation(g.ss[:, :], g.rstd[:, :], ACT.Exp, scale=-0.5).then_inc(rs, 1)
            act.activation(g.lnss[:, :], g.ss2[:, :], ACT.Exp, scale=-0.5).then_inc(rs, 1)
            act.wait_ge(ang, 10)
            act.activation(s.cs, s.ang, ACT.Sin).then_inc(tab, 1)

        @block.vector
        def _(dve):
            count = [0]

            def done(ins):
                count[0] += 1
                ins.then_inc(ang, 1)
                dve.wait_ge(ang, count[0])

            c1 = 6.28125
            c2 = float(np.float32(np.round((2 * np.pi - c1) * 2 ** 21) / 2 ** 21))
            c3 = 2 * np.pi - c1 - c2
            magic = 1.5 * 2 ** 23
            dve.wait_ge(w_in, 128)
            done(dve.tensor_copy(s.n, s.pos))
            done(dve.tensor_scalar(s.ang, s.n, s.cols[:, 0:1], None, ALU.mult))
            done(dve.tensor_scalar(s.n, s.ang, 1.0 / (2 * np.pi), s.cols[:, 1:2], ALU.mult, ALU.add))
            done(dve.tensor_scalar(s.n, s.n, magic, None, ALU.add))
            done(dve.tensor_scalar(s.n, s.n, -magic, None, ALU.add))
            for c in (c1, c2, c3):
                done(dve.scalar_tensor_tensor(out=s.ang, in0=s.n, scalar=-c, in1=s.ang, op0=ALU.mult, op1=ALU.add))
            done(dve.tensor_scalar(s.ang, s.ang, s.cols[:, 2:3], None, ALU.add))
            done(dve.tensor_scalar(s.ang, s.ang, 3.1415925, -3.1415925, ALU.min, ALU.max))
            dve.wait_ge(tab, 1)
            dve.wait_ge(mm, 1)
            dve.tensor_tensor(s.n, g.bank[4][:, :], s.cs, ALU.mult).then_inc(kd, 1)
            dve.wait_ge(rs, 4)
            for t in range(T):
                dve.tensor_scalar(s.qn[:, t, :], g.bank[t][:, 0:QL], g.ss[:, t:t + 1], None, ALU.mult).then_inc(nat, 1)
                dve.scalar_tensor_tensor(out=s.ckv[:, t, :], in0=g.bank[t][:, QL:QL + KVL], scalar=g.lnss[:, t:t + 1],
                                         in1=s.gkv, op0=ALU.mult, op1=ALU.mult).then_inc(nat, 1)
            dve.wait_ge(mm, 2 + T)
            dve.tensor_copy(s.kdup, g.bank[5][:, :]).then_inc(tpc, 1)
            for n in range(2):
                dve.wait_ge(tp, n + 1)
                dve.tensor_scalar(s.qaT[:, n, :], g.bank[6 + n][:, :], s.gq[:, n:n + 1], None, ALU.mult).then_inc(tpc, 1)
            dve.wait_ge(tp, 3)
            dve.tensor_copy(s.ckvT, g.bank[4][:, :]).then_inc(tpc, 1)


def load_mla_in(sp, s, a, w_in):
    w = a["mla_w_in"][0].rearrange("(p k) n -> p k n", k=KD)
    sp.dma_start(s.wn, w[:, :, 0:QL + KVL]).then_inc(w_in, 16)
    r = QL + KVL
    half = ROPE // 2
    sp.dma_start(s.wr[:, :, 0:ROPE], w[:, :, r:r + ROPE]).then_inc(w_in, 16)
    sp.dma_start(s.wr[:, :, ROPE:ROPE + half], w[:, :, r + half:r + ROPE]).then_inc(w_in, 16)
    sp.dma_start(s.wr[:, :, ROPE + half:], w[:, :, r:r + half]).then_inc(w_in, 16)
    sp.dma_start(s.pos, a["positions"][0].partition_broadcast(P)).then_inc(w_in, 16)
    sp.dma_start(s.gkv, a["mla_kv_norm_g"][0].partition_broadcast(P)).then_inc(w_in, 16)
    sp.dma_start(s.gq, a["mla_q_norm_g"][0].rearrange("(p k) -> p k", k=2)).then_inc(w_in, 16)
    sp.dma_start(s.cols[:, 0:3], a["rope_cols"]).then_inc(w_in, 16)


def stage_mla_heads(nc, g, s, a, sync_work=None):
    h = s.h
    tag = "mla"
    w_in = [g.sem(f"{tag}_w_in{i}") for i in range(2)]
    S = {n: g.sem(f"{tag}_{n}") for n in
         "wuk wukT qn qnT qr rot qlat qlatT sc max nmax exp rinv pn pt pT_dve pT_act ol olT o oT".split()}
    wq_d = a["mla_w_q_up"][0].rearrange("(p k) n -> p k n", k=2)
    oT = g.big[:, :].rearrange("p (h s) -> p h s", h=HEADS)
    half = ROPE // 2
    with nc.Block() as block:
        @block.sync
        def _(sp):
            def load(it, i):
                hd = 2 * it + i
                c0 = QK * hd
                parts = ((0, NOPE, 0), (NOPE, ROPE, NOPE), (NOPE + ROPE, half, NOPE + half), (NOPE + ROPE + half, half, NOPE))
                for to, n, frm in parts:
                    sp.dma_start(h.wq[i][:, :, to:to + n], wq_d[:, :, bass.ds(c0 + frm, n)]).then_inc(w_in[i], 16)
                sp.dma_start(h.wkv[i], a["mla_w_kv_up"][0][:, bass.ds(256 * hd, 256)]).then_inc(w_in[i], 16)
            load(0, 0)
            load(0, 1)
            with sp.Fori(1, HEADS // 2) as it:
                for i in range(2):
                    sp.wait_ge(S["o"], 2 * it + i - 1)
                    load(it, i)
            if sync_work:
                sync_work(sp)

        def is_first(it, i):
            return isinstance(it, int) and it == 0 and i == 0

        @block.tensor
        def _(pe):
            def queries(it, i):
                n = 2 * it + i
                pe.wait_ge(w_in[i], 80 * (it + 1))
                if not is_first(it, i):
                    pe.wait_ge(S["qlatT"], n)
                pe.transpose(g.bank[4][:, 0:P], h.wkv[i][:, 0:NOPE], g.ident[:, :]).then_inc(S["wuk"], 1)
                for k in range(2):
                    last = pe.matmul(g.bank[5][:, :], h.wq[i][:, k, 0:NOPE], s.qaT[:, k, :], start=k == 0, stop=k == 1)
                last.then_inc(S["qn"], 1)
                if not is_first(it, i):
                    pe.wait_ge(S["rot"], n)
                for k in range(2):
                    last = pe.matmul(g.bank[6][:, :], h.wq[i][:, k, NOPE:], s.qaT[:, k, :], start=k == 0, stop=k == 1)
                last.then_inc(S["qr"], 1)
                pe.wait_ge(S["wukT"], n + 1)
                pe.wait_ge(S["qnT"], n + 1)
                pe.matmul(g.bank[4][:, :], h.wukT, h.qnT, start=True, stop=True).then_inc(S["qlat"], 1)

            def scores(it, i):
                n = 2 * it + i
                if not is_first(it, i):
                    pe.wait_ge(S["pT_dve"], 2 * n)
                    pe.wait_ge(S["pT_act"], n)
                    pe.wait_ge(S["olT"], n)
                pe.wait_ge(S["qlatT"], n + 1)
                pe.wait_ge(S["rot"], n + 1)
                for t in range(T):
                    keys, tok = (t + 1) * P, slice(t * P, (t + 1) * P)
                    pe.matmul(g.bank[t][:, 0:keys], h.qlatT[:, tok], s.ckvT[:, 0:keys], start=True, stop=False)
                    pe.matmul(g.bank[t][:, 0:keys], h.rot[:, tok], s.kdup[:, 0:keys], start=False, stop=False)
                    pe.matmul(g.bank[t][:, tok], g.ident[:, :], s.neg, start=False, stop=True).then_inc(S["sc"], 1)

            def values(it, i):
                n = 2 * it + i
                pe.wait_ge(S["pn"], T * (n + 1))
                for k in range(T):
                    b, at = min(k, 2), 0 if k < 3 else 2 * P
                    for t in range(k, T):
                        last = pe.transpose(g.bank[b][:, at + (t - k) * P:at + (t - k + 1) * P],
                                            h.p[t][:, k * P:(k + 1) * P], g.ident[:, :])
                    if k != 2:
                        last.then_inc(S["pt"], 1)
                for k in range(T):
                    if k < 2:
                        pe.wait_ge(S["pT_dve"], 2 * n + k + 1)
                    else:
                        pe.wait_ge(S["pT_act"], n + 1)
                    last = pe.matmul(g.bank[3][:, k * P:], s.ckv[:, k, :], h.pT[k], start=k == 0, stop=k == T - 1)
                last.then_inc(S["ol"], 1)
                if not is_first(it, i):
                    pe.wait_ge(S["oT"], n)
                pe.wait_ge(S["olT"], n + 1)
                pe.matmul(g.bank[7][:, :], h.wkv[i][:, NOPE:], h.olT, start=True, stop=True).then_inc(S["o"], 1)

            queries(0, 0)
            scores(0, 0)
            queries(0, 1)
            values(0, 0)
            with pe.Fori(1, HEADS // 2) as it:
                scores(it - 1, 1)
                queries(it, 0)
                values(it - 1, 1)
                scores(it, 0)
                queries(it, 1)
                values(it, 0)
            scores(HEADS // 2 - 1, 1)
            values(HEADS // 2 - 1, 1)

        @block.vector
        def _(dve):
            def queries(it, i):
                n = 2 * it + i
                dve.wait_ge(S["wuk"], n + 1)
                if not is_first(it, i):
                    dve.wait_ge(S["qlat"], n)
                dve.tensor_copy(h.wukT, g.bank[4][:, 0:P]).then_inc(S["wukT"], 1)
                dve.wait_ge(S["qn"], n + 1)
                dve.tensor_copy(h.qnT, g.bank[5][:, :]).then_inc(S["qnT"], 1)
                dve.wait_ge(S["qr"], n + 1)
                if not is_first(it, i):
                    dve.wait_ge(S["sc"], T * n)
                dve.tensor_tensor(h.rot, g.bank[6][:, :], s.cs, ALU.mult).then_inc(S["rot"], 1)
                dve.wait_ge(S["qlat"], n + 1)
                dve.tensor_copy(h.qlatT, g.bank[4][:, :]).then_inc(S["qlatT"], 1)

            def maxima(it, i):
                n = 2 * it + i
                if not is_first(it, i):
                    dve.wait_ge(S["exp"], T * n)
                for t in range(T):
                    dve.wait_ge(S["sc"], T * n + t + 1)
                    dve.tensor_reduce(h.mx[:, t:t + 1], g.bank[t][:, 0:(t + 1) * P], AX, ALU.max).then_inc(S["max"], 1)
                    dve.wait_ge(S["max"], T * n + t + 1)
                    dve.tensor_scalar(h.nm[:, t:t + 1], h.mx[:, t:t + 1], -MLA_SCALE, None, ALU.mult).then_inc(S["nmax"], 1)

            def normalize(it, i):
                n = 2 * it + i
                for t in range(T):
                    dve.wait_ge(S["exp"], T * n + t + 1)
                    dve.reciprocal(h.ri[:, t:t + 1], h.rs[:, t:t + 1]).then_inc(S["rinv"], 1)
                    dve.wait_ge(S["rinv"], T * n + t + 1)
                    dve.tensor_scalar(h.p[t], h.p[t], h.ri[:, t:t + 1], None, ALU.mult).then_inc(S["pn"], 1)

            def turned(it, i):
                n = 2 * it + i
                if not is_first(it, i):
                    dve.wait_ge(S["ol"], n)
                for k in range(2):
                    dve.wait_ge(S["pt"], 3 * n + k + 1)
                    dve.tensor_copy(h.pT[k], g.bank[k][:, 0:(T - k) * P]).then_inc(S["pT_dve"], 1)

            queries(0, 0)
            maxima(0, 0)
            queries(0, 1)
            normalize(0, 0)
            turned(0, 0)
            with dve.Fori(1, HEADS // 2) as it:
                maxima(it - 1, 1)
                queries(it, 0)
                normalize(it - 1, 1)
                turned(it - 1, 1)
                maxima(it, 0)
                queries(it, 1)
                normalize(it, 0)
                turned(it, 0)
            maxima(HEADS // 2 - 1, 1)
            normalize(HEADS // 2 - 1, 1)
            turned(HEADS // 2 - 1, 1)

        @block.scalar
        def _(act):
            def head(it, i):
                n = 2 * it + i
                if not is_first(it, i):
                    act.wait_ge(S["pt"], 3 * n)
                for t in range(T):
                    act.wait_ge(S["nmax"], T * n + t + 1)
                    act.activation(h.p[t], g.bank[t][:, 0:(t + 1) * P], ACT.Exp, bias=h.nm[:, t:t + 1], scale=MLA_SCALE,
                                   accum_out=h.rs[:, t:t + 1]).then_inc(S["exp"], 1)
                act.wait_ge(S["pt"], 3 * n + 3)
                for k in (2, 3):
                    at = 0 if k == 2 else 2 * P
                    if not is_first(it, i):
                        act.wait_ge(S["ol"], n)
                    last = act.activation(h.pT[k], g.bank[2][:, at:at + (T - k) * P], ACT.Copy)
                last.then_inc(S["pT_act"], 1)
                act.wait_ge(S["ol"], n + 1)
                if not is_first(it, i):
                    act.wait_ge(S["o"], n)
                act.activation(h.olT, g.bank[3][:, :], ACT.Copy).then_inc(S["olT"], 1)
                act.wait_ge(S["o"], n + 1)
                act.activation(oT[:, bass.ds(n, 1), :], g.bank[7][:, :].unsqueeze(1), ACT.Copy).then_inc(S["oT"], 1)
            head(0, 0)
            head(0, 1)
            with act.Fori(1, HEADS // 2) as it:
                head(it, 0)
                head(it, 1)


def stage_out(nc, g, tag, w_dram, sync_work=None):
    NS = 12
    slots = g.w[:, 2:4, :].rearrange("p n (s d) -> p (n s) d", d=D)
    w_in = [g.sem(f"{tag}_w_in{i}") for i in range(NS)]
    used, mm, add = g.sem(tag + "_w_used"), g.sem(tag + "_products"), g.sem(tag + "_added")
    oT = g.big[:, :].rearrange("p (h s) -> p h s", h=HEADS)
    with nc.Block() as block:
        @block.sync
        def _(sp):
            for k in range(HEADS):
                if k >= NS:
                    sp.wait_ge(used, k - NS + 1)
                sp.dma_start(slots[:, k % NS, :], w_dram[k * P:(k + 1) * P, :]).then_inc(w_in[k % NS], 16)
            if sync_work:
                sync_work(sp)

        @block.tensor
        def _(pe):
            for k in range(HEADS):
                pe.wait_ge(w_in[k % NS], 16 * (k // NS + 1))
                for t in range(T):
                    for n in range(2):
                        last = pe.matmul(g.bank[2 * t + n][:, :], oT[:, k, t * P:(t + 1) * P],
                                         slots[:, k % NS, 512 * n:512 * (n + 1)], start=k == 0, stop=k == HEADS - 1)
                        if k == HEADS - 1:
                            last.then_inc(mm, 1)
                if k < HEADS - 1:
                    last.then_inc(used, 1)

        @block.vector
        def _(dve):
            for b in range(2 * T):
                dve.wait_ge(mm, b + 1)
                xv = g.x[:, b // 2, 512 * (b % 2):512 * (b % 2) + 512]
                dve.tensor_tensor(xv, g.bank[b][:, :], xv, ALU.add).then_inc(add, 1)



K_HEADS, V_HEADS = 8, 16
CONV = 4
QKW, VW = K_HEADS * P, V_HEADS * P
LEVELS = 7
BETA, NBETA, G, GLOG, BEG = range(5)
(PQ, PK, PV0, PV1, PZ0, PZ1) = range(6)


def gdn_memory(nc, ctx, g):
    s = Memory()
    parts = [workspace(g, 0, 1), workspace(g, 2, 2)]
    left = [GU + DN, 2 * (GU + DN)]

    def tile():
        i = 0 if left[0] >= SEQ else 1
        left[i] -= SEQ
        return parts[i](T, P)
    s.c = [tile() for _ in range(4)]
    s.zn = [tile() for _ in range(2)]
    s.zw = [tile() for _ in range(2)]
    s.qT, s.kT, s.kn = tile(), tile(), tile()
    s.vb, s.kbg, s.kout, s.E, s.eG, s.QKT, s.qin, s.A, s.TT, s.W, s.vn = (
        [tile() for _ in range(2)] for _ in range(11))
    s.Tm = s.eG
    s.Wc = [w.rearrange("p t i -> p (t i)")[:, 0:T * P // 2].rearrange("p (t i) -> p t i", t=T) for w in s.W]
    w = workspace(g, 1, 1)
    s.wq, s.wk, s.wv, s.wz = w(KD, P), w(KD, P), w(KD, 2 * P), w(KD, 2 * P)

    def sb(name, *shape):
        return ctx.enter_context(nc.sbuf_tensor(name, [P, *shape], F32))
    s.tab = sb("gdn_tab", V_HEADS, 5, T)
    s.st = sb("gdn_tab_now", 2, 5, T)
    s.cw = sb("gdn_conv_w", 32, CONV)
    s.cws = sb("gdn_conv_w_now", 4, CONV)
    s.S = [sb(f"gdn_state{i}", P) for i in range(2)]
    s.ge = [sb(f"gdn_end_decay{i}", T) for i in range(2)]
    s.gcol = sb("gdn_gain", 1)
    s.lm = sb("level_masks", LEVELS, P // 2)
    f = g.big[:, 4096:8192]
    s.gates_in = g.sem("gates_in")
    s.w_in = [g.sem(f"gd_w_in{i}") for i in range(4)]
    s.wba, s.cwr = f[:, 0:256].rearrange("p (k n) -> p k n", k=KD), f[:, 256:384]
    s.dt, s.al = f[:, 384:400], f[:, 400:416]
    s.xa, s.ab, s.sp, s.gl = (f[:, 512 + 64 * i:576 + 64 * i].rearrange("p (t h) -> p t h", t=T) for i in range(4))
    s.bt, s.Gc, s.eGc = (f[:, 768 + 64 * i:832 + 64 * i].rearrange("p (t h) -> p t h", t=T) for i in range(3))
    return s


def load_gates(sp, s, a):
    w_in = s.gates_in
    w = a["gdn_w_in"][0].rearrange("(p k) n -> p k n", k=KD)
    sp.dma_start(s.wba, w[:, :, 2 * QKW + 2 * VW:]).then_inc(w_in, 16)
    sp.dma_start(s.cwr, a["gdn_conv_w"][0].rearrange("c (n p) -> (c n) p", p=P)).then_inc(w_in, 16)
    sp.dma_start(s.dt, a["gdn_dt_bias"][0].partition_broadcast(P)).then_inc(w_in, 16)
    sp.dma_start(s.al, a["gdn_a_log"][0].partition_broadcast(P)).then_inc(w_in, 16)
    sp.dma_start(s.gcol[:, :], a["gdn_norm_g"][0].rearrange("(p o) -> p o", o=1)).then_inc(w_in, 16)


def load_delta(sp, s, a, part, kh):
    w_d = a["gdn_w_in"][0].rearrange("(p k) n -> p k n", k=KD)
    dst, base, n = ((s.wq, 0, P), (s.wk, QKW, P), (s.wv, 2 * QKW, 2 * P), (s.wz, 2 * QKW + VW, 2 * P))[part]
    sp.dma_start(dst, w_d[:, :, bass.ds(base + n * kh, n)]).then_inc(s.w_in[part], 16)


def gates_programs(nc, g, s):
    tag = "gates"
    proj, act_s, dve_s, run = g.sem(tag + "_products"), g.sem(tag + "_act"), g.sem(tag + "_dve"), g.sem(tag + "_sums")
    lm = g.sem(tag + "_masks")
    ba = g.bank[5][:, 0:128].rearrange("p (t c h) -> p t c h", t=T, c=2)

    def masks(pool):
        pool.memset(s.lm[:, :, :], 1.0).then_inc(lm, 1)
        for lv in range(LEVELS):
            b = 1 << lv
            mask = s.lm[:, lv, :].rearrange("p (n c) -> p n c", c=b)
            pairs = P // (2 * b)
            pool.wait_ge(lm, 2 * lv + 1)
            pool.affine_select(out=mask, in_=mask, compare_op=ALU.is_ge, fill=0.0, base=0,
                               pattern=[[-2 * b, pairs], [0, b]], channel_multiplier=1).then_inc(lm, 1)
            pool.wait_ge(lm, 2 * lv + 2)
            pool.affine_select(out=mask, in_=mask, compare_op=ALU.is_ge, fill=0.0, base=b - 1,
                               pattern=[[2 * b, pairs], [0, b]], channel_multiplier=-1).then_inc(lm, 1)

    def products(pe):
        pe.wait_ge(s.gates_in, 80)
        for t in range(T):
            for k in range(KD):
                last = pe.matmul(g.bank[5][:, 32 * t:32 * t + 32], g.hT[:, k, t * P:(t + 1) * P], s.wba[:, k, :],
                                 start=k == 0, stop=k == KD - 1)
        last.then_inc(proj, 1)
        pe.transpose(g.bank[6][:, 0:P], s.cwr, g.ident[:, :]).then_inc(proj, 1)

    def running_sums(pe):
        pe.wait_ge(dve_s, 4)
        pe.matmul(g.bank[7][:, 0:T * V_HEADS], g.tri[:, :], s.gl.rearrange("p t h -> p (t h)"),
                  start=True, stop=True).then_inc(proj, 1)

    def scalar_part(act):
        act.wait_ge(proj, 1)
        act.activation(s.bt, ba[:, :, 0, :], ACT.Sigmoid).then_inc(act_s, 1)
        act.activation(s.al, s.al, ACT.Exp).then_inc(act_s, 1)
        act.wait_ge(dve_s, 1)
        act.activation(s.ab, s.xa, ACT.Abs).then_inc(act_s, 1)
        act.wait_ge(act_s, 3)
        act.activation(s.sp, s.ab, ACT.Exp, scale=-1.0).then_inc(act_s, 1)
        act.wait_ge(act_s, 4)
        act.activation(s.sp, s.sp, ACT.Ln, bias=g.ones[:, 0:1]).then_inc(act_s, 1)

    def scalar_end(act):
        act.wait_ge(dve_s, 6)
        act.activation(s.eGc, s.Gc, ACT.Exp).then_inc(act_s, 1)

    count = [0]

    def done(dve, ins):
        count[0] += 1
        ins.then_inc(dve_s, 1)
        dve.wait_ge(dve_s, count[0])

    def vector_part(dve):
        def bc(v):
            return v.unsqueeze(1).to_broadcast([P, T, V_HEADS])
        dve.wait_ge(s.gates_in, 80)
        dve.wait_ge(act_s, 1)
        done(dve, dve.tensor_tensor(s.xa, ba[:, :, 1, :], bc(s.dt), ALU.add))
        dve.wait_ge(act_s, 5)
        done(dve, dve.scalar_tensor_tensor(out=s.gl, in0=s.xa, scalar=0.0, in1=s.sp, op0=ALU.max, op1=ALU.add))
        done(dve, dve.tensor_tensor(s.gl, s.gl, bc(s.al), ALU.mult))
        done(dve, dve.tensor_scalar(s.gl, s.gl, -1.0, None, ALU.mult))
        dve.wait_ge(proj, 2)
        done(dve, dve.tensor_copy(s.cw[:, :, :], g.bank[6][:, 0:P].rearrange("p (c n) -> p n c", c=CONV)))

    def vector_end(dve):
        dve.wait_ge(proj, 3)
        done(dve, dve.tensor_copy(s.Gc, g.bank[7][:, 0:T * V_HEADS].rearrange("p (t h) -> p t h", t=T)))
        dve.wait_ge(act_s, 6)

        def put(n, v):
            return dve.tensor_copy(s.tab[:, :, n, :], v.rearrange("p t h -> p h t"))
        done(dve, put(BETA, s.bt))
        done(dve, put(G, s.Gc))
        done(dve, put(GLOG, s.gl))
        done(dve, dve.tensor_scalar(s.tab[:, :, NBETA, :], s.tab[:, :, BETA, :], -1.0, None, ALU.mult))
        done(dve, dve.tensor_tensor(s.tab[:, :, BEG, :], s.bt.rearrange("p t h -> p h t"),
                               s.eGc.rearrange("p t h -> p h t"), ALU.mult))
        dve.wait_ge(lm, 2 * LEVELS + 1)

    programs = Memory()
    programs.masks, programs.products, programs.running_sums = masks, products, running_sums
    programs.scalar_part, programs.scalar_end = scalar_part, scalar_end
    programs.vector_part, programs.vector_end = vector_part, vector_end
    return programs


def stage_delta(nc, g, s, a):
    S = {n: g.sem("gd_" + n) for n in
         ("squares norms_sum norms qk v_turned tables decay_rhs decay_bc v_beta decay_diff exp_diff exp_G k_turned kk kq "
          "k_nat k_beta k_out A_raw A QKT_raw QKT q_in end_decay z_now TT_is_I TT first_product W YT T_turned T "
          "w_product w_neg v_product v_new o state_product state o_squares o_sums o_rstd o_normed o_gated "
          "projected conv_step silu z_next conv_w").split()}
    gates = gates_programs(nc, g, s)
    w_in = s.w_in
    oT = g.big[:, :].rearrange("p (h t i) -> p h t i", h=V_HEADS, t=T)
    bank = [b[:, :].rearrange("p (t i) -> p t i", t=T) for b in g.bank]
    LAST = K_HEADS - 1

    def wait(eng, name, per, it, n):
        eng.wait_ge(S[name], per * it + n)

    def first(it):
        return isinstance(it, int) and it == 0

    def cols(v):
        return v.unsqueeze(2).to_broadcast([P, T, P])

    def rows(v):
        return v.unsqueeze(1).to_broadcast([P, T, P])

    def rows2(v):
        return v.unsqueeze(1).to_broadcast([P, T, P // 2])

    def weights(tile):
        return (s.wq[:, :, :], s.wk[:, :, :], s.wv[:, :, 0:P], s.wv[:, :, P:], s.wz[:, :, 0:P], s.wz[:, :, P:])[tile]

    def odd(v, lv, t=slice(None)):
        return v[:, t, :].rearrange("p t (n h c) -> p t n h c" if isinstance(t, slice) else "p (n h c) -> p n h c",
                                    h=2, c=1 << lv)[..., 1, :]

    def blocks_of(v, lv):
        return v.rearrange("p t (n c) -> p t n c", c=1 << lv)

    FILL = [4, 4, 2, 2] + [3] * (2 * LEVELS - 2)
    assert sum(FILL) == 6 * KD
    with nc.Block() as block:
        @block.sync
        def _(sp):
            with sp.Fori(1, K_HEADS) as kh:
                for part, used in enumerate((1, 2, 4, 6)):
                    sp.wait_ge(S["projected"], 6 * (kh - 1) + used)
                    load_delta(sp, s, a, part, kh)

        @block.tensor
        def _(pe):
            def project(n, tile, ks):
                if 0 in ks:
                    pe.wait_ge(w_in[(0, 1, 2, 2, 3, 3)[tile]], 16 * (n + 1))
                    if tile >= 2:
                        wait(pe, "conv_step", 16, n, 4 * (tile - 1))
                    elif not first(n):
                        wait(pe, "z_next", 2, n - 1, tile + 1)
                for k in ks:
                    last = pe.matmul(g.bank[tile % 2][:, :], weights(tile)[:, k, :], g.hT[:, k, :],
                                     start=k == 0, stop=k == KD - 1)
                if KD - 1 in ks:
                    last.then_inc(S["projected"], 1)

            def each(out, lhs, rhs, transposed=False):
                for t in range(T):
                    if transposed:
                        last = pe.transpose(out[:, t, :], lhs[:, t, :], g.ident[:, :])
                    else:
                        last = pe.matmul(out[:, t, :], lhs[:, t, :], rhs[:, t, :], start=True, stop=True)
                return last

            def flat(v):
                return v.rearrange("p t i -> p (t i)")

            def norms_sums(n):
                for i in range(2):
                    wait(pe, "squares", 2, n, i + 1)
                    if not first(n):
                        wait(pe, "state", 6, n - 1, 5 + i)
                    pe.matmul(g.bank[5 + 2 * i][:, :], g.ones[:, :], flat(s.E[i]), start=True, stop=True)\
                        .then_inc(S["norms_sum"], 1)

            def head_pair(it, more):
                n = it + 1

                def fill(slot):
                    if more:
                        for step in range(sum(FILL[:slot]), sum(FILL[:slot + 1])):
                            project(n, step // KD, (step % KD,))

                fill(0)
                for i in range(2):
                    wait(pe, "silu", 4, it, 3 + i)
                    if not first(it):
                        wait(pe, "o_rstd", 4, it - 1, 2)
                    each(bank[2 + i], s.c[2 + i], None, True).then_inc(S["v_turned"], 1)
                for i in range(2):
                    wait(pe, "decay_rhs", 2, it, i + 1)
                    wait(pe, "norms", 4, it, i + 1)
                    pe.matmul(g.bank[5 + 2 * i][:, :], g.ones[:, :], flat(s.W[i]), start=True, stop=True)\
                        .then_inc(S["decay_bc"], 1)
                wait(pe, "qk", 2, it, 2)
                if not first(it):
                    wait(pe, "o_normed", 2, it - 1, 2)
                each(bank[4], s.kT, None, True).then_inc(S["k_turned"], 1)
                each(bank[6], s.kT, s.kT).then_inc(S["kk"], 1)
                wait(pe, "v_beta", 2, it, 1)
                each(bank[2], s.kT, s.qT).then_inc(S["kq"], 1)
                fill(1)
                for lv in range(LEVELS):
                    for i in range(2):
                        wait(pe, "TT", 14, it, 2 * (lv - 1) + i + 1) if lv else wait(pe, "TT_is_I", 2, it, i + 1)
                        if lv == 0:
                            wait(pe, "A", 2, it, i + 1)
                            if i == 0:
                                wait(pe, "QKT_raw", 2, it, 2)
                            else:
                                wait(pe, "v_beta", 2, it, 2)
                        else:
                            if lv == 1:
                                wait(pe, "exp_G", 2, it, 2)
                                wait(pe, "k_nat", 1, it, 1)
                            else:
                                wait(pe, "T", 12, it, 2 * (lv - 2) + i + 1)
                            each(bank[4 + 2 * i], s.TT[i], None, True).then_inc(S["T_turned"], 1)
                            wait(pe, "W", 14, it, 2 * (lv - 1) + i + 1)
                        for t in range(T):
                            last = pe.matmul(g.bank[2 + i][:, 64 * t:64 * (t + 1)].rearrange("p (n c) -> p n c", c=1 << lv),
                                             s.A[i][:, t, :], odd(s.TT[i], lv, t), start=True, stop=True)
                        last.then_inc(S["first_product"], 1)
                    fill(2 + 2 * lv)
                    if lv:
                        for i in range(2):
                            wait(pe, "W", 14, it, 2 * lv + i + 1)
                            wait(pe, "T", 12, it, 2 * (lv - 1) + i + 1)
                            for t in range(T):
                                last = pe.matmul(g.bank[5 + 2 * i][:, 64 * t:64 * (t + 1)], s.Tm[i][:, t, :],
                                                 s.Wc[i][:, t, :], start=True, stop=True)
                            last.then_inc(S["YT"], 1)
                    fill(3 + 2 * lv)
                for i in range(2):
                    wait(pe, "TT", 14, it, 2 * (LEVELS - 1) + i + 1)
                    wait(pe, "k_beta", 2, it, i + 1)
                    each(bank[2 + i], s.kbg[i], s.TT[i]).then_inc(S["w_product"], 1)
                for c in range(T):
                    for i in range(2):
                        if c == 0:
                            wait(pe, "w_neg", 2, it, i + 1)
                        else:
                            wait(pe, "v_new", 8, it, 2 * (c - 1) + i + 1)
                        last = pe.matmul(bank[2 + i][:, c, :], s.TT[i][:, c, :], s.vb[i][:, c, :], start=True, stop=c == 0)
                        if c > 0:
                            wait(pe, "state", 6, it, 2 * (c - 1) + i + 1)
                            last = pe.matmul(bank[2 + i][:, c, :], s.W[i][:, c, :], s.S[i][:, :], start=False, stop=True)
                        last.then_inc(S["v_product"], 1)
                    for i in range(2):
                        if c == 0:
                            wait(pe, "q_in", 2, it, i + 1)
                            wait(pe, "QKT", 2, it, i + 1)
                            wait(pe, "k_out", 2, it, i + 1)
                            wait(pe, "T", 12, it, 10 + i + 1)
                        if c > 0:
                            pe.matmul(bank[4 + 2 * i][:, c, :], s.S[i][:, :], s.qin[i][:, c, :], start=True, stop=False)
                        wait(pe, "v_new", 8, it, 2 * c + i + 1)
                        pe.matmul(bank[4 + 2 * i][:, c, :], s.vn[i][:, c, :], s.QKT[i][:, c, :], start=c == 0, stop=True)\
                            .then_inc(S["o"], 1)
                        if c < T - 1:
                            pe.matmul(bank[5 + 2 * i][:, 0, :], s.kout[i][:, c, :], s.vn[i][:, c, :], start=True, stop=True)\
                                .then_inc(S["state_product"], 1)
                if more:
                    norms_sums(n)
                for i in range(2):
                    wait(pe, "o_squares", 2, it, i + 1)
                    wait(pe, "v_new", 8, it, 7 + i)
                    pe.matmul(g.bank[2 + i][:, :], g.ones[:, :], flat(s.W[i]), start=True, stop=True)\
                        .then_inc(S["o_sums"], 1)

            gates.products(pe)
            project(0, 0, range(KD))
            gates.running_sums(pe)
            for tile in range(1, 6):
                project(0, tile, range(KD))
            norms_sums(0)
            head_pair(0, True)
            with pe.Fori(1, LAST) as it:
                head_pair(it, True)
            head_pair(LAST, False)

        @block.vector
        def _(dve):
            def conv(n, tile):
                c = s.c[tile].rearrange("p t i -> p (t i)")
                wait(dve, "projected", 6, n, tile + 1)
                if tile == 0:
                    wait(dve, "conv_w", 3, n, 3)
                if not first(n):
                    if tile < 2:
                        wait(dve, "squares", 2, n - 1, tile + 1)
                        wait(dve, "qk", 2, n - 1, tile + 1)
                    else:
                        wait(dve, "v_turned", 2, n - 1, tile - 1)
                src, cw = g.bank[tile % 2], s.cws[:, tile, :]
                dve.tensor_scalar(c, src[:, :], cw[:, CONV - 1:CONV], None, ALU.mult).then_inc(S["conv_step"], 1)
                for lag in range(1, CONV):
                    wait(dve, "conv_step", 16, n, 4 * tile + lag)
                    dve.scalar_tensor_tensor(out=c[:, lag:], in0=src[:, 0:SEQ - lag], scalar=cw[:, CONV - 1 - lag:CONV - lag],
                                             in1=c[:, lag:], op0=ALU.mult, op1=ALU.add).then_inc(S["conv_step"], 1)

            def conv_weights(n):
                if not first(n):
                    wait(dve, "conv_step", 16, n - 1, 16)
                dve.tensor_copy(s.cws[:, 0:1, :], s.cw[:, bass.ds(n, 1), :]).then_inc(S["conv_w"], 1)
                dve.tensor_copy(s.cws[:, 1:2, :], s.cw[:, bass.ds(K_HEADS + n, 1), :]).then_inc(S["conv_w"], 1)
                dve.tensor_copy(s.cws[:, 2:4, :], s.cw[:, bass.ds(2 * K_HEADS + 2 * n, 2), :]).then_inc(S["conv_w"], 1)

            def tables(n):
                if not first(n):
                    wait(dve, "k_beta", 2, n - 1, 2)
                    wait(dve, "decay_rhs", 2, n - 1, 2)
                dve.tensor_copy(s.st[:, :, :, :], s.tab[:, bass.ds(2 * n, 2), :, :]).then_inc(S["tables"], 1)

            def head_pair(it, more):
                n = it + 1
                if more:
                    conv_weights(n)
                wait(dve, "tables", 1, it, 1)
                for i in range(2):
                    wait(dve, "v_turned", 2, it, i + 1)
                    dve.tensor_tensor(s.vb[i], bank[2 + i], cols(s.st[:, i, BETA, :]), ALU.mult).then_inc(S["v_beta"], 1)
                wait(dve, "norms", 4, it, 4)
                dve.scalar_tensor_tensor(out=s.qT.rearrange("p t i -> p (t i)"), in0=s.c[PQ].rearrange("p t i -> p (t i)"),
                                         scalar=float(P) ** -0.5, in1=s.eG[0].rearrange("p t i -> p (t i)"),
                                         op0=ALU.mult, op1=ALU.mult).then_inc(S["qk"], 1)
                dve.tensor_tensor(s.kT, s.c[PK], s.eG[1], ALU.mult).then_inc(S["qk"], 1)
                for i in range(2):
                    wait(dve, "decay_bc", 2, it, i + 1)
                    wait(dve, "norms_sum", 2, it, i + 1)
                    dve.tensor_tensor(s.E[i], bank[5 + 2 * i], cols(s.st[:, i, G, :]), ALU.subtract)\
                        .then_inc(S["decay_diff"], 1)
                wait(dve, "k_turned", 1, it, 1)
                if not first(it):
                    wait(dve, "k_out", 2, it - 1, 2)
                dve.tensor_copy(s.kn, bank[4]).then_inc(S["k_nat"], 1)
                for i in range(2):
                    wait(dve, "kk", 1, it, 1)
                    wait(dve, "exp_diff", 4, it, 2 * i + 2)
                    dve.tensor_tensor(s.A[i], bank[6], s.E[i], ALU.mult).then_inc(S["A_raw"], 1)
                for i in range(2):
                    wait(dve, "kq", 1, it, 1)
                    if not first(it):
                        wait(dve, "o", 8, it - 1, 7 + i)
                    dve.tensor_tensor(s.QKT[i], bank[2], s.E[i], ALU.mult).then_inc(S["QKT_raw"], 1)
                    wait(dve, "A_raw", 2, it, i + 1)
                    dve.tensor_tensor(s.A[i], s.A[i], cols(s.st[:, i, NBETA, :]), ALU.mult).then_inc(S["A"], 1)
                for lv in range(LEVELS):
                    for i in range(2):
                        wait(dve, "first_product", 14, it, 2 * lv + i + 1)
                        dve.tensor_tensor(s.Wc[i], g.bank[2 + i][:, 0:256].rearrange("p (t i) -> p t i", t=T),
                                          rows2(s.lm[:, lv, :]), ALU.mult).then_inc(S["W"], 1)
                    if more and lv in (1, 2, 3, 5):
                        conv(n, (1, 2, 3, 5).index(lv))
                    for i in range(2):
                        if lv == 0:
                            wait(dve, "W", 14, it, i + 1)
                            step = blocks_of(s.Wc[i], lv)
                        else:
                            wait(dve, "YT", 12, it, 2 * (lv - 1) + i + 1)
                            wait(dve, "TT", 14, it, 2 * (lv - 1) + i + 1)
                            step = blocks_of(g.bank[5 + 2 * i][:, 0:256].rearrange("p (t i) -> p t i", t=T), lv)
                        dve.tensor_tensor(odd(s.TT[i], lv), step, odd(s.TT[i], lv), ALU.add).then_inc(S["TT"], 1)
                for c in range(T - 1):
                    for i in range(2):
                        wait(dve, "state_product", 6, it, 2 * c + i + 1)
                        if c == 0:
                            dve.tensor_copy(s.S[i][:, :], bank[5 + 2 * i][:, 0, :]).then_inc(S["state"], 1)
                        else:
                            wait(dve, "state", 6, it, 2 * (c - 1) + i + 1)
                            wait(dve, "end_decay", 2, it, i + 1)
                            dve.scalar_tensor_tensor(out=s.S[i][:, :], in0=s.S[i][:, :], scalar=s.ge[i][:, c:c + 1],
                                                     in1=bank[5 + 2 * i][:, 0, :], op0=ALU.mult, op1=ALU.add)\
                                .then_inc(S["state"], 1)
                if more:
                    tables(n)
                for i in range(2):
                    wait(dve, "o_rstd", 4, it, i + 3)
                    dve.scalar_tensor_tensor(out=s.vn[i].rearrange("p t i -> p (t i)"), in0=g.bank[4 + 2 * i][:, :],
                                             scalar=s.gcol[:, 0:1], in1=s.A[i].rearrange("p t i -> p (t i)"),
                                             op0=ALU.mult, op1=ALU.mult).then_inc(S["o_normed"], 1)
                    wait(dve, "o_normed", 2, it, i + 1)
                    wait(dve, "z_now", 2, it, i + 1)
                    dve.tensor_tensor(oT[:, bass.ds(2 * it + i, 1)], s.vn[i].unsqueeze(1), s.zw[i].unsqueeze(1), ALU.mult)\
                        .then_inc(S["o_gated"], 1)

            gates.vector_part(dve)
            conv_weights(0)
            conv(0, 0)
            gates.vector_end(dve)
            for tile in range(1, 4):
                conv(0, tile)
            tables(0)
            head_pair(0, True)
            with dve.Fori(1, LAST) as it:
                head_pair(it, True)
            head_pair(LAST, False)

        @block.scalar
        def _(act):
            def silu_conv(n, tile):
                wait(act, "conv_step", 16, n, 4 * tile + 4)
                act.activation(s.c[tile], s.c[tile], ACT.Silu).then_inc(S["silu"], 1)

            def squares(n):
                for i in range(2):
                    wait(act, "silu", 4, n, i + 1)
                    if not first(n):
                        wait(act, "QKT_raw", 2, n - 1, i + 1)
                        wait(act, "k_out", 2, n - 1, i + 1)
                    act.activation(s.E[i], s.c[i], ACT.Square).then_inc(S["squares"], 1)

            def silu_z(n, i):
                wait(act, "projected", 6, n, 5 + i)
                if not first(n):
                    wait(act, "z_now", 2, n - 1, i + 1)
                act.activation(s.zn[i], bank[i], ACT.Silu).then_inc(S["z_next"], 1)

            def norms_ln(n):
                for i in range(2):
                    wait(act, "norms_sum", 2, n, i + 1)
                    if not first(n):
                        wait(act, "YT", 12, n - 1, 11 + i)
                    act.activation(s.eG[i], bank[5 + 2 * i], ACT.Ln, bias=g.eps[:, 0:1]).then_inc(S["norms"], 1)

            def norms_exp(n):
                for i in range(2):
                    wait(act, "norms", 4, n, i + 1)
                    act.activation(s.eG[i], s.eG[i], ACT.Exp, scale=-0.5).then_inc(S["norms"], 1)

            def head_pair(it, more):
                n = it + 1
                for i in range(2):
                    wait(act, "decay_diff", 2, it, i + 1)
                    act.activation(s.E[i], s.E[i], ACT.Abs).then_inc(S["exp_diff"], 1)
                    wait(act, "exp_diff", 4, it, 2 * i + 1)
                    act.activation(s.E[i], s.E[i], ACT.Exp, scale=-1.0).then_inc(S["exp_diff"], 1)
                    wait(act, "qk", 2, it, 2)
                    act.activation(s.eG[i], bank[5 + 2 * i], ACT.Exp).then_inc(S["exp_G"], 1)
                for lv in range(1, LEVELS):
                    for i in range(2):
                        wait(act, "T_turned", 12, it, 2 * (lv - 1) + i + 1)
                        if lv == 1:
                            wait(act, "q_in", 2, it, i + 1)
                            wait(act, "end_decay", 2, it, i + 1)
                        else:
                            wait(act, "YT", 12, it, 2 * (lv - 2) + i + 1)
                        act.activation(s.Tm[i], bank[4 + 2 * i], ACT.Copy).then_inc(S["T"], 1)
                    if more and lv in (2, 3, 4, 6):
                        silu_conv(n, (2, 3, 4, 6).index(lv))
                    if more and lv == 6:
                        silu_z(n, 0)
                if more:
                    silu_z(n, 1)
                    squares(n)
                for i in range(2):
                    wait(act, "w_product", 2, it, i + 1)
                    act.activation(s.W[i], bank[2 + i], ACT.Copy, scale=-1.0).then_inc(S["w_neg"], 1)
                for c in range(T):
                    for i in range(2):
                        wait(act, "v_product", 8, it, 2 * c + i + 1)
                        if c == 0 and not first(it):
                            wait(act, "o_gated", 2, it - 1, i + 1)
                        act.activation(s.vn[i][:, c, :], bank[2 + i][:, c, :], ACT.Copy).then_inc(S["v_new"], 1)
                for i in range(2):
                    wait(act, "o", 8, it, 7 + i)
                    act.activation(s.W[i], bank[4 + 2 * i], ACT.Square).then_inc(S["o_squares"], 1)
                for i in range(2):
                    wait(act, "o_sums", 2, it, i + 1)
                    act.activation(s.A[i], bank[2 + i], ACT.Ln, scale=1.0 / P, bias=g.eps[:, 0:1]).then_inc(S["o_rstd"], 1)
                if more:
                    norms_ln(n)
                for i in range(2):
                    wait(act, "o_rstd", 4, it, i + 1)
                    act.activation(s.A[i], s.A[i], ACT.Exp, scale=-0.5).then_inc(S["o_rstd"], 1)
                if more:
                    norms_exp(n)

            gates.scalar_part(act)
            gates.scalar_end(act)
            for tile in range(4):
                silu_conv(0, tile)
            for i in range(2):
                silu_z(0, i)
            squares(0)
            norms_ln(0)
            norms_exp(0)
            head_pair(0, True)
            with act.Fori(1, LAST) as it:
                head_pair(it, True)
            head_pair(LAST, False)

        @block.gpsimd
        def _(pool):
            def head_pair(it):
                for i in range(2):
                    wait(pool, "tables", 1, it, 1)
                    if not first(it):
                        wait(pool, "o_sums", 2, it - 1, i + 1)
                    pool.tensor_tensor(s.W[i], rows(g.tri[:, :]), cols(s.st[:, i, GLOG, :]), ALU.mult)\
                        .then_inc(S["decay_rhs"], 1)
                for i in range(2):
                    if not first(it):
                        wait(pool, "v_product", 8, it - 1, 7 + i)
                    pool.tensor_tensor(s.TT[i], rows(g.ident[:, :]), rows(g.ones[:, :]), ALU.mult).then_inc(S["TT_is_I"], 1)
                for i in range(2):
                    wait(pool, "exp_G", 2, it, i + 1)
                    wait(pool, "qk", 2, it, 1)
                    pool.tensor_tensor(s.qin[i], s.qT, s.eG[i], ALU.mult).then_inc(S["q_in"], 1)
                    pool.tensor_copy(s.ge[i][:, :], s.eG[i][:, :, P - 1]).then_inc(S["end_decay"], 1)
                for i in range(2):
                    if not first(it):
                        wait(pool, "w_product", 2, it - 1, i + 1)
                    wait(pool, "k_nat", 1, it, 1)
                    wait(pool, "exp_diff", 4, it, 2 * i + 2)
                    pool.tensor_tensor(s.kout[i], s.kn, s.E[i][:, :, P - 1:P].to_broadcast([P, T, P]), ALU.mult)\
                        .then_inc(S["k_out"], 1)
                for i in range(2):
                    wait(pool, "z_next", 2, it, i + 1)
                    if not first(it):
                        wait(pool, "o_gated", 2, it - 1, i + 1)
                    pool.tensor_tensor(s.zw[i], s.zn[i], rows(g.ones[:, :]), ALU.mult).then_inc(S["z_now"], 1)
                for i in range(2):
                    wait(pool, "QKT_raw", 2, it, i + 1)
                    pool.tensor_tensor(s.QKT[i], s.QKT[i], rows(g.tri[:, :]), ALU.mult).then_inc(S["QKT"], 1)
                    pool.tensor_tensor(s.kbg[i], s.kn, cols(s.st[:, i, BEG, :]), ALU.mult).then_inc(S["k_beta"], 1)

            gates.masks(pool)
            head_pair(0)
            with pool.Fori(1, LAST) as it:
                head_pair(it)
            head_pair(LAST)


def build(nc, a, out, parts):
    with ExitStack() as ctx:
        g = make_shared(nc, ctx)
        m = moe_memory(nc, ctx, g)
        gd, ml = gdn_memory(nc, ctx, g), mla_memory(nc, g)
        m.wr_in = [g.sem(f"router_in{l}") for l in range(2)]
        ple_w = [g.sem(f"ple_w_in{l}") for l in range(2)]
        for layer in range(2):
            def load_router(sp, layer=layer):
                for dst, src in ((m.wr[:, :, 0:GROUPS], a["moe_router_group"]), (m.wr[:, :, GROUPS:], a["moe_router_expert"])):
                    sp.dma_start(dst, src[layer].rearrange("(p k) n -> p k n", k=KD)).then_inc(m.wr_in[layer], 16)
                for i in range(2):
                    load_expert(sp, m, a, layer, i, i, m.loaded[layer][i])

            def load_more(sp, layer=layer):
                if ("gdn", "mla")[layer] not in parts:
                    load_router(sp)
                for i in range(2, NBUF):
                    load_expert(sp, m, a, layer, i, i, m.loaded[layer][i])
                sp.wait_ge(m.rows_zeroed, 16 * len(zero_chunks(m)))

            if layer == 0:
                with semaphores_of(nc, g):
                    stage_setup(nc, g, m, gd, a)
            if ("gdn", "mla")[layer] in parts:
                with semaphores_of(nc, g):
                    if layer == 0:
                        stage_norm(nc, g, "gdn_norm", 0)
                        stage_delta(nc, g, gd, a)
                        stage_out(nc, g, "gdn_out", a["gdn_w_out"][0], load_router if "moe" in parts else None)
                    else:
                        w_in = g.sem("mla_w_in")
                        stage_norm(nc, g, "mla_norm", 1, lambda sp: load_mla_in(sp, ml, a, w_in))
                        stage_mla_in(nc, g, ml, a, w_in)
                        stage_mla_heads(nc, g, ml, a)
                        stage_out(nc, g, "mla_out", a["mla_w_out"][0], load_router if "moe" in parts else None)
            if "moe" not in parts:
                continue
            with semaphores_of(nc, g):
                stage_norm(nc, g, f"ffn_norm{layer}", 2 + layer, load_more)
                stage_route(nc, g, m, a, layer)
                stage_experts(nc, g, m, a, layer)
                stage_overflow(nc, g, m, a, layer)
                stage_combine(nc, g, m, layer, lambda sp, layer=layer: ple_load(sp, a, g, layer, ple_w[layer]))
                stage_norm(nc, g, f"ple_norm{layer}", 4 + layer)
                stage_ple(nc, g, a, layer, ple_w[layer])
        with semaphores_of(nc, g):
            stage_final(nc, g, a, out)


_INS = ['x', 'p', 'positions', 'norm_mix_g', 'norm_ffn_g', 'norm_ple_g', 'gdn_w_in', 'gdn_conv_w', 'gdn_a_log',
        'gdn_dt_bias', 'gdn_norm_g', 'gdn_w_out', 'mla_w_in', 'mla_q_norm_g', 'mla_kv_norm_g', 'mla_w_q_up',
        'mla_w_kv_up', 'mla_w_out', 'moe_router_group', 'moe_router_expert', 'moe_w_gate_up', 'moe_w_down',
        'ple_w_proj', 'ple_w_gate', 'final_norm_g']
PARTS = ["gdn", "mla", "moe"]


def kernel(**inputs):
    import concourse.bacc as bacc
    from concourse.bass_utils import run_bass_kernel_spmd
    nc = bacc.Bacc("TRN2", target_bir_lowering=False, num_devices=1)
    arrays, a = {}, {}
    given = {name: np.ascontiguousarray(inputs[name]) for name in _INS}
    given["rope_cols"] = rope_columns()
    for name, v in given.items():
        arrays["in_" + name] = v
        ap = nc.dram_tensor("in_" + name, v.shape, mybir.dt.from_np(v.dtype), kind="ExternalInput").ap()
        a[name] = ap
    out = nc.dram_tensor("out_0", (1, SEQ, D), F32, kind="ExternalOutput").ap()
    build(nc, a, out, PARTS)
    r = run_bass_kernel_spmd(nc, [arrays], core_ids=[0])
    return r.results[0]["out_0"]
```

```python
from contextlib import ExitStack, contextmanager

import numpy as np
import concourse.bass as bass
from concourse import mybir

P = 128
F32 = mybir.dt.float32
I32 = mybir.dt.int32
U32 = mybir.dt.uint32
ALU = mybir.AluOpType
ACT = mybir.ActivationFunctionType
AX = mybir.AxisListType.X

SEQ, D = 512, 1024
T = SEQ // P
KD = D // P
EPS = 1e-6

EXPERTS, GROUPS, PER_GROUP, FF = 64, 8, 8, 256
SLOTS = 32
OVER = 2 * SEQ // SLOTS
ROWS = (EXPERTS + OVER) * SLOTS
NBUF = 4
GU = KD * 2 * FF
DN = 2 * D
PLE = 256


class Memory:
    pass


@contextmanager
def semaphores_of(nc, g):
    outer, taken = g.sem, []

    def take(name):
        taken.append(nc.alloc_semaphore(name=name))
        return taken[-1]
    g.sem = take
    yield
    g.sem = outer
    nc.clear_and_free_semaphores(taken)
    nc.all_engine_barrier()


def make_shared(nc, ctx):
    def sb(name, shape, dt=F32):
        return ctx.enter_context(nc.sbuf_tensor(name, shape, dt))
    g = Memory()
    g.sem = lambda name: ctx.enter_context(nc.semaphore(name))
    g.bank = [ctx.enter_context(nc.psum_tensor(f"bank{i}", [P, 512], F32)) for i in range(8)]
    g.x = sb("x_res", [P, T, D])
    g.hT = sb("hT", [P, KD, SEQ])
    g.big = sb("big", [P, 8192])
    g.xn = g.big[:, 0:T * D].rearrange("p (t d) -> p t d", t=T)
    g.w = sb("w_ring", [P, NBUF, GU + DN])
    g.ident = sb("ident", [P, P])
    g.ones = sb("ones", [P, P])
    g.tri = sb("tri", [P, P])
    g.tri_strict = sb("tri_strict", [P, P])
    g.eps = sb("eps", [P, 1])
    g.sel = sb("sel", [P, 2, SLOTS])
    g.half = sb("half", [P, 2])
    g.iota8 = sb("iota8", [P, 8])
    g.iota_e = sb("iota_e", [P, EXPERTS])
    g.iota_b = sb("iota_b", [P, OVER])
    g.gains = sb("gains", [P, 6, KD])
    g.ss = sb("ss", [P, T])
    g.lnss = sb("lnss", [P, T])
    g.ss2 = sb("ss2", [P, T])
    g.rstd = sb("rstd", [P, T])
    return g


def zero_chunks(m):
    return [m.xd[n:n + 512, :] for n in range(0, ROWS, 512)] +\
        [m.yd[n:n + 512, :] for n in range(EXPERTS * SLOTS, ROWS, 512)]


def load_first(sp, m, gd, a):
    load_gates(sp, gd, a)
    for part in range(4):
        load_delta(sp, gd, a, part, 0)
    sp.wait_ge(m.zeros_made, 1)
    for rows in zero_chunks(m):
        sp.dma_start(rows.rearrange("(p r) (a c) -> p (r a) c", p=P, a=4),
                     m.zeros.unsqueeze(1).to_broadcast([P, 16, 256])).then_inc(m.rows_zeroed, 16)


def stage_setup(nc, g, m, gd, a):
    step, small, xin = g.sem("setup_step"), g.sem("small_loaded"), g.sem("x_loaded")
    with nc.Block() as block:
        @block.sync
        def _(sp):
            sp.dma_start(g.x[:, :, :], a["x"][0].rearrange("(t p) d -> p t d", p=P)).then_inc(xin, 16)
            for n, src in enumerate((a["norm_mix_g"], a["norm_ffn_g"], a["norm_ple_g"])):
                for layer in range(2):
                    sp.dma_start(g.gains[:, 2 * n + layer, :],
                                 src[layer].rearrange("(p k) -> p k", k=KD)).then_inc(small, 16)
            load_first(sp, m, gd, a)
            sp.wait_ge(small, 96)
            sp.wait_ge(xin, 16)

        @block.gpsimd
        def _(pool):
            count = [0]

            def done(ins):
                count[0] += 1
                ins.then_inc(step, 1)
                pool.wait_ge(step, count[0])

            pool.memset(m.zeros, 0.0).then_inc(m.zeros_made, 1)
            pool.memset(g.ones[:, :], 1.0).then_inc(step, 1)
            pool.memset(g.eps[:, :], EPS).then_inc(step, 1)
            pool.memset(g.ident[:, :], 0.0).then_inc(step, 1)
            pool.memset(g.tri[:, :], 1.0).then_inc(step, 1)
            pool.memset(g.tri_strict[:, :], 1.0).then_inc(step, 1)
            pool.memset(g.sel[:, :, :], 0.0).then_inc(step, 1)
            count[0] = 6
            done(pool.memset(g.half[:, :], 0.0))
            done(pool.memset(m.both[:, T, :], 0.0))
            for q in range(4):
                done(pool.memset(g.half[32 * q:32 * q + 32, q % 2:q % 2 + 1], 1.0))
            done(pool.affine_select(out=g.ident[:, :], in_=g.ident[:, :], compare_op=ALU.not_equal, fill=1.0,
                                    base=0, pattern=[[-1, P]], channel_multiplier=1))
            done(pool.affine_select(out=g.tri[:, :], in_=g.tri[:, :], compare_op=ALU.is_ge, fill=0.0,
                                    base=0, pattern=[[1, P]], channel_multiplier=-1))
            done(pool.affine_select(out=g.tri_strict[:, :], in_=g.tri_strict[:, :], compare_op=ALU.is_gt, fill=0.0,
                                    base=0, pattern=[[1, P]], channel_multiplier=-1))
            for q in range(2):
                done(pool.affine_select(out=g.sel[:, :, :], in_=g.sel[:, :, :], compare_op=ALU.not_equal, fill=1.0,
                                        base=-32 * q, pattern=[[-64, 2], [-1, SLOTS]], channel_multiplier=1))
            done(pool.iota(g.iota8[:, :], pattern=[[1, 8]], base=-8, channel_multiplier=0,
                           allow_small_or_imprecise_dtypes=True))
            done(pool.iota(g.iota_e[:, :], pattern=[[SLOTS, EXPERTS]], base=0, channel_multiplier=0,
                           allow_small_or_imprecise_dtypes=True))
            done(pool.iota(g.iota_b[:, :], pattern=[[1, OVER]], base=0, channel_multiplier=0,
                           allow_small_or_imprecise_dtypes=True))


def square_sums(act, g, t, scratch, signal):
    act.activation(scratch[:, t * D:(t + 1) * D], g.x[:, t, :], ACT.Square, accum_out=g.ss[:, t:t + 1]).then_inc(signal, 1)


def stage_norm(nc, g, tag, gain, sync_work=None, summed=True):
    sq, rs, xn = g.sem(tag + "_squares"), g.sem(tag + "_rstd"), [g.sem(f"{tag}_xn{t}") for t in range(T)]
    halves = [(g.bank[2 * t], g.bank[2 * t + 1]) for t in range(T)]
    tp, ev = g.sem(tag + "_transposed"), [g.sem(tag + "_taken_dve"), g.sem(tag + "_taken_act")]
    gcol = g.gains[:, gain, :]
    with nc.Block() as block:
        if sync_work:
            block.sync(sync_work)

        @block.scalar
        def _(act):
            if not summed:
                for t in range(T):
                    square_sums(act, g, t, g.big, sq)
                act.wait_ge(sq, T)
            act.activation(g.lnss[:, :], g.ss[:, :], ACT.Ln, scale=1.0 / D, bias=g.eps[:, 0:1]).then_inc(rs, 1)
            act.wait_ge(rs, 1)
            act.activation(g.rstd[:, :], g.lnss[:, :], ACT.Exp, scale=-0.5).then_inc(rs, 1)
            for t in range(1, T, 2):
                act.wait_ge(rs, 2)
                act.activation(g.xn[:, t, :], g.x[:, t, :], ACT.Copy, scale=g.rstd[:, t:t + 1]).then_inc(xn[t], 1)
            for t in range(T):
                act.wait_ge(tp, 2 * t + 2)
                for k in range(KD // 2, KD):
                    act.activation(g.hT[:, k, t * P:(t + 1) * P], halves[t][1][:, (k - KD // 2) * P:(k - KD // 2 + 1) * P], ACT.Copy,
                                   scale=gcol[:, k:k + 1]).then_inc(ev[1], 1)

        @block.vector
        def _(dve):
            dve.wait_ge(rs, 2)
            for t in range(0, T, 2):
                dve.tensor_scalar(g.xn[:, t, :], g.x[:, t, :], g.rstd[:, t:t + 1], None, ALU.mult).then_inc(xn[t], 1)
            for t in range(T):
                dve.wait_ge(tp, 2 * t + 1)
                dve.tensor_tensor(g.hT[:, 0:KD // 2, t * P:(t + 1) * P],
                                  halves[t][0][:, :].rearrange("p (k i) -> p k i", k=KD // 2),
                                  gcol[:, 0:KD // 2].unsqueeze(2).to_broadcast([P, KD // 2, P]),
                                  ALU.mult).then_inc(ev[0], 1)

        @block.tensor
        def _(pe):
            for t in range(T):
                pe.wait_ge(xn[t], 1)
                for h in range(2):
                    for k in range(KD // 2):
                        last = pe.transpose(halves[t][h][:, k * P:(k + 1) * P], g.xn[:, t, KD // 2 * h + k::KD],
                                            g.ident[:, :])
                    last.then_inc(tp, 1)


def moe_memory(nc, ctx, g):
    def sb(name, shape, dt=F32):
        return ctx.enter_context(nc.sbuf_tensor(name, shape, dt))
    m = Memory()
    m.wr = sb("w_router", [P, KD, GROUPS + EXPERTS])
    m.lg = sb("logits", [P, T, GROUPS + EXPERTS])
    m.s = {n: sb("r_" + n, [P, T]) for n in
           "gmax gidx gz gprob m1 i1 m2 i2 dif q s r".split()}
    m.e8 = {n: sb("r_" + n, [P, T, 8]) for n in "eq cand ohg gexp ing oh1 oh2 masked".split()}
    m.ew = [sb(f"expert_w{k}", [P, T]) for k in range(2)]
    m.oh = [sb(f"onehot{k}", [P, T, EXPERTS]) for k in range(2)]
    m.both = sb("onehot_both", [P, T + 1, EXPERTS])
    m.rank = sb("rank", [P, T, EXPERTS])
    m.tmp = sb("rank_tmp", [P, T, EXPERTS])
    m.cnt = sb("cnt", [P, EXPERTS])
    m.cnt_i = sb("cnt_i", [P, EXPERTS], I32)
    m.nov = sb("nov", [P, EXPERTS])
    m.cs = [sb(f"cs{i}", [P, EXPERTS]) for i in range(2)]
    m.base = sb("base", [P, EXPERTS])
    m.first = sb("first", [P, EXPERTS])
    m.destf = sb("destf", [P, 2, T])
    m.dest = [sb(f"dest{k}_{t}", [P, 1], U32) for k in range(2) for t in range(T)]
    m.cmp = g.big[0:1, 4096:4096 + OVER * EXPERTS].rearrange("p (b e) -> p b e", b=OVER)
    m.tblf = sb("tblf", [1, OVER + 1])
    m.tbl = sb("tbl", [1, OVER + 1], I32)
    m.xT = [sb(f"xT{i}", [P, KD, SLOTS]) for i in range(2)]
    m.sg = [sb(f"sg{i}", [P, 64]) for i in range(2)]
    m.um = [sb(f"um{i}", [P, 2, 64]) for i in range(2)]
    m.h2 = [sb(f"h2_{i}", [P, 2, 64]) for i in range(2)]
    m.hTe = [sb(f"hTe{i}", [P, 2, SLOTS]) for i in range(2)]
    m.y = [sb(f"y{i}", [P, 256]) for i in range(2)]
    m.xs = [g.big[0:SLOTS, 4096 + D * i:4096 + D * (i + 1)] for i in range(NBUF)]
    m.gu = [g.w[:, i, 0:GU].rearrange("p (k f) -> p k f", k=KD) for i in range(NBUF)]
    m.dn = [g.w[:, i, GU:GU + DN].rearrange("p (i d) -> p i d", i=2) for i in range(NBUF)]
    m.gu.append(g.hT[:, :, :].rearrange("p k (a f) -> p (k a) f", f=2 * FF))
    m.dn.append(sb("last_down", [P, 2, D])[:, :, :])
    m.xd = nc.dram_tensor("rows_in", [ROWS, D], F32, kind="Internal").ap()
    m.yd = nc.dram_tensor("rows_out", [ROWS, D], F32, kind="Internal").ap()
    m.zeros = m.rank[:, :, :].rearrange("p t e -> p (t e)")
    m.zeros_made, m.rows_zeroed = g.sem("zeros_made"), g.sem("rows_zeroed")
    m.loaded = [[g.sem(f"expert_w_loaded{l}_{i}") for i in range(NBUF + 1)] for l in range(2)]
    m.ple_in = [g.sem(f"ple{l}_p_loaded") for l in range(2)]
    m.over_w, m.over_rows = ([g.sem(f"over{l}_{n}_loaded") for l in range(2)] for n in ("w", "rows"))
    return m


def load_expert(sp, m, a, layer, buf, e, signal, down_free=None):
    if isinstance(e, int):
        gu, dn = a["moe_w_gate_up"][layer, e], a["moe_w_down"][layer, e]
        gu, dn = gu.rearrange("(p k) f -> p k f", k=KD), dn.rearrange("(i p) d -> p i d", p=P)
    else:
        gu = a["moe_w_gate_up"][layer, bass.ds(e, 1)].rearrange("a (p k) f -> p (a k) f", k=KD)
        dn = a["moe_w_down"][layer, bass.ds(e, 1)].rearrange("a (i p) d -> p (a i) d", p=P)
    sp.dma_start(m.gu[buf], gu).then_inc(signal, 16)
    if down_free:
        sp.wait_ge(*down_free)
    sp.dma_start(m.dn[buf], dn).then_inc(signal, 16)


def stage_route(nc, g, m, a, layer):
    tag = f"route{layer}"
    wr_in, logits, lgc = g.sem(tag + "_w_in"), g.sem(tag + "_logits"), g.sem(tag + "_logits_taken")
    vs, ex_in, ex = g.sem(tag + "_step"), g.sem(tag + "_exp_in"), g.sem(tag + "_exp")
    both, counted, rows = g.sem(tag + "_onehots"), g.sem(tag + "_counted"), g.sem(tag + "_dest")
    sent = g.sem(tag + "_rows_sent")
    with nc.Block() as block:
        @block.sync
        def _(sp):
            sp.wait_ge(logits, 1)
            load_expert(sp, m, a, layer, NBUF, EXPERTS - 1, m.loaded[layer][NBUF])

        @block.tensor
        def _(pe):
            pe.wait_ge(m.wr_in[layer], 32)
            n = GROUPS + EXPERTS
            for t in range(T):
                for k in range(KD):
                    last = pe.matmul(g.bank[0][:, t * n:(t + 1) * n], g.hT[:, k, t * P:(t + 1) * P], m.wr[:, k, :],
                                     start=k == 0, stop=k == KD - 1)
            last.then_inc(logits, 1)
            pe.wait_ge(both, 1)
            pe.matmul(g.bank[1][:, 0:(T + 1) * EXPERTS], g.tri_strict[:, :], m.both[:, :, :].rearrange("p t e -> p (t e)"),
                      start=True, stop=False)
            for u in range(T):
                n = T - u
                last = pe.matmul(g.bank[1][:, (u + 1) * EXPERTS:(T + 1) * EXPERTS].rearrange("p (t e) -> p t e", t=n),
                                 g.ones[:, :], m.both[:, u, :].unsqueeze(1).to_broadcast([P, n, EXPERTS]),
                                 start=False, stop=u == T - 1)
            last.then_inc(counted, 1)

        @block.scalar
        def _(act):
            act.wait_ge(ex_in, 1)
            act.activation(m.e8["gexp"][:, :, :], m.e8["cand"][:, :, :], ACT.Exp).then_inc(ex, 1)
            act.wait_ge(ex_in, 2)
            act.activation(m.s["q"][:, :], m.s["dif"][:, :], ACT.Exp).then_inc(ex, 1)

        @block.vector
        def _(dve):
            count = [0]

            def done(ins):
                count[0] += 1
                ins.then_inc(vs, 1)
                dve.wait_ge(vs, count[0])

            def bc(v, n):
                return v[:, :].unsqueeze(2).to_broadcast([P, T, n])

            def first_of(src, top, idx, onehot):
                done(dve.tensor_reduce(top[:, :], src, AX, ALU.max))
                done(dve.tensor_tensor(m.e8["eq"][:, :, :], src, bc(top, 8), ALU.is_equal))
                done(dve.tensor_tensor(m.e8["masked"][:, :, :], m.e8["eq"][:, :, :], iota8, ALU.mult))
                done(dve.tensor_reduce(idx[:, :], m.e8["masked"][:, :, :], AX, ALU.min))
                done(dve.tensor_tensor(onehot[:, :, :], iota8, bc(idx, 8), ALU.is_equal))

            iota8 = g.iota8[:, :].unsqueeze(1).to_broadcast([P, T, 8])
            s, e8 = m.s, m.e8
            dve.wait_ge(logits, 1)
            done(dve.tensor_copy(m.lg[:, :, :], g.bank[0][:, 0:T * 72].rearrange("p (t n) -> p t n", t=T)))
            gl = m.lg[:, :, 0:GROUPS]
            el = m.lg[:, :, GROUPS:].rearrange("p t (g e) -> p t g e", g=GROUPS)
            first_of(gl, s["gmax"], s["gidx"], e8["ohg"])
            dve.tensor_tensor(e8["cand"][:, :, :], gl, bc(s["gmax"], 8), ALU.subtract).then_inc(ex_in, 1)
            picked = m.tmp[:, :, :].rearrange("p t (g e) -> p t g e", g=GROUPS)
            done(dve.tensor_tensor(picked, el, e8["ohg"][:, :, :].unsqueeze(3).to_broadcast([P, T, GROUPS, PER_GROUP]),
                                   ALU.mult))
            done(dve.tensor_reduce(e8["ing"][:, :, :], m.tmp[:, :, :].rearrange("p t (g e) -> p t e g", g=GROUPS),
                                   AX, ALU.add))
            first_of(e8["ing"][:, :, :], s["m1"], s["i1"], e8["oh1"])
            done(dve.scalar_tensor_tensor(out=e8["eq"][:, :, :], in0=e8["oh1"][:, :, :],
                                          scalar=-3e38, in1=e8["ing"][:, :, :], op0=ALU.mult, op1=ALU.add))
            done(dve.tensor_copy(e8["ing"][:, :, :], e8["eq"][:, :, :]))
            first_of(e8["ing"][:, :, :], s["m2"], s["i2"], e8["oh2"])
            dve.tensor_tensor(s["dif"][:, :], s["m2"][:, :], s["m1"][:, :], ALU.subtract).then_inc(ex_in, 1)
            for k, name in enumerate(("oh1", "oh2")):
                done(dve.tensor_tensor(m.oh[k][:, :, :].rearrange("p t (g e) -> p t g e", g=GROUPS),
                                       e8["ohg"][:, :, :].unsqueeze(3).to_broadcast([P, T, GROUPS, PER_GROUP]),
                                       e8[name][:, :, :].unsqueeze(2).to_broadcast([P, T, GROUPS, PER_GROUP]), ALU.mult))
            dve.tensor_tensor(m.both[:, 0:T, :], m.oh[0][:, :, :], m.oh[1][:, :, :], ALU.add).then_inc(both, 1)
            dve.wait_ge(ex, 2)
            done(dve.tensor_reduce(s["gz"][:, :], e8["gexp"][:, :, :], AX, ALU.add))
            done(dve.reciprocal(s["gprob"][:, :], s["gz"][:, :]))
            done(dve.tensor_scalar(s["s"][:, :], s["q"][:, :], 1.0, None, ALU.add))
            done(dve.reciprocal(s["r"][:, :], s["s"][:, :]))
            done(dve.tensor_tensor(m.ew[0][:, :], s["gprob"][:, :], s["r"][:, :], ALU.mult))
            done(dve.tensor_tensor(m.ew[1][:, :], m.ew[0][:, :], s["q"][:, :], ALU.mult))
            dve.wait_ge(counted, 1)
            done(dve.tensor_copy(m.rank[:, :, :], g.bank[1][:, 0:T * EXPERTS].rearrange("p (t e) -> p t e", t=T)))
            done(dve.tensor_scalar(m.cnt_i[:, :], g.bank[1][:, T * EXPERTS:(T + 1) * EXPERTS], SLOTS - 1.0, None, ALU.add))
            done(dve.tensor_scalar(m.cnt_i[:, :], m.cnt_i[:, :], SLOTS.bit_length() - 1, None, ALU.arith_shift_right))
            done(dve.tensor_scalar(m.nov[:, :], m.cnt_i[:, :], -1.0, 0.0, ALU.add, ALU.max))
            cs, n = m.nov, 1
            while n < EXPERTS:
                to = m.cs[0] if cs is not m.cs[0] else m.cs[1]
                count[0] += 1
                dve.tensor_copy(to[:, 0:n], cs[:, 0:n]).then_inc(vs, 1)
                done(dve.tensor_tensor(to[:, n:], cs[:, n:], cs[:, 0:EXPERTS - n], ALU.add))
                cs, n = to, 2 * n
            done(dve.tensor_tensor(m.base[:, :], cs[:, :], m.nov[:, :], ALU.subtract))
            done(dve.tensor_scalar(m.base[:, :], m.base[:, :], float(SLOTS), float(SLOTS * (EXPERTS - 1)), ALU.mult, ALU.add))
            done(dve.tensor_tensor(m.first[:, :], g.iota_e[:, :], m.base[:, :], ALU.subtract))
            done(dve.tensor_scalar(m.tmp[:, :, :], m.rank[:, :, :], float(SLOTS), None, ALU.is_lt))
            done(dve.tensor_tensor(m.tmp[:, :, :], m.tmp[:, :, :],
                                   m.first[:, :].unsqueeze(1).to_broadcast([P, T, EXPERTS]), ALU.mult))
            done(dve.tensor_tensor(m.rank[:, :, :], m.rank[:, :, :], m.tmp[:, :, :], ALU.add))
            done(dve.tensor_tensor(m.rank[:, :, :], m.rank[:, :, :],
                                   m.base[:, :].unsqueeze(1).to_broadcast([P, T, EXPERTS]), ALU.add))
            for k in range(2):
                done(dve.tensor_tensor(m.tmp[:, :, :], m.rank[:, :, :], m.oh[k][:, :, :], ALU.mult))
                done(dve.tensor_reduce(m.destf[:, k, :], m.tmp[:, :, :], AX, ALU.add))
                for t in range(T):
                    dve.tensor_copy(m.dest[k * T + t][:, :], m.destf[:, k, t:t + 1]).then_inc(rows, 1)
            done(dve.tensor_tensor(m.cmp[:, :, :], cs[0:1, :].unsqueeze(1).to_broadcast([1, OVER, EXPERTS]),
                                   g.iota_b[0:1, :].unsqueeze(2).to_broadcast([1, OVER, EXPERTS]), ALU.is_le))
            done(dve.tensor_reduce(m.tblf[:, 0:OVER], m.cmp[:, :, :], AX, ALU.add))
            done(dve.tensor_scalar(m.tbl[:, 0:OVER], m.tblf[:, 0:OVER], EXPERTS - 1.0, None, ALU.min))
            done(dve.tensor_scalar(m.tbl[:, OVER:OVER + 1], cs[0:1, EXPERTS - 1:EXPERTS], 0.0, None, ALU.max))

        @block.gpsimd
        def _(pool):
            for i in range(2 * T):
                pool.wait_ge(rows, i + 1)
                pool.indirect_dma_start(m.xd, bass.IndirectOffsetOnAxis(ap=m.dest[i][:, 0:1], axis=0),
                                        g.xn[:, i % T, :], None).then_inc(sent, 16)
            pool.wait_ge(sent, 16 * 2 * T)


def stage_experts(nc, g, m, a, layer):
    tag = f"exp{layer}"
    loaded = m.loaded[layer]
    xs_in = [g.sem(f"{tag}_rows_in{i}") for i in range(NBUF)]
    names = "xt xT gu sg um h2 ht hT dn y".split()
    S = {n: g.sem(f"{tag}_{n}") for n in names}
    y_out = [g.sem(f"{tag}_y_out{i}") for i in range(2)]
    gcol = g.gains[:, 2 + layer, :].unsqueeze(2).to_broadcast([P, KD, SLOTS])
    PASSES = EXPERTS // NBUF
    with nc.Block() as block:
        @block.sync
        def _(sp):
            for i in range(NBUF):
                sp.dma_start(m.xs[i], m.xd[SLOTS * i:SLOTS * (i + 1), :]).then_inc(xs_in[i], 16)

            def load_turn(it, weights=NBUF):
                for i in range(NBUF):
                    last = NBUF * (it - 1) + i + 1
                    if i < weights:
                        sp.wait_ge(S["gu"], last)
                        load_expert(sp, m, a, layer, i, NBUF * it + i, loaded[i], (S["dn"], last))
                    else:
                        sp.wait_ge(S["dn"], last)
                    sp.dma_start(m.xs[i], m.xd[bass.ds(SLOTS * (NBUF * it + i), SLOTS), :]).then_inc(xs_in[i], 16)

            with sp.Fori(1, PASSES - 1) as it:
                load_turn(it)
            load_turn(PASSES - 1, NBUF - 1)
            sp.wait_ge(S["dn"], EXPERTS - NBUF + 1)
            with sp.If(overflow_blocks(sp, m) > 0):
                load_overflow(sp, m, a, layer, 0)
            sp.wait_ge(S["dn"], EXPERTS - NBUF + 2)
            load_ple_proj(sp, a, ple_memory(g), layer, m.ple_in[layer])

        @block.tensor
        def _(pe):
            def buffer(it, i):
                return NBUF if i == NBUF - 1 and isinstance(it, int) and it == PASSES - 1 else i

            def rows(it, i):
                j = i % 2
                pe.wait_ge(xs_in[i], 16 * (it + 1))
                if not (isinstance(it, int) and it == 0 and i < 2):
                    pe.wait_ge(S["xT"], NBUF * it + i - 1)
                pe.matmul(g.bank[j][:, 0:SLOTS], m.xs[i][:, 0::KD], g.ident[0:SLOTS, 0:SLOTS], start=True, stop=True)
                for k in range(1, KD):
                    last = pe.transpose(g.bank[j][:, SLOTS * k:SLOTS * (k + 1)], m.xs[i][:, k::KD],
                                        g.ident[0:SLOTS, 0:SLOTS])
                last.then_inc(S["xt"], 1)

            def gate_up(it, i):
                j, buf = i % 2, buffer(it, i)
                pe.wait_ge(loaded[buf], 32 if buf == NBUF else 32 * (it + 1))
                pe.wait_ge(S["xT"], NBUF * it + i + 1)
                if not (isinstance(it, int) and it == 0 and i < 2):
                    pe.wait_ge(S["um"], NBUF * it + i - 1)
                    pe.wait_ge(S["sg"], NBUF * it + i - 1)
                for k in range(KD):
                    w = m.gu[buf][:, k, :].rearrange("p (h q c) -> p q h c", h=2, q=4)
                    for q in range(4):
                        last = pe.matmul(g.bank[2 + j][32 * q:32 * q + 32, 0:P].rearrange("p (h c) -> p h c", h=2),
                                         m.xT[j][:, k, :], w[:, q], start=k == 0, stop=k == KD - 1)
                last.then_inc(S["gu"], 1)

            def down(it, i):
                j, b = buffer(it - 1, NBUF - 1) if i == 0 else i - 1, NBUF * it + i - 1
                r = (i - 1) % 2
                pe.wait_ge(S["h2"], b + 1)
                if not (isinstance(b, int) and b < 2):
                    pe.wait_ge(S["hT"], b - 1)
                pe.matmul(g.bank[4 + r][:, 0:2 * SLOTS], m.h2[r][:, :, :].rearrange("p h c -> p (h c)"),
                          g.sel[:, :, :].rearrange("p i s -> p (i s)"), start=True, stop=True).then_inc(S["ht"], 1)
                pe.wait_ge(S["hT"], b + 1)
                if not (isinstance(b, int) and b < 2):
                    pe.wait_ge(S["y"], b - 1)
                for n in range(2):
                    for q in range(4):
                        last = pe.matmul(g.bank[6 + r][32 * q:32 * q + 32, 0:256], m.hTe[r][:, n, :],
                                         m.dn[j][:, n, 256 * q:256 * (q + 1)], start=n == 0, stop=n == 1)
                last.then_inc(S["dn"], 1)

            def turn(it):
                for i in range(NBUF):
                    rows(it, i)
                    if not (isinstance(it, int) and it == 0 and i == 0):
                        down(it, i)
                    gate_up(it, i)

            turn(0)
            with pe.Fori(1, PASSES - 1) as it:
                turn(it)
            turn(PASSES - 1)
            down(PASSES, 0)

        def vector_turn(dve, it):
            first = isinstance(it, int) and it == 0
            for i in range(NBUF):
                j, b = i % 2, NBUF * it + i
                early = first and i < 2
                dve.wait_ge(S["xt"], b + 1)
                if not early:
                    dve.wait_ge(S["gu"], b - 1)
                dve.tensor_tensor(m.xT[j][:, :, :], g.bank[j][:, 0:KD * SLOTS].rearrange("p (k s) -> p k s", k=KD),
                                  gcol, ALU.mult).then_inc(S["xT"], 1)
                dve.wait_ge(S["gu"], b + 1)
                dve.wait_ge(S["sg"], b + 1)
                dve.tensor_tensor(m.um[j][:, :, :], g.bank[2 + j][:, 64:128].unsqueeze(1).to_broadcast([P, 2, 64]),
                                  g.half[:, :].unsqueeze(2).to_broadcast([P, 2, 64]), ALU.mult).then_inc(S["um"], 1)
                dve.wait_ge(S["um"], b + 1)
                if not early:
                    dve.wait_ge(S["ht"], b - 1)
                dve.tensor_tensor(m.h2[j][:, :, :], m.um[j][:, :, :],
                                  m.sg[j][:, :].unsqueeze(1).to_broadcast([P, 2, 64]), ALU.mult).then_inc(S["h2"], 1)
                dve.wait_ge(S["ht"], b + 1)
                if not early:
                    dve.wait_ge(S["dn"], b - 1)
                dve.tensor_copy(m.hTe[j][:, :, :],
                                g.bank[4 + j][:, 0:2 * SLOTS].rearrange("p (i s) -> p i s", i=2)).then_inc(S["hT"], 1)

        @block.vector
        def _(dve):
            vector_turn(dve, 0)
            with dve.Fori(1, PASSES) as it:
                vector_turn(dve, it)

        def scalar_turn(act, it):
            first = isinstance(it, int) and it == 0
            for i in range(NBUF):
                j, b = i % 2, NBUF * it + i
                early = first and i < 2
                act.wait_ge(S["gu"], b + 1)
                if not early:
                    act.wait_ge(S["h2"], b - 1)
                act.activation(m.sg[j][:, :], g.bank[2 + j][:, 0:64], ACT.Silu).then_inc(S["sg"], 1)
                act.wait_ge(S["dn"], b + 1)
                if not early:
                    act.wait_ge(y_out[j], 16 * 4 * (2 * it + i // 2))
                act.activation(m.y[j][:, :], g.bank[6 + j][:, 0:256], ACT.Copy).then_inc(S["y"], 1)
                act.wait_ge(S["y"], b + 1)
                for q in range(4):
                    act.dma_start(m.yd[bass.ds(SLOTS * b, SLOTS), 256 * q:256 * (q + 1)],
                                  m.y[j][32 * q:32 * q + 32, :]).then_inc(y_out[j], 16)

        @block.scalar
        def _(act):
            scalar_turn(act, 0)
            with act.Fori(1, PASSES) as it:
                scalar_turn(act, it)
            for j in range(2):
                act.wait_ge(y_out[j], 16 * 4 * EXPERTS // 2)


def overflow_blocks(eng, m):
    return eng.value_load(m.tbl[0:1, OVER:OVER + 1], min_val=0, max_val=OVER)


def load_overflow(sp, m, a, layer, b):
    e = sp.value_load(m.tbl[0:1, bass.ds(b, 1)], min_val=0, max_val=EXPERTS - 1)
    load_expert(sp, m, a, layer, 0, e, m.over_w[layer])
    sp.dma_start(m.xs[0], m.xd[bass.ds(SLOTS * (EXPERTS + b), SLOTS), :]).then_inc(m.over_rows[layer], 16)


def stage_overflow(nc, g, m, a, layer):
    tag = f"over{layer}"
    names = "xt xT gu sg um h2 ht hT dn y out".split()
    S = {n: g.sem(f"{tag}_{n}") for n in names}
    gcol = g.gains[:, 2 + layer, :].unsqueeze(2).to_broadcast([P, KD, SLOTS])

    with nc.Block() as block:
        @block.sync
        def _(sp):
            n = overflow_blocks(sp, m)
            with sp.If(n > 1), sp.Fori(1, n) as it:
                sp.wait_ge(S["dn"], it)
                load_overflow(sp, m, a, layer, it)

        @block.tensor
        def _(pe):
            n = overflow_blocks(pe, m)
            with pe.If(n > 0), pe.Fori(0, n) as it:
                pe.wait_ge(m.over_rows[layer], 16 * (it + 1))
                for k in range(KD):
                    last = pe.matmul(g.bank[0][:, SLOTS * k:SLOTS * (k + 1)], m.xs[0][:, k::KD],
                                     g.ident[0:SLOTS, 0:SLOTS], start=True, stop=True)
                last.then_inc(S["xt"], 1)
                pe.wait_ge(m.over_w[layer], 32 * (it + 1))
                pe.wait_ge(S["xT"], it + 1)
                for k in range(KD):
                    w = m.gu[0][:, k, :].rearrange("p (h q c) -> p q h c", h=2, q=4)
                    for q in range(4):
                        last = pe.matmul(g.bank[2][32 * q:32 * q + 32, 0:P].rearrange("p (h c) -> p h c", h=2),
                                         m.xT[0][:, k, :], w[:, q], start=k == 0, stop=k == KD - 1)
                last.then_inc(S["gu"], 1)
                pe.wait_ge(S["h2"], it + 1)
                pe.matmul(g.bank[4][:, 0:2 * SLOTS], m.h2[0][:, :, :].rearrange("p h c -> p (h c)"),
                          g.sel[:, :, :].rearrange("p i s -> p (i s)"), start=True, stop=True).then_inc(S["ht"], 1)
                pe.wait_ge(S["hT"], it + 1)
                for n in range(2):
                    for q in range(4):
                        last = pe.matmul(g.bank[6][32 * q:32 * q + 32, 0:256], m.hTe[0][:, n, :],
                                         m.dn[0][:, n, 256 * q:256 * (q + 1)], start=n == 0, stop=n == 1)
                last.then_inc(S["dn"], 1)
                pe.wait_ge(S["y"], it + 1)

        @block.vector
        def _(dve):
            n = overflow_blocks(dve, m)
            with dve.If(n > 0), dve.Fori(0, n) as it:
                dve.wait_ge(S["xt"], it + 1)
                dve.tensor_tensor(m.xT[0][:, :, :], g.bank[0][:, 0:KD * SLOTS].rearrange("p (k s) -> p k s", k=KD),
                                  gcol, ALU.mult).then_inc(S["xT"], 1)
                dve.wait_ge(S["gu"], it + 1)
                dve.wait_ge(S["sg"], it + 1)
                dve.tensor_tensor(m.um[0][:, :, :], g.bank[2][:, 64:128].unsqueeze(1).to_broadcast([P, 2, 64]),
                                  g.half[:, :].unsqueeze(2).to_broadcast([P, 2, 64]), ALU.mult).then_inc(S["um"], 1)
                dve.wait_ge(S["um"], it + 1)
                dve.tensor_tensor(m.h2[0][:, :, :], m.um[0][:, :, :],
                                  m.sg[0][:, :].unsqueeze(1).to_broadcast([P, 2, 64]), ALU.mult).then_inc(S["h2"], 1)
                dve.wait_ge(S["ht"], it + 1)
                dve.tensor_copy(m.hTe[0][:, :, :],
                                g.bank[4][:, 0:2 * SLOTS].rearrange("p (i s) -> p i s", i=2)).then_inc(S["hT"], 1)

        @block.scalar
        def _(act):
            n = overflow_blocks(act, m)
            with act.If(n > 0), act.Fori(0, n) as it:
                act.wait_ge(S["gu"], it + 1)
                act.activation(m.sg[0][:, :], g.bank[2][:, 0:64], ACT.Silu).then_inc(S["sg"], 1)
                act.wait_ge(S["dn"], it + 1)
                act.activation(m.y[0][:, :], g.bank[6][:, 0:256], ACT.Copy).then_inc(S["y"], 1)
                act.wait_ge(S["y"], it + 1)
                for q in range(4):
                    act.dma_start(m.yd[bass.ds(SLOTS * (EXPERTS + it), SLOTS), 256 * q:256 * (q + 1)],
                                  m.y[0][32 * q:32 * q + 32, :]).then_inc(S["out"], 16)
                act.wait_ge(S["out"], 16 * 4 * (it + 1))


def ple_memory(g):
    s = Memory()
    take = workspace(g, 1, 1)
    s.p, s.pT, s.wp = take(T, PLE), take(2, SEQ), take(2, D)
    s.proj = workspace(g, 0, 1)(T, D)
    s.wg = workspace(g, 2, 2)(KD, D)
    return s


def load_ple_proj(sp, a, s, layer, signal):
    sp.dma_start(s.p, a["p"][layer, 0].rearrange("(t p) c -> p t c", p=P)).then_inc(signal, 16)
    sp.dma_start(s.wp, a["ple_w_proj"][layer].rearrange("(k p) n -> p k n", p=P)).then_inc(signal, 16)


def stage_combine(nc, g, m, layer, sync_work=None):
    s = ple_memory(g)
    tp, pT, product, taken = (g.sem(f"comb{layer}_{n}") for n in "p_transposed pT p_projected p_projected_taken".split())
    steps = [(t, h) for t in range(T) for h in range(2)]
    tag = f"comb{layer}"
    got = [g.sem(f"{tag}_row{i}") for i in range(2 * T)]
    added, squares = g.sem(tag + "_added"), g.sem(tag + "_squares")
    rows = g.big[:, :].rearrange("p (n d) -> p n d", d=D)
    with nc.Block() as block:
        @block.sync
        def _(sp):
            for i in range(2 * T):
                sp.wait_ge(got[i], 16)
            if sync_work:
                sync_work(sp)

        @block.gpsimd
        def _(pool):
            for i in range(2 * T):
                pool.indirect_dma_start(rows[:, i, :], None, m.yd,
                                        bass.IndirectOffsetOnAxis(ap=m.dest[i][:, 0:1], axis=0)).then_inc(got[i], 16)

        @block.vector
        def _(dve):
            for i in range(2 * T):
                t = i % T
                dve.wait_ge(got[i], 16)
                if i >= T:
                    dve.wait_ge(added, i - T + 1)
                dve.scalar_tensor_tensor(out=g.x[:, t, :], in0=rows[:, i, :], scalar=m.ew[i // T][:, t:t + 1],
                                         in1=g.x[:, t, :], op0=ALU.mult, op1=ALU.add).then_inc(added, 1)

        @block.tensor
        def _(pe):
            pe.wait_ge(m.ple_in[layer], 32)
            for k in range(2):
                for t in range(T):
                    last = pe.transpose(g.bank[6 + k][:, t * P:(t + 1) * P], s.p[:, t, k * P:(k + 1) * P], g.ident[:, :])
                last.then_inc(tp, 1)
            pe.wait_ge(pT, 2)
            for n, (t, h) in enumerate(steps):
                if n >= 4:
                    pe.wait_ge(taken, n - 3)
                for k in range(2):
                    last = pe.matmul(g.bank[n % 4][:, :], s.pT[:, k, t * P:(t + 1) * P], s.wp[:, k, 512 * h:512 * (h + 1)],
                                     start=k == 0, stop=k == 1)
                last.then_inc(product, 1)

        @block.scalar
        def _(act):
            for k in range(2):
                act.wait_ge(tp, k + 1)
                act.activation(s.pT[:, k, :], g.bank[6 + k][:, :], ACT.Copy).then_inc(pT, 1)
            for n, (t, h) in enumerate(steps):
                act.wait_ge(product, n + 1)
                act.activation(s.proj[:, t, 512 * h:512 * (h + 1)], g.bank[n % 4][:, :], ACT.Copy).then_inc(taken, 1)
                if n >= T:
                    act.wait_ge(added, n + 1)
                    square_sums(act, g, n - T, g.hT[:, :, :].rearrange("p k s -> p (k s)"), squares)


def ple_load(sp, a, g, layer, wsem):
    sp.dma_start(ple_memory(g).wg, a["ple_w_gate"][layer].rearrange("(p k) n -> p k n", k=KD)).then_inc(wsem, 16)


def stage_ple(nc, g, a, layer, wsem, sync_work=None):
    tag = f"ple{layer}"
    squares = g.sem(tag + "_squares")
    gate, sig, mul, add = (g.sem(f"{tag}_{n}") for n in "gate sigmoid product added".split())
    s = ple_memory(g)
    sg = [g.big[:, 4096 + 512 * i:4608 + 512 * i] for i in range(2)]
    pr = [g.big[:, 5120 + 512 * i:5632 + 512 * i] for i in range(2)]
    steps = [(t, h) for t in range(T) for h in range(2)]
    with nc.Block() as block:
        if sync_work:
            block.sync(sync_work)

        @block.tensor
        def _(pe):
            pe.wait_ge(wsem, 16)
            for n, (t, h) in enumerate(steps):
                if n >= 3:
                    pe.wait_ge(sig, n - 2)
                for k in range(KD):
                    last = pe.matmul(g.bank[n % 3][:, :], g.hT[:, k, t * P:(t + 1) * P], s.wg[:, k, 512 * h:512 * (h + 1)],
                                     start=k == 0, stop=k == KD - 1)
                last.then_inc(gate, 1)

        @block.scalar
        def _(act):
            for n in range(len(steps)):
                act.wait_ge(gate, n + 1)
                if n >= 2:
                    act.wait_ge(mul, n - 1)
                act.activation(sg[n % 2], g.bank[n % 3][:, :], ACT.Sigmoid).then_inc(sig, 1)
                if n % 2 == 0 and n > 0:
                    act.wait_ge(add, n)
                    square_sums(act, g, n // 2 - 1, g.big, squares)
            act.wait_ge(add, 2 * T)
            square_sums(act, g, T - 1, g.big, squares)

        @block.vector
        def _(dve):
            for n, (t, h) in enumerate(steps):
                dve.wait_ge(sig, n + 1)
                if n >= 2:
                    dve.wait_ge(add, n - 1)
                dve.tensor_tensor(pr[n % 2], s.proj[:, t, 512 * h:512 * (h + 1)], sg[n % 2], ALU.mult).then_inc(mul, 1)
                dve.wait_ge(mul, n + 1)
                xv = g.x[:, t, 512 * h:512 * (h + 1)]
                dve.tensor_tensor(xv, xv, pr[n % 2], ALU.add).then_inc(add, 1)


def stage_final(nc, g, a, out):
    rs, gin = g.sem("final_rstd"), g.sem("final_gain_in")
    fin, sent = g.sem("final_rows"), g.sem("final_sent")
    gb = g.big[:, 4096:5120]
    with nc.Block() as block:
        @block.sync
        def _(sp):
            sp.dma_start(gb, a["final_norm_g"].partition_broadcast(P)).then_inc(gin, 16)
            for t in range(T):
                sp.wait_ge(fin, t + 1)
                sp.dma_start(out[0, t * P:(t + 1) * P, :], g.xn[:, t, :]).then_inc(sent, 16)
            sp.wait_ge(sent, 16 * T)

        @block.scalar
        def _(act):
            act.activation(g.lnss[:, :], g.ss[:, :], ACT.Ln, scale=1.0 / D, bias=g.eps[:, 0:1]).then_inc(rs, 1)
            act.wait_ge(rs, 1)
            act.activation(g.rstd[:, :], g.lnss[:, :], ACT.Exp, scale=-0.5).then_inc(rs, 1)

        @block.vector
        def _(dve):
            dve.wait_ge(rs, 2)
            dve.wait_ge(gin, 16)
            for t in range(T):
                dve.scalar_tensor_tensor(out=g.xn[:, t, :], in0=g.x[:, t, :], scalar=g.rstd[:, t:t + 1],
                                         in1=gb, op0=ALU.mult, op1=ALU.mult).then_inc(fin, 1)


HEADS = 16
NOPE, ROPE, VDIM, QL, KVL = 128, 64, 128, 256, 128
QK = NOPE + ROPE
MLA_SCALE = QK ** -0.5
NEG = -1e30


def workspace(g, first, nbufs):
    flat = g.w[:, first:first + nbufs, :].rearrange("p n f -> p (n f)")
    at = [0]

    def take(*shape):
        n = int(np.prod(shape))
        v = flat[:, at[0]:at[0] + n]
        at[0] += n
        assert at[0] <= nbufs * (GU + DN), at[0]
        if len(shape) == 2:
            v = v.rearrange("p (a b) -> p a b", a=shape[0])
        if len(shape) == 3:
            v = v.rearrange("p (a b c) -> p a b c", a=shape[0], b=shape[1])
        return v
    return take


def rope_columns():
    inv = (np.float32(10000.0) ** (-np.arange(0, ROPE, 2, dtype=np.float32) / np.float32(ROPE))).astype(np.float32)
    turns = np.repeat(np.array([0.25, 0.25, 0.5, 0.0], np.float32), 32)
    return np.stack([np.tile(inv, 4), turns, (turns.astype(np.float64) * 2 * np.pi).astype(np.float32)], axis=1)


def mla_memory(nc, g):
    s = Memory()
    take = workspace(g, 2, 2)
    s.wn = take(KD, QL + KVL)
    s.qn = take(T, QL)
    s.cs = take(SEQ)
    s.kdup = take(SEQ)
    s.ckv = take(T, KVL)
    s.ckvT = take(SEQ)
    s.qaT = take(2, SEQ)
    s.neg = take(P)
    s.dup = take(P)
    s.cols = take(4)
    s.gq = take(2)
    take = workspace(g, 1, 1)
    s.wr = take(KD, P)
    s.pos = take(SEQ).bitcast(I32)
    s.gkv = take(KVL)
    s.ang = take(SEQ)
    s.n = take(SEQ)
    h = Memory()
    flat = g.w[:, 2:4, :].rearrange("p n f -> p (n f)")
    at = [0]

    def reuse(*shape):
        n = int(np.prod(shape))
        v = flat[:, at[0]:at[0] + n]
        at[0] += n
        assert at[0] <= KD * (QL + KVL) + T * QL
        return v.rearrange("p (a b) -> p a b", a=shape[0]) if len(shape) == 2 else v
    h.qlatT, h.rot, h.qnT = reuse(SEQ), reuse(SEQ), reuse(SEQ)
    h.p = [reuse((t + 1) * P) for t in range(T)]
    h.wukT = reuse(P)
    take2 = workspace(g, 1, 1)
    h.pT = [take2((T - k) * P) for k in range(T)]
    h.olT = take2(SEQ)
    h.mx, h.nm, h.rs, h.ri = (take2(T) for _ in range(4))
    take3 = workspace(g, 1, 1)
    take3(4096)
    h.wq = [take3(2, 2 * P) for _ in range(2)]
    h.wkv = [take3(2 * P) for _ in range(2)]
    h.w_in = [g.sem(f"head_w_in{i}") for i in range(2)]
    s.h = h
    return s


def stage_mla_in(nc, g, s, a, w_in):
    tag = "mla_in"
    cst, mm, rs, nat = g.sem(tag + "_consts"), g.sem(tag + "_products"), g.sem(tag + "_rstd"), g.sem(tag + "_natural")
    sq, tp, tpc, tab = g.sem(tag + "_squares"), g.sem(tag + "_transposed"), g.sem(tag + "_taken"), g.sem(tag + "_table")
    kd, ang = g.sem(tag + "_key_dup"), g.sem(tag + "_angles")
    with nc.Block() as block:
        @block.sync
        def _(sp):
            for i in range(2):
                load_head(sp, s, a, 0, i)

        @block.gpsimd
        def _(pool):
            pool.memset(s.neg, 0.0).then_inc(cst, 1)
            pool.memset(s.dup, 0.0).then_inc(cst, 1)
            pool.wait_ge(cst, 2)
            pool.affine_select(out=s.neg, in_=s.neg, compare_op=ALU.is_ge, fill=NEG, base=0, pattern=[[-1, P]],
                               channel_multiplier=1).then_inc(cst, 1)
            for n, base in enumerate((0, 64, -64)):
                pool.wait_ge(cst, 3 + n)
                pool.affine_select(out=s.dup, in_=s.dup, compare_op=ALU.not_equal, fill=1.0, base=base,
                                   pattern=[[-1, P]], channel_multiplier=1).then_inc(cst, 1)

        @block.tensor
        def _(pe):
            pe.wait_ge(w_in, 128)
            for k in range(KD):
                last = pe.matmul(g.bank[4][:, :], s.wr[:, k, :], g.hT[:, k, :], start=k == 0, stop=k == KD - 1)
            last.then_inc(mm, 1)
            for t in range(T):
                for k in range(KD):
                    last = pe.matmul(g.bank[t][:, 0:QL + KVL], g.hT[:, k, t * P:(t + 1) * P], s.wn[:, k, :],
                                     start=k == 0, stop=k == KD - 1)
                last.then_inc(mm, 1)
            pe.wait_ge(kd, 1)
            pe.wait_ge(cst, 6)
            pe.matmul(g.bank[5][:, :], s.dup, s.n, start=True, stop=True).then_inc(mm, 1)
            pe.wait_ge(nat, 2 * T)
            for n in range(3):
                for t in range(T):
                    src = s.qn[:, t, n::2] if n < 2 else s.ckv[:, t, :]
                    if n == 2 and t == 0:
                        pe.wait_ge(tpc, 1)
                    last = pe.transpose(g.bank[(6, 7, 4)[n]][:, t * P:(t + 1) * P], src, g.ident[:, :])
                last.then_inc(tp, 1)

        @block.scalar
        def _(act):
            act.wait_ge(ang, 10)
            act.activation(s.cs, s.ang, ACT.Sin).then_inc(tab, 1)
            for t in range(T):
                act.wait_ge(mm, 2 + t)
                act.activation(g.xn[:, t, 0:QL], g.bank[t][:, 0:QL], ACT.Square, accum_out=g.ss[:, t:t + 1]).then_inc(sq, 1)
                act.activation(g.xn[:, t, QL:QL + KVL], g.bank[t][:, QL:QL + KVL], ACT.Square,
                               accum_out=g.lnss[:, t:t + 1]).then_inc(sq, 1)
            act.wait_ge(sq, 2 * T)
            act.activation(g.rstd[:, :], g.ss[:, :], ACT.Ln, scale=1.0 / QL, bias=g.eps[:, 0:1]).then_inc(rs, 1)
            act.activation(g.ss2[:, :], g.lnss[:, :], ACT.Ln, scale=1.0 / KVL, bias=g.eps[:, 0:1]).then_inc(rs, 1)
            act.wait_ge(rs, 2)
            act.activation(g.ss[:, :], g.rstd[:, :], ACT.Exp, scale=-0.5).then_inc(rs, 1)
            act.activation(g.lnss[:, :], g.ss2[:, :], ACT.Exp, scale=-0.5).then_inc(rs, 1)

        @block.vector
        def _(dve):
            count = [0]

            def done(ins):
                count[0] += 1
                ins.then_inc(ang, 1)
                dve.wait_ge(ang, count[0])

            c1 = 6.28125
            c2 = float(np.float32(np.round((2 * np.pi - c1) * 2 ** 21) / 2 ** 21))
            c3 = 2 * np.pi - c1 - c2
            magic = 1.5 * 2 ** 23
            dve.wait_ge(w_in, 128)
            done(dve.tensor_copy(s.n, s.pos))
            done(dve.tensor_scalar(s.ang, s.n, s.cols[:, 0:1], None, ALU.mult))
            done(dve.tensor_scalar(s.n, s.ang, 1.0 / (2 * np.pi), s.cols[:, 1:2], ALU.mult, ALU.add))
            done(dve.tensor_scalar(s.n, s.n, magic, None, ALU.add))
            done(dve.tensor_scalar(s.n, s.n, -magic, None, ALU.add))
            for c in (c1, c2, c3):
                done(dve.scalar_tensor_tensor(out=s.ang, in0=s.n, scalar=-c, in1=s.ang, op0=ALU.mult, op1=ALU.add))
            done(dve.tensor_scalar(s.ang, s.ang, s.cols[:, 2:3], None, ALU.add))
            done(dve.tensor_scalar(s.ang, s.ang, 3.1415925, -3.1415925, ALU.min, ALU.max))
            dve.wait_ge(tab, 1)
            dve.wait_ge(mm, 1)
            dve.tensor_tensor(s.n, g.bank[4][:, :], s.cs, ALU.mult).then_inc(kd, 1)
            dve.wait_ge(rs, 4)
            for t in range(T):
                dve.tensor_scalar(s.qn[:, t, :], g.bank[t][:, 0:QL], g.ss[:, t:t + 1], None, ALU.mult).then_inc(nat, 1)
                dve.scalar_tensor_tensor(out=s.ckv[:, t, :], in0=g.bank[t][:, QL:QL + KVL], scalar=g.lnss[:, t:t + 1],
                                         in1=s.gkv, op0=ALU.mult, op1=ALU.mult).then_inc(nat, 1)
            dve.wait_ge(mm, 2 + T)
            dve.tensor_copy(s.kdup, g.bank[5][:, :]).then_inc(tpc, 1)
            for n in range(2):
                dve.wait_ge(tp, n + 1)
                dve.tensor_scalar(s.qaT[:, n, :], g.bank[6 + n][:, :], s.gq[:, n:n + 1], None, ALU.mult).then_inc(tpc, 1)
            dve.wait_ge(tp, 3)
            dve.tensor_copy(s.ckvT, g.bank[4][:, :]).then_inc(tpc, 1)


def load_mla_in(sp, s, a, w_in):
    w = a["mla_w_in"][0].rearrange("(p k) n -> p k n", k=KD)
    sp.dma_start(s.wn, w[:, :, 0:QL + KVL]).then_inc(w_in, 16)
    r = QL + KVL
    half = ROPE // 2
    sp.dma_start(s.wr[:, :, 0:ROPE], w[:, :, r:r + ROPE]).then_inc(w_in, 16)
    sp.dma_start(s.wr[:, :, ROPE:ROPE + half], w[:, :, r + half:r + ROPE]).then_inc(w_in, 16)
    sp.dma_start(s.wr[:, :, ROPE + half:], w[:, :, r:r + half]).then_inc(w_in, 16)
    sp.dma_start(s.pos, a["positions"][0].partition_broadcast(P)).then_inc(w_in, 16)
    sp.dma_start(s.gkv, a["mla_kv_norm_g"][0].partition_broadcast(P)).then_inc(w_in, 16)
    sp.dma_start(s.gq, a["mla_q_norm_g"][0].rearrange("(p k) -> p k", k=2)).then_inc(w_in, 16)
    sp.dma_start(s.cols[:, 0:3], a["rope_cols"]).then_inc(w_in, 16)


def load_head(sp, s, a, it, i, kv_free=None):
    h = s.h
    wq_d = a["mla_w_q_up"][0].rearrange("(p k) n -> p k n", k=2)
    half = ROPE // 2
    hd = 2 * it + i
    parts = ((0, QK, 0), (QK, half, NOPE + half), (QK + half, half, NOPE))
    for to, n, frm in parts:
        sp.dma_start(h.wq[i][:, :, to:to + n], wq_d[:, :, bass.ds(QK * hd + frm, n)]).then_inc(h.w_in[i], 16)
    if kv_free:
        sp.wait_ge(*kv_free)
    sp.dma_start(h.wkv[i], a["mla_w_kv_up"][0][:, bass.ds(256 * hd, 256)]).then_inc(h.w_in[i], 16)


def stage_mla_heads(nc, g, s, a, early_in):
    h = s.h
    tag = "mla"
    w_in = h.w_in
    S = {n: g.sem(f"{tag}_{n}") for n in
         "wuk wukT qn qnT qr rot qlat qlatT sc max nmax exp rinv pn pt pT_dve pT_act ol olT o oT".split()}
    oT = g.big[:, :].rearrange("p (h s) -> p h s", h=HEADS)
    with nc.Block() as block:
        @block.sync
        def _(sp):
            load_early_rows(sp, g, 0, a["mla_w_out"][0], early_in)
            with sp.Fori(1, HEADS // 2) as it:
                for i in range(2):
                    sp.wait_ge(S["qr"], 2 * it + i - 1)
                    load_head(sp, s, a, it, i, (S["o"], 2 * it + i - 1))

        def is_first(it, i):
            return isinstance(it, int) and it == 0 and i == 0

        @block.tensor
        def _(pe):
            def queries(it, i):
                n = 2 * it + i
                pe.wait_ge(w_in[i], 64 * (it + 1))
                if not is_first(it, i):
                    pe.wait_ge(S["qlatT"], n)
                pe.transpose(g.bank[4][:, 0:P], h.wkv[i][:, 0:NOPE], g.ident[:, :]).then_inc(S["wuk"], 1)
                for k in range(2):
                    last = pe.matmul(g.bank[5][:, :], h.wq[i][:, k, 0:NOPE], s.qaT[:, k, :], start=k == 0, stop=k == 1)
                last.then_inc(S["qn"], 1)
                if not is_first(it, i):
                    pe.wait_ge(S["rot"], n)
                for k in range(2):
                    last = pe.matmul(g.bank[6][:, :], h.wq[i][:, k, NOPE:], s.qaT[:, k, :], start=k == 0, stop=k == 1)
                last.then_inc(S["qr"], 1)
                pe.wait_ge(S["wukT"], n + 1)
                pe.wait_ge(S["qnT"], n + 1)
                pe.matmul(g.bank[4][:, :], h.wukT, h.qnT, start=True, stop=True).then_inc(S["qlat"], 1)

            def scores(it, i):
                n = 2 * it + i
                if not is_first(it, i):
                    pe.wait_ge(S["pT_dve"], 2 * n)
                    pe.wait_ge(S["pT_act"], n)
                pe.wait_ge(S["qlatT"], n + 1)
                pe.wait_ge(S["rot"], n + 1)
                for t in range(T):
                    keys, tok = (t + 1) * P, slice(t * P, (t + 1) * P)
                    if t == T - 1 and not is_first(it, i):
                        pe.wait_ge(S["olT"], n)
                    pe.matmul(g.bank[t][:, 0:keys], h.qlatT[:, tok], s.ckvT[:, 0:keys], start=True, stop=False)
                    pe.matmul(g.bank[t][:, 0:keys], h.rot[:, tok], s.kdup[:, 0:keys], start=False, stop=False)
                    pe.matmul(g.bank[t][:, tok], g.ident[:, :], s.neg, start=False, stop=True).then_inc(S["sc"], 1)
                    if t == 1 and not is_first(it, i):
                        output(it, i)

            def output(it, i):
                n = 2 * it + i - 1
                if not (isinstance(n, int) and n == 0):
                    pe.wait_ge(S["oT"], n)
                pe.wait_ge(S["olT"], n + 1)
                pe.matmul(g.bank[7][:, :], h.wkv[1 - i][:, NOPE:], h.olT, start=True, stop=True).then_inc(S["o"], 1)

            def values(it, i):
                n = 2 * it + i
                pe.wait_ge(S["pn"], T * (n + 1))
                for k in range(T):
                    b, at = min(k, 2), 0 if k < 3 else 2 * P
                    for t in range(k, T):
                        last = pe.transpose(g.bank[b][:, at + (t - k) * P:at + (t - k + 1) * P],
                                            h.p[t][:, k * P:(k + 1) * P], g.ident[:, :])
                    if k != 2:
                        last.then_inc(S["pt"], 1)
                for k in range(T):
                    if k < 2:
                        pe.wait_ge(S["pT_dve"], 2 * n + k + 1)
                    else:
                        pe.wait_ge(S["pT_act"], n + 1)
                    last = pe.matmul(g.bank[3][:, k * P:], s.ckv[:, k, :], h.pT[k], start=k == 0, stop=k == T - 1)
                last.then_inc(S["ol"], 1)

            queries(0, 0)
            scores(0, 0)
            queries(0, 1)
            values(0, 0)
            with pe.Fori(1, HEADS // 2) as it:
                scores(it - 1, 1)
                queries(it, 0)
                values(it - 1, 1)
                scores(it, 0)
                queries(it, 1)
                values(it, 0)
            scores(HEADS // 2 - 1, 1)
            values(HEADS // 2 - 1, 1)
            output(HEADS // 2, 0)

        @block.vector
        def _(dve):
            def key_weights(it, i):
                n = 2 * it + i
                dve.wait_ge(S["wuk"], n + 1)
                if not is_first(it, i):
                    dve.wait_ge(S["qlat"], n)
                dve.tensor_copy(h.wukT, g.bank[4][:, 0:P]).then_inc(S["wukT"], 1)

            def rotated(it, i):
                n = 2 * it + i
                dve.wait_ge(S["qr"], n + 1)
                if not is_first(it, i):
                    dve.wait_ge(S["sc"], T * n)
                dve.tensor_tensor(h.rot, g.bank[6][:, :], s.cs, ALU.mult).then_inc(S["rot"], 1)

            def maxima(it, i):
                n = 2 * it + i
                if not is_first(it, i):
                    dve.wait_ge(S["exp"], T * n)
                for t in range(T):
                    dve.wait_ge(S["sc"], T * n + t + 1)
                    dve.tensor_reduce(h.mx[:, t:t + 1], g.bank[t][:, 0:(t + 1) * P], AX, ALU.max).then_inc(S["max"], 1)
                    dve.wait_ge(S["max"], T * n + t + 1)
                    dve.tensor_scalar(h.nm[:, t:t + 1], h.mx[:, t:t + 1], -MLA_SCALE, None, ALU.mult).then_inc(S["nmax"], 1)

            def normalize(it, i):
                n = 2 * it + i
                for t in range(T):
                    dve.wait_ge(S["exp"], T * n + t + 1)
                    dve.reciprocal(h.ri[:, t:t + 1], h.rs[:, t:t + 1]).then_inc(S["rinv"], 1)
                    dve.wait_ge(S["rinv"], T * n + t + 1)
                    dve.tensor_scalar(h.p[t], h.p[t], h.ri[:, t:t + 1], None, ALU.mult).then_inc(S["pn"], 1)

            def turned(it, i):
                n = 2 * it + i
                if not is_first(it, i):
                    dve.wait_ge(S["ol"], n)
                for k in range(2):
                    dve.wait_ge(S["pt"], 3 * n + k + 1)
                    dve.tensor_copy(h.pT[k], g.bank[k][:, 0:(T - k) * P]).then_inc(S["pT_dve"], 1)

            def turn(it, i, following):
                maxima(it, i)
                if following:
                    key_weights(*following)
                normalize(it, i)
                if following:
                    rotated(*following)
                turned(it, i)

            key_weights(0, 0)
            rotated(0, 0)
            turn(0, 0, (0, 1))
            with dve.Fori(1, HEADS // 2) as it:
                turn(it - 1, 1, (it, 0))
                turn(it, 0, (it, 1))
            turn(HEADS // 2 - 1, 1, None)

        @block.scalar
        def _(act):
            def queries(it, i):
                n = 2 * it + i
                act.wait_ge(S["qn"], n + 1)
                if not is_first(it, i):
                    act.wait_ge(S["qlat"], n)
                act.activation(h.qnT, g.bank[5][:, :], ACT.Copy).then_inc(S["qnT"], 1)
                act.wait_ge(S["qlat"], n + 1)
                if not is_first(it, i):
                    act.wait_ge(S["sc"], T * n)
                act.activation(h.qlatT, g.bank[4][:, :], ACT.Copy).then_inc(S["qlatT"], 1)

            def output(it, i):
                n = 2 * it + i - 1
                act.wait_ge(S["o"], n + 1)
                act.activation(oT[:, bass.ds(n, 1), :], g.bank[7][:, :].unsqueeze(1), ACT.Copy).then_inc(S["oT"], 1)

            def head(it, i, following):
                n = 2 * it + i
                if not is_first(it, i):
                    act.wait_ge(S["pt"], 3 * n)
                for t in range(T):
                    act.wait_ge(S["nmax"], T * n + t + 1)
                    act.activation(h.p[t], g.bank[t][:, 0:(t + 1) * P], ACT.Exp, bias=h.nm[:, t:t + 1], scale=MLA_SCALE,
                                   accum_out=h.rs[:, t:t + 1]).then_inc(S["exp"], 1)
                if not is_first(it, i):
                    output(it, i)
                if following:
                    queries(*following)
                act.wait_ge(S["pt"], 3 * n + 3)
                for k in (2, 3):
                    at = 0 if k == 2 else 2 * P
                    if not is_first(it, i):
                        act.wait_ge(S["ol"], n)
                    last = act.activation(h.pT[k], g.bank[2][:, at:at + (T - k) * P], ACT.Copy)
                last.then_inc(S["pT_act"], 1)
                act.wait_ge(S["ol"], n + 1)
                if not is_first(it, i):
                    act.wait_ge(S["o"], n)
                act.activation(h.olT, g.bank[3][:, :], ACT.Copy).then_inc(S["olT"], 1)

            queries(0, 0)
            head(0, 0, (0, 1))
            with act.Fori(1, HEADS // 2) as it:
                head(it - 1, 1, (it, 0))
                head(it, 0, (it, 1))
            head(HEADS // 2 - 1, 1, None)
            output(HEADS // 2, 0)


EARLY = 4


def early_rows(g, buf):
    return g.w[:, buf, 0:EARLY * D].rearrange("p (s d) -> p s d", d=D)


def load_early_rows(sp, g, buf, w_dram, signal):
    sp.dma_start(early_rows(g, buf), w_dram[0:EARLY * P, :].rearrange("(s p) d -> p s d", p=P)).then_inc(signal, 16)


def stage_out(nc, g, tag, w_dram, early, early_in, sync_work=None):
    NS = HEADS - EARLY
    slots = g.w[:, 2:4, :].rearrange("p n (s d) -> p (n s) d", d=D)
    w_in = [g.sem(f"{tag}_w_in{i}") for i in range(NS)]
    squares = g.sem(tag + "_squares")
    used, mm, add = g.sem(tag + "_w_used"), g.sem(tag + "_products"), g.sem(tag + "_added")
    oT = g.big[:, :].rearrange("p (h s) -> p h s", h=HEADS)
    with nc.Block() as block:
        @block.sync
        def _(sp):
            for k in range(NS):
                head = EARLY + k
                sp.dma_start(slots[:, k, :], w_dram[head * P:(head + 1) * P, :]).then_inc(w_in[k], 16)
            if sync_work:
                sp.wait_ge(used, EARLY)
                sync_work(sp)

        @block.tensor
        def _(pe):
            for k in range(HEADS):
                w = early_rows(g, early)[:, k, :] if k < EARLY else slots[:, k - EARLY, :]
                pe.wait_ge(early_in if k < EARLY else w_in[k - EARLY], 16)
                for t in range(T):
                    for n in range(2):
                        last = pe.matmul(g.bank[2 * t + n][:, :], oT[:, k, t * P:(t + 1) * P],
                                         w[:, 512 * n:512 * (n + 1)], start=k == 0, stop=k == HEADS - 1)
                        if k == HEADS - 1:
                            last.then_inc(mm, 1)
                if k < HEADS - 1:
                    last.then_inc(used, 1)

        @block.vector
        def _(dve):
            for b in range(2 * T):
                dve.wait_ge(mm, b + 1)
                xv = g.x[:, b // 2, 512 * (b % 2):512 * (b % 2) + 512]
                dve.tensor_tensor(xv, g.bank[b][:, :], xv, ALU.add).then_inc(add, 1)

        @block.scalar
        def _(act):
            for t in range(T):
                act.wait_ge(add, 2 * t + 2)
                square_sums(act, g, t, g.hT[:, :, :].rearrange("p k s -> p (k s)"), squares)



K_HEADS, V_HEADS = 8, 16
CONV = 4
QKW, VW = K_HEADS * P, V_HEADS * P
LEVELS = 7
BETA, NBETA, G, GLOG, BEG = range(5)
(PQ, PK, PV0, PV1, PZ0, PZ1) = range(6)


def gdn_memory(nc, ctx, g):
    s = Memory()
    parts = [workspace(g, 0, 1), workspace(g, 2, 2)]
    left = [GU + DN, 2 * (GU + DN)]

    def tile():
        i = 0 if left[0] >= SEQ else 1
        left[i] -= SEQ
        return parts[i](T, P)
    s.c = [tile() for _ in range(4)]
    s.zn = [tile() for _ in range(2)]
    s.zw = [tile() for _ in range(2)]
    s.qT, s.kT, s.kn = tile(), tile(), tile()
    s.vb, s.kbg, s.kout, s.E, s.eG, s.QKT, s.qin, s.A, s.TT, s.W, s.vn = (
        [tile() for _ in range(2)] for _ in range(11))
    s.Tm = s.eG
    s.Wc = [w.rearrange("p t i -> p (t i)")[:, 0:T * P // 2].rearrange("p (t i) -> p t i", t=T) for w in s.W]
    w = workspace(g, 1, 1)
    s.wq, s.wk, s.wv, s.wz = w(KD, P), w(KD, P), w(KD, 2 * P), w(KD, 2 * P)

    def sb(name, *shape):
        return ctx.enter_context(nc.sbuf_tensor(name, [P, *shape], F32))
    s.tab = sb("gdn_tab", V_HEADS, 5, T)
    s.st = sb("gdn_tab_now", 2, 5, T)
    s.cw = sb("gdn_conv_w", 32, CONV)
    s.cws = sb("gdn_conv_w_now", 4, CONV)
    s.S = [sb(f"gdn_state{i}", P) for i in range(2)]
    s.ge = [sb(f"gdn_end_decay{i}", T) for i in range(2)]
    s.gcol = sb("gdn_gain", 1)
    s.lm = sb("level_masks", LEVELS, P // 2)
    f = g.big[:, 4096:8192]
    s.gates_in = g.sem("gates_in")
    s.w_in = [g.sem(f"gd_w_in{i}") for i in range(4)]
    s.wba, s.cwr = f[:, 0:256].rearrange("p (k n) -> p k n", k=KD), f[:, 256:384]
    s.dt, s.al = f[:, 384:400], f[:, 400:416]
    s.xa, s.ab, s.sp, s.gl = (f[:, 512 + 64 * i:576 + 64 * i].rearrange("p (t h) -> p t h", t=T) for i in range(4))
    s.bt, s.Gc, s.eGc = (f[:, 768 + 64 * i:832 + 64 * i].rearrange("p (t h) -> p t h", t=T) for i in range(3))
    return s


def load_gates(sp, s, a):
    w_in = s.gates_in
    w = a["gdn_w_in"][0].rearrange("(p k) n -> p k n", k=KD)
    sp.dma_start(s.wba, w[:, :, 2 * QKW + 2 * VW:]).then_inc(w_in, 16)
    sp.dma_start(s.cwr, a["gdn_conv_w"][0].rearrange("c (n p) -> (c n) p", p=P)).then_inc(w_in, 16)
    sp.dma_start(s.dt, a["gdn_dt_bias"][0].partition_broadcast(P)).then_inc(w_in, 16)
    sp.dma_start(s.al, a["gdn_a_log"][0].partition_broadcast(P)).then_inc(w_in, 16)
    sp.dma_start(s.gcol[:, :], a["gdn_norm_g"][0].rearrange("(p o) -> p o", o=1)).then_inc(w_in, 16)


def load_delta(sp, s, a, part, kh):
    w_d = a["gdn_w_in"][0].rearrange("(p k) n -> p k n", k=KD)
    dst, base, n = ((s.wq, 0, P), (s.wk, QKW, P), (s.wv, 2 * QKW, 2 * P), (s.wz, 2 * QKW + VW, 2 * P))[part]
    sp.dma_start(dst, w_d[:, :, bass.ds(base + n * kh, n)]).then_inc(s.w_in[part], 16)


def gates_programs(nc, g, s):
    tag = "gates"
    proj, act_s, dve_s, run = g.sem(tag + "_products"), g.sem(tag + "_act"), g.sem(tag + "_dve"), g.sem(tag + "_sums")
    lm = g.sem(tag + "_masks")
    ba = g.bank[5][:, 0:128].rearrange("p (t c h) -> p t c h", t=T, c=2)

    def masks(pool):
        pool.memset(s.lm[:, :, :], 1.0).then_inc(lm, 1)
        for lv in range(LEVELS):
            b = 1 << lv
            mask = s.lm[:, lv, :].rearrange("p (n c) -> p n c", c=b)
            pairs = P // (2 * b)
            pool.wait_ge(lm, 2 * lv + 1)
            pool.affine_select(out=mask, in_=mask, compare_op=ALU.is_ge, fill=0.0, base=0,
                               pattern=[[-2 * b, pairs], [0, b]], channel_multiplier=1).then_inc(lm, 1)
            pool.wait_ge(lm, 2 * lv + 2)
            pool.affine_select(out=mask, in_=mask, compare_op=ALU.is_ge, fill=0.0, base=b - 1,
                               pattern=[[2 * b, pairs], [0, b]], channel_multiplier=-1).then_inc(lm, 1)

    def products(pe):
        pe.wait_ge(s.gates_in, 80)
        for t in range(T):
            for k in range(KD):
                last = pe.matmul(g.bank[5][:, 32 * t:32 * t + 32], g.hT[:, k, t * P:(t + 1) * P], s.wba[:, k, :],
                                 start=k == 0, stop=k == KD - 1)
        last.then_inc(proj, 1)
        pe.transpose(g.bank[6][:, 0:P], s.cwr, g.ident[:, :]).then_inc(proj, 1)

    def running_sums(pe):
        pe.wait_ge(dve_s, 4)
        pe.matmul(g.bank[7][:, 0:T * V_HEADS], g.tri[:, :], s.gl.rearrange("p t h -> p (t h)"),
                  start=True, stop=True).then_inc(proj, 1)

    def scalar_part(act):
        act.wait_ge(proj, 1)
        act.activation(s.bt, ba[:, :, 0, :], ACT.Sigmoid).then_inc(act_s, 1)
        act.activation(s.al, s.al, ACT.Exp).then_inc(act_s, 1)
        act.wait_ge(dve_s, 1)
        act.activation(s.ab, s.xa, ACT.Abs).then_inc(act_s, 1)
        act.wait_ge(act_s, 3)
        act.activation(s.sp, s.ab, ACT.Exp, scale=-1.0).then_inc(act_s, 1)
        act.wait_ge(act_s, 4)
        act.activation(s.sp, s.sp, ACT.Ln, bias=g.ones[:, 0:1]).then_inc(act_s, 1)

    def scalar_end(act):
        act.wait_ge(dve_s, 6)
        act.activation(s.eGc, s.Gc, ACT.Exp).then_inc(act_s, 1)

    count = [0]

    def done(dve, ins):
        count[0] += 1
        ins.then_inc(dve_s, 1)
        dve.wait_ge(dve_s, count[0])

    def vector_part(dve):
        def bc(v):
            return v.unsqueeze(1).to_broadcast([P, T, V_HEADS])
        dve.wait_ge(s.gates_in, 80)
        dve.wait_ge(act_s, 1)
        done(dve, dve.tensor_tensor(s.xa, ba[:, :, 1, :], bc(s.dt), ALU.add))
        dve.wait_ge(act_s, 5)
        done(dve, dve.scalar_tensor_tensor(out=s.gl, in0=s.xa, scalar=0.0, in1=s.sp, op0=ALU.max, op1=ALU.add))
        done(dve, dve.tensor_tensor(s.gl, s.gl, bc(s.al), ALU.mult))
        done(dve, dve.tensor_scalar(s.gl, s.gl, -1.0, None, ALU.mult))
        dve.wait_ge(proj, 2)
        done(dve, dve.tensor_copy(s.cw[:, :, :], g.bank[6][:, 0:P].rearrange("p (c n) -> p n c", c=CONV)))

    def vector_end(dve):
        dve.wait_ge(proj, 3)
        done(dve, dve.tensor_copy(s.Gc, g.bank[7][:, 0:T * V_HEADS].rearrange("p (t h) -> p t h", t=T)))
        dve.wait_ge(act_s, 6)

        def put(n, v):
            return dve.tensor_copy(s.tab[:, :, n, :], v.rearrange("p t h -> p h t"))
        done(dve, put(BETA, s.bt))
        done(dve, put(G, s.Gc))
        done(dve, put(GLOG, s.gl))
        done(dve, dve.tensor_scalar(s.tab[:, :, NBETA, :], s.tab[:, :, BETA, :], -1.0, None, ALU.mult))
        done(dve, dve.tensor_tensor(s.tab[:, :, BEG, :], s.bt.rearrange("p t h -> p h t"),
                               s.eGc.rearrange("p t h -> p h t"), ALU.mult))
        dve.wait_ge(lm, 2 * LEVELS + 1)

    programs = Memory()
    programs.masks, programs.products, programs.running_sums = masks, products, running_sums
    programs.scalar_part, programs.scalar_end = scalar_part, scalar_end
    programs.vector_part, programs.vector_end = vector_part, vector_end
    return programs


def stage_delta(nc, g, s, a, early_in):
    S = {n: g.sem("gd_" + n) for n in
         ("squares norms_sum norms qk v_turned tables decay_rhs decay_bc v_beta decay_diff exp_diff exp_G k_turned kk kq "
          "k_nat k_beta k_out A_raw A QKT_raw QKT q_in end_decay z_now TT_is_I TT first_product W YT T_turned T "
          "w_product w_neg v_product v_new o state_product state o_squares o_sums o_rstd o_normed o_gated "
          "projected conv_step silu z_next conv_w").split()}
    gates = gates_programs(nc, g, s)
    w_in = s.w_in
    oT = g.big[:, :].rearrange("p (h t i) -> p h t i", h=V_HEADS, t=T)
    bank = [b[:, :].rearrange("p (t i) -> p t i", t=T) for b in g.bank]
    LAST = K_HEADS - 1

    def wait(eng, name, per, it, n):
        eng.wait_ge(S[name], per * it + n)

    def first(it):
        return isinstance(it, int) and it == 0

    def cols(v):
        return v.unsqueeze(2).to_broadcast([P, T, P])

    def rows(v):
        return v.unsqueeze(1).to_broadcast([P, T, P])

    def rows2(v):
        return v.unsqueeze(1).to_broadcast([P, T, P // 2])

    def weights(tile):
        return (s.wq[:, :, :], s.wk[:, :, :], s.wv[:, :, 0:P], s.wv[:, :, P:], s.wz[:, :, 0:P], s.wz[:, :, P:])[tile]

    def odd(v, lv, t=slice(None)):
        return v[:, t, :].rearrange("p t (n h c) -> p t n h c" if isinstance(t, slice) else "p (n h c) -> p n h c",
                                    h=2, c=1 << lv)[..., 1, :]

    def blocks_of(v, lv):
        return v.rearrange("p t (n c) -> p t n c", c=1 << lv)

    FILL = [4, 4, 2, 2] + [3] * (2 * LEVELS - 2)
    assert sum(FILL) == 6 * KD
    with nc.Block() as block:
        @block.sync
        def _(sp):
            with sp.Fori(1, K_HEADS) as kh:
                for part, used in enumerate((1, 2, 4, 6)):
                    sp.wait_ge(S["projected"], 6 * (kh - 1) + used)
                    load_delta(sp, s, a, part, kh)
            sp.wait_ge(S["projected"], 6 * K_HEADS)
            load_early_rows(sp, g, 1, a["gdn_w_out"][0], early_in)

        @block.tensor
        def _(pe):
            def project(n, tile, ks):
                if 0 in ks:
                    pe.wait_ge(w_in[(0, 1, 2, 2, 3, 3)[tile]], 16 * (n + 1))
                    if tile >= 2:
                        wait(pe, "conv_step", 16, n, 4 * (tile - 1))
                    elif not first(n):
                        wait(pe, "z_next", 2, n - 1, tile + 1)
                for k in ks:
                    last = pe.matmul(g.bank[tile % 2][:, :], weights(tile)[:, k, :], g.hT[:, k, :],
                                     start=k == 0, stop=k == KD - 1)
                if KD - 1 in ks:
                    last.then_inc(S["projected"], 1)

            def each(out, lhs, rhs, transposed=False):
                for t in range(T):
                    if transposed:
                        last = pe.transpose(out[:, t, :], lhs[:, t, :], g.ident[:, :])
                    else:
                        last = pe.matmul(out[:, t, :], lhs[:, t, :], rhs[:, t, :], start=True, stop=True)
                return last

            def flat(v):
                return v.rearrange("p t i -> p (t i)")

            def norms_sums(n):
                for i in range(2):
                    wait(pe, "squares", 2, n, i + 1)
                    if not first(n):
                        wait(pe, "state", 6, n - 1, 5 + i)
                    pe.matmul(g.bank[5 + 2 * i][:, :], g.ones[:, :], flat(s.E[i]), start=True, stop=True)\
                        .then_inc(S["norms_sum"], 1)

            def head_pair(it, more):
                n = it + 1

                def fill(slot):
                    if more:
                        for step in range(sum(FILL[:slot]), sum(FILL[:slot + 1])):
                            project(n, step // KD, (step % KD,))

                fill(0)
                for i in range(2):
                    wait(pe, "silu", 4, it, 3 + i)
                    if not first(it):
                        wait(pe, "o_rstd", 4, it - 1, 2)
                    each(bank[2 + i], s.c[2 + i], None, True).then_inc(S["v_turned"], 1)
                for i in range(2):
                    wait(pe, "decay_rhs", 2, it, i + 1)
                    wait(pe, "norms", 4, it, i + 1)
                    pe.matmul(g.bank[5 + 2 * i][:, :], g.ones[:, :], flat(s.W[i]), start=True, stop=True)\
                        .then_inc(S["decay_bc"], 1)
                wait(pe, "qk", 2, it, 2)
                if not first(it):
                    wait(pe, "o_normed", 2, it - 1, 2)
                each(bank[4], s.kT, None, True).then_inc(S["k_turned"], 1)
                each(bank[6], s.kT, s.kT).then_inc(S["kk"], 1)
                wait(pe, "v_beta", 2, it, 1)
                each(bank[2], s.kT, s.qT).then_inc(S["kq"], 1)
                fill(1)
                for lv in range(LEVELS):
                    for i in range(2):
                        wait(pe, "TT", 14, it, 2 * (lv - 1) + i + 1) if lv else wait(pe, "TT_is_I", 2, it, i + 1)
                        if lv == 0:
                            wait(pe, "A", 2, it, i + 1)
                            if i == 0:
                                wait(pe, "QKT_raw", 2, it, 2)
                            else:
                                wait(pe, "v_beta", 2, it, 2)
                        else:
                            if lv == 1:
                                wait(pe, "exp_G", 2, it, 2)
                                wait(pe, "k_nat", 1, it, 1)
                            else:
                                wait(pe, "T", 12, it, 2 * (lv - 2) + i + 1)
                            each(bank[4 + 2 * i], s.TT[i], None, True).then_inc(S["T_turned"], 1)
                            wait(pe, "W", 14, it, 2 * (lv - 1) + i + 1)
                        for t in range(T):
                            last = pe.matmul(g.bank[2 + i][:, 64 * t:64 * (t + 1)].rearrange("p (n c) -> p n c", c=1 << lv),
                                             s.A[i][:, t, :], odd(s.TT[i], lv, t), start=True, stop=True)
                        last.then_inc(S["first_product"], 1)
                    fill(2 + 2 * lv)
                    if lv:
                        for i in range(2):
                            wait(pe, "W", 14, it, 2 * lv + i + 1)
                            wait(pe, "T", 12, it, 2 * (lv - 1) + i + 1)
                            for t in range(T):
                                last = pe.matmul(g.bank[5 + 2 * i][:, 64 * t:64 * (t + 1)], s.Tm[i][:, t, :],
                                                 s.Wc[i][:, t, :], start=True, stop=True)
                            last.then_inc(S["YT"], 1)
                    fill(3 + 2 * lv)
                for i in range(2):
                    wait(pe, "TT", 14, it, 2 * (LEVELS - 1) + i + 1)
                    wait(pe, "k_beta", 2, it, i + 1)
                    each(bank[2 + i], s.kbg[i], s.TT[i]).then_inc(S["w_product"], 1)
                for c in range(T):
                    for i in range(2):
                        if c == 0:
                            wait(pe, "w_neg", 2, it, i + 1)
                        else:
                            wait(pe, "v_new", 8, it, 2 * (c - 1) + i + 1)
                        last = pe.matmul(bank[2 + i][:, c, :], s.TT[i][:, c, :], s.vb[i][:, c, :], start=True, stop=c == 0)
                        if c > 0:
                            wait(pe, "state", 6, it, 2 * (c - 1) + i + 1)
                            last = pe.matmul(bank[2 + i][:, c, :], s.W[i][:, c, :], s.S[i][:, :], start=False, stop=True)
                        last.then_inc(S["v_product"], 1)
                    for i in range(2):
                        if c == 0:
                            wait(pe, "q_in", 2, it, i + 1)
                            wait(pe, "QKT", 2, it, i + 1)
                            wait(pe, "k_out", 2, it, i + 1)
                            wait(pe, "T", 12, it, 10 + i + 1)
                        if c > 0:
                            pe.matmul(bank[4 + 2 * i][:, c, :], s.S[i][:, :], s.qin[i][:, c, :], start=True, stop=False)
                        wait(pe, "v_new", 8, it, 2 * c + i + 1)
                        pe.matmul(bank[4 + 2 * i][:, c, :], s.vn[i][:, c, :], s.QKT[i][:, c, :], start=c == 0, stop=True)\
                            .then_inc(S["o"], 1)
                        if c < T - 1:
                            pe.matmul(bank[5 + 2 * i][:, 0, :], s.kout[i][:, c, :], s.vn[i][:, c, :], start=True, stop=True)\
                                .then_inc(S["state_product"], 1)
                if more:
                    norms_sums(n)
                for i in range(2):
                    wait(pe, "o_squares", 2, it, i + 1)
                    wait(pe, "v_new", 8, it, 7 + i)
                    pe.matmul(g.bank[2 + i][:, :], g.ones[:, :], flat(s.W[i]), start=True, stop=True)\
                        .then_inc(S["o_sums"], 1)

            gates.products(pe)
            project(0, 0, range(KD))
            gates.running_sums(pe)
            for tile in range(1, 6):
                project(0, tile, range(KD))
            norms_sums(0)
            head_pair(0, True)
            with pe.Fori(1, LAST) as it:
                head_pair(it, True)
            head_pair(LAST, False)

        @block.vector
        def _(dve):
            def conv(n, tile):
                c = s.c[tile].rearrange("p t i -> p (t i)")
                wait(dve, "projected", 6, n, tile + 1)
                if tile == 0:
                    wait(dve, "conv_w", 3, n, 3)
                if not first(n):
                    if tile < 2:
                        wait(dve, "squares", 2, n - 1, tile + 1)
                        wait(dve, "qk", 2, n - 1, tile + 1)
                    else:
                        wait(dve, "v_turned", 2, n - 1, tile - 1)
                src, cw = g.bank[tile % 2], s.cws[:, tile, :]
                dve.tensor_scalar(c, src[:, :], cw[:, CONV - 1:CONV], None, ALU.mult).then_inc(S["conv_step"], 1)
                for lag in range(1, CONV):
                    wait(dve, "conv_step", 16, n, 4 * tile + lag)
                    dve.scalar_tensor_tensor(out=c[:, lag:], in0=src[:, 0:SEQ - lag], scalar=cw[:, CONV - 1 - lag:CONV - lag],
                                             in1=c[:, lag:], op0=ALU.mult, op1=ALU.add).then_inc(S["conv_step"], 1)

            def conv_weights(n):
                if not first(n):
                    wait(dve, "conv_step", 16, n - 1, 16)
                dve.tensor_copy(s.cws[:, 0:1, :], s.cw[:, bass.ds(n, 1), :]).then_inc(S["conv_w"], 1)
                dve.tensor_copy(s.cws[:, 1:2, :], s.cw[:, bass.ds(K_HEADS + n, 1), :]).then_inc(S["conv_w"], 1)
                dve.tensor_copy(s.cws[:, 2:4, :], s.cw[:, bass.ds(2 * K_HEADS + 2 * n, 2), :]).then_inc(S["conv_w"], 1)

            def tables(n):
                if not first(n):
                    wait(dve, "k_beta", 2, n - 1, 2)
                    wait(dve, "decay_rhs", 2, n - 1, 2)
                dve.tensor_copy(s.st[:, :, :, :], s.tab[:, bass.ds(2 * n, 2), :, :]).then_inc(S["tables"], 1)

            def head_pair(it, more):
                n = it + 1
                if more:
                    conv_weights(n)
                wait(dve, "tables", 1, it, 1)
                for i in range(2):
                    wait(dve, "v_turned", 2, it, i + 1)
                    dve.tensor_tensor(s.vb[i], bank[2 + i], cols(s.st[:, i, BETA, :]), ALU.mult).then_inc(S["v_beta"], 1)
                wait(dve, "norms", 4, it, 4)
                dve.scalar_tensor_tensor(out=s.qT.rearrange("p t i -> p (t i)"), in0=s.c[PQ].rearrange("p t i -> p (t i)"),
                                         scalar=float(P) ** -0.5, in1=s.eG[0].rearrange("p t i -> p (t i)"),
                                         op0=ALU.mult, op1=ALU.mult).then_inc(S["qk"], 1)
                dve.tensor_tensor(s.kT, s.c[PK], s.eG[1], ALU.mult).then_inc(S["qk"], 1)
                for i in range(2):
                    wait(dve, "decay_bc", 2, it, i + 1)
                    wait(dve, "norms_sum", 2, it, i + 1)
                    dve.tensor_tensor(s.E[i], bank[5 + 2 * i], cols(s.st[:, i, G, :]), ALU.subtract)\
                        .then_inc(S["decay_diff"], 1)
                wait(dve, "k_turned", 1, it, 1)
                if not first(it):
                    wait(dve, "k_out", 2, it - 1, 2)
                dve.tensor_copy(s.kn, bank[4]).then_inc(S["k_nat"], 1)
                for i in range(2):
                    wait(dve, "kk", 1, it, 1)
                    wait(dve, "exp_diff", 4, it, 2 * i + 2)
                    dve.tensor_tensor(s.A[i], bank[6], s.E[i], ALU.mult).then_inc(S["A_raw"], 1)
                for i in range(2):
                    wait(dve, "kq", 1, it, 1)
                    if not first(it):
                        wait(dve, "o", 8, it - 1, 7 + i)
                    dve.tensor_tensor(s.QKT[i], bank[2], s.E[i], ALU.mult).then_inc(S["QKT_raw"], 1)
                    wait(dve, "A_raw", 2, it, i + 1)
                    dve.tensor_tensor(s.A[i], s.A[i], cols(s.st[:, i, NBETA, :]), ALU.mult).then_inc(S["A"], 1)
                for lv in range(LEVELS):
                    for i in range(2):
                        wait(dve, "first_product", 14, it, 2 * lv + i + 1)
                        dve.tensor_tensor(s.Wc[i], g.bank[2 + i][:, 0:256].rearrange("p (t i) -> p t i", t=T),
                                          rows2(s.lm[:, lv, :]), ALU.mult).then_inc(S["W"], 1)
                    if more and lv in (1, 2, 3, 5):
                        conv(n, (1, 2, 3, 5).index(lv))
                    for i in range(2):
                        if lv == 0:
                            wait(dve, "W", 14, it, i + 1)
                            step = blocks_of(s.Wc[i], lv)
                        else:
                            wait(dve, "YT", 12, it, 2 * (lv - 1) + i + 1)
                            wait(dve, "TT", 14, it, 2 * (lv - 1) + i + 1)
                            step = blocks_of(g.bank[5 + 2 * i][:, 0:256].rearrange("p (t i) -> p t i", t=T), lv)
                        dve.tensor_tensor(odd(s.TT[i], lv), step, odd(s.TT[i], lv), ALU.add).then_inc(S["TT"], 1)
                for c in range(T - 1):
                    for i in range(2):
                        wait(dve, "state_product", 6, it, 2 * c + i + 1)
                        if c == 0:
                            dve.tensor_copy(s.S[i][:, :], bank[5 + 2 * i][:, 0, :]).then_inc(S["state"], 1)
                        else:
                            wait(dve, "state", 6, it, 2 * (c - 1) + i + 1)
                            wait(dve, "end_decay", 2, it, i + 1)
                            dve.scalar_tensor_tensor(out=s.S[i][:, :], in0=s.S[i][:, :], scalar=s.ge[i][:, c:c + 1],
                                                     in1=bank[5 + 2 * i][:, 0, :], op0=ALU.mult, op1=ALU.add)\
                                .then_inc(S["state"], 1)
                if more:
                    tables(n)
                for i in range(2):
                    wait(dve, "o_rstd", 4, it, i + 3)
                    dve.scalar_tensor_tensor(out=s.vn[i].rearrange("p t i -> p (t i)"), in0=g.bank[4 + 2 * i][:, :],
                                             scalar=s.gcol[:, 0:1], in1=s.A[i].rearrange("p t i -> p (t i)"),
                                             op0=ALU.mult, op1=ALU.mult).then_inc(S["o_normed"], 1)
                    wait(dve, "o_normed", 2, it, i + 1)
                    wait(dve, "z_now", 2, it, i + 1)
                    dve.tensor_tensor(oT[:, bass.ds(2 * it + i, 1)], s.vn[i].unsqueeze(1), s.zw[i].unsqueeze(1), ALU.mult)\
                        .then_inc(S["o_gated"], 1)

            gates.vector_part(dve)
            conv_weights(0)
            conv(0, 0)
            gates.vector_end(dve)
            for tile in range(1, 4):
                conv(0, tile)
            tables(0)
            head_pair(0, True)
            with dve.Fori(1, LAST) as it:
                head_pair(it, True)
            head_pair(LAST, False)

        @block.scalar
        def _(act):
            def silu_conv(n, tile):
                wait(act, "conv_step", 16, n, 4 * tile + 4)
                act.activation(s.c[tile], s.c[tile], ACT.Silu).then_inc(S["silu"], 1)

            def squares(n):
                for i in range(2):
                    wait(act, "silu", 4, n, i + 1)
                    if not first(n):
                        wait(act, "QKT_raw", 2, n - 1, i + 1)
                        wait(act, "k_out", 2, n - 1, i + 1)
                    act.activation(s.E[i], s.c[i], ACT.Square).then_inc(S["squares"], 1)

            def silu_z(n, i):
                wait(act, "projected", 6, n, 5 + i)
                if not first(n):
                    wait(act, "z_now", 2, n - 1, i + 1)
                act.activation(s.zn[i], bank[i], ACT.Silu).then_inc(S["z_next"], 1)

            def norms_ln(n):
                for i in range(2):
                    wait(act, "norms_sum", 2, n, i + 1)
                    if not first(n):
                        wait(act, "YT", 12, n - 1, 11 + i)
                    act.activation(s.eG[i], bank[5 + 2 * i], ACT.Ln, bias=g.eps[:, 0:1]).then_inc(S["norms"], 1)

            def norms_exp(n):
                for i in range(2):
                    wait(act, "norms", 4, n, i + 1)
                    act.activation(s.eG[i], s.eG[i], ACT.Exp, scale=-0.5).then_inc(S["norms"], 1)

            def head_pair(it, more):
                n = it + 1
                for i in range(2):
                    wait(act, "decay_diff", 2, it, i + 1)
                    act.activation(s.E[i], s.E[i], ACT.Abs).then_inc(S["exp_diff"], 1)
                    wait(act, "exp_diff", 4, it, 2 * i + 1)
                    act.activation(s.E[i], s.E[i], ACT.Exp, scale=-1.0).then_inc(S["exp_diff"], 1)
                    wait(act, "qk", 2, it, 2)
                    act.activation(s.eG[i], bank[5 + 2 * i], ACT.Exp).then_inc(S["exp_G"], 1)
                for lv in range(1, LEVELS):
                    for i in range(2):
                        wait(act, "T_turned", 12, it, 2 * (lv - 1) + i + 1)
                        if lv == 1:
                            wait(act, "q_in", 2, it, i + 1)
                            wait(act, "end_decay", 2, it, i + 1)
                        else:
                            wait(act, "YT", 12, it, 2 * (lv - 2) + i + 1)
                        act.activation(s.Tm[i], bank[4 + 2 * i], ACT.Copy).then_inc(S["T"], 1)
                    if more and lv in (2, 3, 4, 6):
                        silu_conv(n, (2, 3, 4, 6).index(lv))
                    if more and lv == 6:
                        silu_z(n, 0)
                if more:
                    silu_z(n, 1)
                    squares(n)
                for i in range(2):
                    wait(act, "w_product", 2, it, i + 1)
                    act.activation(s.W[i], bank[2 + i], ACT.Copy, scale=-1.0).then_inc(S["w_neg"], 1)
                for c in range(T):
                    for i in range(2):
                        wait(act, "v_product", 8, it, 2 * c + i + 1)
                        if c == 0 and not first(it):
                            wait(act, "o_gated", 2, it - 1, i + 1)
                        act.activation(s.vn[i][:, c, :], bank[2 + i][:, c, :], ACT.Copy).then_inc(S["v_new"], 1)
                for i in range(2):
                    wait(act, "o", 8, it, 7 + i)
                    act.activation(s.W[i], bank[4 + 2 * i], ACT.Square).then_inc(S["o_squares"], 1)
                for i in range(2):
                    wait(act, "o_sums", 2, it, i + 1)
                    act.activation(s.A[i], bank[2 + i], ACT.Ln, scale=1.0 / P, bias=g.eps[:, 0:1]).then_inc(S["o_rstd"], 1)
                if more:
                    norms_ln(n)
                for i in range(2):
                    wait(act, "o_rstd", 4, it, i + 1)
                    act.activation(s.A[i], s.A[i], ACT.Exp, scale=-0.5).then_inc(S["o_rstd"], 1)
                if more:
                    norms_exp(n)

            gates.scalar_part(act)
            gates.scalar_end(act)
            for tile in range(4):
                silu_conv(0, tile)
            for i in range(2):
                silu_z(0, i)
            squares(0)
            norms_ln(0)
            norms_exp(0)
            head_pair(0, True)
            with act.Fori(1, LAST) as it:
                head_pair(it, True)
            head_pair(LAST, False)

        @block.gpsimd
        def _(pool):
            def head_pair(it):
                for i in range(2):
                    wait(pool, "tables", 1, it, 1)
                    if not first(it):
                        wait(pool, "o_sums", 2, it - 1, i + 1)
                    pool.tensor_tensor(s.W[i], rows(g.tri[:, :]), cols(s.st[:, i, GLOG, :]), ALU.mult)\
                        .then_inc(S["decay_rhs"], 1)
                for i in range(2):
                    if not first(it):
                        wait(pool, "v_product", 8, it - 1, 7 + i)
                    pool.tensor_tensor(s.TT[i], rows(g.ident[:, :]), rows(g.ones[:, :]), ALU.mult).then_inc(S["TT_is_I"], 1)
                for i in range(2):
                    wait(pool, "exp_G", 2, it, i + 1)
                    wait(pool, "qk", 2, it, 1)
                    pool.tensor_tensor(s.qin[i], s.qT, s.eG[i], ALU.mult).then_inc(S["q_in"], 1)
                    pool.tensor_copy(s.ge[i][:, :], s.eG[i][:, :, P - 1]).then_inc(S["end_decay"], 1)
                for i in range(2):
                    if not first(it):
                        wait(pool, "w_product", 2, it - 1, i + 1)
                    wait(pool, "k_nat", 1, it, 1)
                    wait(pool, "exp_diff", 4, it, 2 * i + 2)
                    pool.tensor_tensor(s.kout[i], s.kn, s.E[i][:, :, P - 1:P].to_broadcast([P, T, P]), ALU.mult)\
                        .then_inc(S["k_out"], 1)
                for i in range(2):
                    wait(pool, "z_next", 2, it, i + 1)
                    if not first(it):
                        wait(pool, "o_gated", 2, it - 1, i + 1)
                    pool.tensor_tensor(s.zw[i], s.zn[i], rows(g.ones[:, :]), ALU.mult).then_inc(S["z_now"], 1)
                for i in range(2):
                    wait(pool, "QKT_raw", 2, it, i + 1)
                    pool.tensor_tensor(s.QKT[i], s.QKT[i], rows(g.tri[:, :]), ALU.mult).then_inc(S["QKT"], 1)
                    pool.tensor_tensor(s.kbg[i], s.kn, cols(s.st[:, i, BEG, :]), ALU.mult).then_inc(S["k_beta"], 1)

            gates.masks(pool)
            head_pair(0)
            with pool.Fori(1, LAST) as it:
                head_pair(it)
            head_pair(LAST)


def build(nc, a, out):
    with ExitStack() as ctx:
        g = make_shared(nc, ctx)
        m = moe_memory(nc, ctx, g)
        gd, ml = gdn_memory(nc, ctx, g), mla_memory(nc, g)
        m.wr_in = [g.sem(f"router_in{l}") for l in range(2)]
        ple_w = [g.sem(f"ple_w_in{l}") for l in range(2)]
        for layer in range(2):
            def load_router(sp, layer=layer):
                for dst, src in ((m.wr[:, :, 0:GROUPS], a["moe_router_group"]), (m.wr[:, :, GROUPS:], a["moe_router_expert"])):
                    sp.dma_start(dst, src[layer].rearrange("(p k) n -> p k n", k=KD)).then_inc(m.wr_in[layer], 16)
                for i in range(2):
                    load_expert(sp, m, a, layer, i, i, m.loaded[layer][i])

            def load_more(sp, layer=layer):
                for i in range(2, NBUF):
                    load_expert(sp, m, a, layer, i, i, m.loaded[layer][i])
                sp.wait_ge(m.rows_zeroed, 16 * len(zero_chunks(m)))

            if layer == 0:
                with semaphores_of(nc, g):
                    stage_setup(nc, g, m, gd, a)
            with semaphores_of(nc, g):
                early_in = g.sem(f"early_rows_in{layer}")
                if layer == 0:
                    stage_norm(nc, g, "gdn_norm", 0, summed=False)
                    stage_delta(nc, g, gd, a, early_in)
                    stage_out(nc, g, "gdn_out", a["gdn_w_out"][0], 1, early_in, load_router)
                else:
                    w_in = g.sem("mla_w_in")
                    stage_norm(nc, g, "mla_norm", 1, lambda sp: load_mla_in(sp, ml, a, w_in))
                    stage_mla_in(nc, g, ml, a, w_in)
                    stage_mla_heads(nc, g, ml, a, early_in)
                    stage_out(nc, g, "mla_out", a["mla_w_out"][0], 0, early_in, load_router)
            with semaphores_of(nc, g):
                stage_norm(nc, g, f"ffn_norm{layer}", 2 + layer, load_more)
                stage_route(nc, g, m, a, layer)
                stage_experts(nc, g, m, a, layer)
                stage_overflow(nc, g, m, a, layer)
                stage_combine(nc, g, m, layer, lambda sp, layer=layer: ple_load(sp, a, g, layer, ple_w[layer]))
                stage_norm(nc, g, f"ple_norm{layer}", 4 + layer)
                stage_ple(nc, g, a, layer, ple_w[layer])
        with semaphores_of(nc, g):
            stage_final(nc, g, a, out)


_INS = ['x', 'p', 'positions', 'norm_mix_g', 'norm_ffn_g', 'norm_ple_g', 'gdn_w_in', 'gdn_conv_w', 'gdn_a_log',
        'gdn_dt_bias', 'gdn_norm_g', 'gdn_w_out', 'mla_w_in', 'mla_q_norm_g', 'mla_kv_norm_g', 'mla_w_q_up',
        'mla_w_kv_up', 'mla_w_out', 'moe_router_group', 'moe_router_expert', 'moe_w_gate_up', 'moe_w_down',
        'ple_w_proj', 'ple_w_gate', 'final_norm_g']


def kernel(**inputs):
    import concourse.bacc as bacc
    from concourse.bass_utils import run_bass_kernel_spmd
    nc = bacc.Bacc("TRN2", target_bir_lowering=False, num_devices=1)
    arrays, a = {}, {}
    given = {name: np.ascontiguousarray(inputs[name]) for name in _INS}
    given["rope_cols"] = rope_columns()
    for name, v in given.items():
        arrays["in_" + name] = v
        ap = nc.dram_tensor("in_" + name, v.shape, mybir.dt.from_np(v.dtype), kind="ExternalInput").ap()
        a[name] = ap
    out = nc.dram_tensor("out_0", (1, SEQ, D), F32, kind="ExternalOutput").ap()
    build(nc, a, out)
    r = run_bass_kernel_spmd(nc, [arrays], core_ids=[0])
    return r.results[0]["out_0"]
```
